# Optimizing a Trainium2 kernel written in Bass

```python
import jax
import jax.numpy as jnp
from jax import lax
import numpy as np

D_MODEL = 1024
BATCH = 1
SEQ = 256
DEPTH = 1
DEC_BATCH = 8
DEC_SEQ = 16
PAST_LEN = 128

CHUNK = 64
Q_BLOCK = 128
N_MEM = 256
H_R = 4
DK_R = 64
DV_R = 128
ROPE_BASE = 10000.0
H_F = 8
D_F = 64
H_M = 4
D_M = 128
N_BRANCH = 3
N_GROUPS = 4
E_PER_GROUP = 8
D_EXPERT = 256
TOP_K = 2
EPS = 1e-6

RQK_W = H_R * DK_R
RV_W = H_R * DV_R
FOX_W = H_F * D_F
MEM_W = H_M * D_M
GATE_W = N_BRANCH * D_MODEL
SPLIT_SIZES = (RQK_W, RQK_W, RV_W, RV_W, FOX_W, FOX_W, FOX_W, H_F, MEM_W, GATE_W)
SPLIT_POINTS = tuple(sum(SPLIT_SIZES[:i + 1]) for i in range(len(SPLIT_SIZES) - 1))
N_IN = sum(SPLIT_SIZES)

kernel_name = 'hybrid_retention_fox_hmoe_stream_step'

F32 = jnp.float32

def rmsnorm(x, g):
    xf = x.astype(F32)
    y = xf * lax.rsqrt(jnp.mean(xf * xf, axis=-1, keepdims=True) + EPS)
    return (y * g.astype(F32)).astype(x.dtype)

def heads(t, h, d):
    return t.reshape(t.shape[:-1] + (h, d))

def rope(t, pos):
    half = t.shape[-1] // 2
    inv = ROPE_BASE ** (-jnp.arange(half, dtype=F32) / half)
    ang = pos.astype(F32)[:, None] * inv[None, :]
    c = jnp.cos(ang)[:, None, :]
    s = jnp.sin(ang)[:, None, :]
    t1 = t[..., :half].astype(F32)
    t2 = t[..., half:].astype(F32)
    return jnp.concatenate([t1 * c - t2 * s, t1 * s + t2 * c], axis=-1).astype(t.dtype)

def retention_log_decay():
    return jnp.log1p(-jnp.exp2(-5.0 - jnp.arange(H_R, dtype=F32)))

def retention_chunk(state, q, k, v, lg):
    n = q.shape[1]
    idx = jnp.arange(n, dtype=F32)
    diff = idx[:, None] - idx[None, :]
    causal = diff >= 0
    dmat = jnp.where(causal[None], jnp.exp(jnp.where(causal, diff, 0.0)[None] * lg[:, None, None]), 0.0)
    sc = jnp.einsum('bihk,bjhk->bhij', q, k) * dmat[None]
    intra = jnp.einsum('bhij,bjhv->bihv', sc, v)
    q_dec = jnp.exp((idx + 1.0)[:, None] * lg[None, :])
    inter = jnp.einsum('bihk,bhkv->bihv', q * q_dec[None, :, :, None], state)
    k_dec = jnp.exp((n - 1.0 - idx)[:, None] * lg[None, :])
    new_state = (jnp.exp(n * lg)[None, :, None, None] * state
                 + jnp.einsum('bjhk,bjhv->bhkv', k * k_dec[None, :, :, None], v))
    return new_state, intra + inter

def retention_prompt(q, k, v):
    b, s, h, dk = q.shape
    nc = s // CHUNK
    lg = retention_log_decay()

    def to_chunks(t):
        return jnp.swapaxes(t.astype(F32).reshape((b, nc, CHUNK) + t.shape[2:]), 0, 1)

    def step(state, inp):
        qc, kc, vc = inp
        return retention_chunk(state, qc, kc, vc, lg)

    s0 = jnp.zeros((b, h, dk, DV_R), F32)
    s_fin, o = lax.scan(step, s0, (to_chunks(q), to_chunks(k), to_chunks(v)))
    return s_fin, jnp.swapaxes(o, 0, 1).reshape(b, s, h, DV_R)

def retention_out(o, rg, g_ret_out):
    normed = rmsnorm(o, g_ret_out).astype(rg.dtype)
    gated = normed * jax.nn.silu(heads(rg, H_R, DV_R))
    return gated.reshape(gated.shape[:2] + (RV_W,))

def fox_attend(q, fq, qpos, k, v, fk, kpos):
    s = jnp.einsum('bqhd,bkhd->bhqk', q, k).astype(F32) * (D_F ** -0.5)
    s = s + (jnp.swapaxes(fq, 1, 2)[:, :, :, None] - jnp.swapaxes(fk, 1, 2)[:, :, None, :])
    mask = qpos[:, None] >= kpos[None, :]
    s = jnp.where(mask[None, None], s, -jnp.inf)
    p = jax.nn.softmax(s, axis=-1).astype(v.dtype)
    return jnp.einsum('bhqk,bkhd->bqhd', p, v)

def fox_prompt(q, k, v, logf):
    b, s, h, d = q.shape
    nb = s // Q_BLOCK
    f_cum = jnp.cumsum(logf, axis=1)
    pos = jnp.arange(s)
    qb = jnp.swapaxes(q.reshape(b, nb, Q_BLOCK, h, d), 0, 1)
    fb = jnp.swapaxes(f_cum.reshape(b, nb, Q_BLOCK, h), 0, 1)
    pb = pos.reshape(nb, Q_BLOCK)
    out = lax.map(lambda a: fox_attend(a[0], a[1], a[2], k, v, f_cum, pos), (qb, fb, pb))
    return jnp.swapaxes(out, 0, 1).reshape(b, s, FOX_W)

def mem_kv(mem, g_mem_in, w_mem_kv, g_mem_k):
    hm = rmsnorm(mem, g_mem_in)
    mk, mv = jnp.split(hm @ w_mem_kv, 2, axis=-1)
    return rmsnorm(heads(mk, H_M, D_M), g_mem_k), heads(mv, H_M, D_M)

def mem_attend(q, k, v):
    s = jnp.einsum('bqhd,bkhd->bhqk', q, k).astype(F32) * (D_M ** -0.5)
    p = jax.nn.softmax(s, axis=-1).astype(v.dtype)
    o = jnp.einsum('bhqk,bkhd->bqhd', p, v)
    return o.reshape(o.shape[:2] + (MEM_W,))

def prep(x, pos, g_norm1, w_in, b_forget, g_fox_q, g_fox_k, g_mem_q):
    h = rmsnorm(x, g_norm1)
    z = h @ w_in
    rq, rk, rv, rg, fq, fk, fv, ff, mq, gl = jnp.split(z, SPLIT_POINTS, axis=-1)
    rq = rope(heads(rq, H_R, DK_R), pos)
    rk = rope(heads(rk, H_R, DK_R), pos) * (DK_R ** -0.5)
    rv = heads(rv, H_R, DV_R)
    fq = rmsnorm(heads(fq, H_F, D_F), g_fox_q)
    fk = rmsnorm(heads(fk, H_F, D_F), g_fox_k)
    fv = heads(fv, H_F, D_F)
    logf = jax.nn.log_sigmoid((ff + b_forget).astype(F32))
    mq = rmsnorm(heads(mq, H_M, D_M), g_mem_q)
    gates = jax.nn.sigmoid(gl.astype(F32)).reshape(gl.shape[:-1] + (N_BRANCH, D_MODEL)).astype(x.dtype)
    return rq, rk, rv, rg, fq, fk, fv, logf, mq, gates

def hier_moe(h, w_rg, b_rg, w_re, b_re, w_g, w_u, w_d):
    shp = h.shape
    t = h.reshape(-1, shp[-1])
    lg = (t @ w_rg + b_rg).astype(F32)
    oh_g = jax.nn.one_hot(jnp.argmax(lg, axis=-1), N_GROUPS, dtype=F32)
    p_sel = jnp.sum(jax.nn.softmax(lg, axis=-1) * oh_g, axis=-1, keepdims=True)
    le = (t @ w_re + b_re).astype(F32).reshape(-1, N_GROUPS, E_PER_GROUP)
    le_sel = jnp.einsum('tge,tg->te', le, oh_g)
    top_v, top_i = lax.top_k(le_sel, TOP_K)
    wk = jax.nn.softmax(top_v, axis=-1) * p_sel
    w_exp = jnp.sum(jax.nn.one_hot(top_i, E_PER_GROUP, dtype=F32) * wk[..., None], axis=1)
    comb = (oh_g[:, :, None] * w_exp[:, None, :]).astype(t.dtype)
    out = jnp.zeros_like(t)
    for g in range(N_GROUPS):
        a = jnp.einsum('td,edf->tef', t, w_g[g])
        u = jnp.einsum('td,edf->tef', t, w_u[g])
        out = out + jnp.einsum('tef,efd->td', jax.nn.silu(a) * u * comb[:, g, :, None], w_d[g])
    return out.reshape(shp)

def merge_and_ffn(x, o_r, o_f, o_m, gates, w_br_ret, w_br_fox, w_br_mem, w_out, g_norm2,
                  w_route_group, b_route_group, w_route_expert, b_route_expert,
                  w_exp_gate, w_exp_up, w_exp_down):
    merged = (gates[..., 0, :] * (o_r @ w_br_ret)
              + gates[..., 1, :] * (o_f @ w_br_fox)
              + gates[..., 2, :] * (o_m @ w_br_mem))
    x = x + merged @ w_out
    return x + hier_moe(rmsnorm(x, g_norm2), w_route_group, b_route_group, w_route_expert,
                        b_route_expert, w_exp_gate, w_exp_up, w_exp_down)

def setup_inputs(seed: int = 0) -> dict:
    key = jax.random.key(seed)
    ks = jax.random.split(key, 40)
    L = DEPTH

    def nrm(k, shape, scale=1.0):
        return jax.random.normal(k, shape, F32) * scale

    def gain(k, shape):
        return 1.0 + 0.1 * jax.random.normal(k, shape, F32)

    return {
        'x_prompt': nrm(ks[0], (BATCH, SEQ, D_MODEL)),
        'x_sample': nrm(ks[1], (DEC_BATCH, DEC_SEQ, D_MODEL)),
        'state_ret': nrm(ks[2], (L, DEC_BATCH, H_R, DK_R, DV_R), 0.5),
        'cache_fox_k': nrm(ks[3], (L, DEC_BATCH, PAST_LEN, H_F, D_F)),
        'cache_fox_v': nrm(ks[4], (L, DEC_BATCH, PAST_LEN, H_F, D_F)),
        'cache_fox_logf': jax.nn.log_sigmoid(nrm(ks[5], (L, DEC_BATCH, PAST_LEN, H_F)) + 2.0),
        'cache_mem_k': nrm(ks[6], (L, DEC_BATCH, N_MEM, H_M, D_M)),
        'cache_mem_v': nrm(ks[7], (L, DEC_BATCH, N_MEM, H_M, D_M)),
        'mem_prompt': nrm(ks[8], (BATCH, N_MEM, D_MODEL)),
        'g_norm1': gain(ks[9], (L, D_MODEL)),
        'w_in': nrm(ks[10], (L, D_MODEL, N_IN), D_MODEL ** -0.5),
        'b_forget': 2.0 + nrm(ks[11], (L, H_F), 0.1),
        'g_fox_q': gain(ks[12], (L, D_F)),
        'g_fox_k': gain(ks[13], (L, D_F)),
        'g_mem_q': gain(ks[14], (L, D_M)),
        'g_mem_in': gain(ks[15], (L, D_MODEL)),
        'w_mem_kv': nrm(ks[16], (L, D_MODEL, 2 * MEM_W), D_MODEL ** -0.5),
        'g_mem_k': gain(ks[17], (L, D_M)),
        'g_ret_out': gain(ks[18], (L, DV_R)),
        'w_br_ret': nrm(ks[19], (L, RV_W, D_MODEL), RV_W ** -0.5),
        'w_br_fox': nrm(ks[20], (L, FOX_W, D_MODEL), FOX_W ** -0.5),
        'w_br_mem': nrm(ks[21], (L, MEM_W, D_MODEL), MEM_W ** -0.5),
        'w_out': nrm(ks[22], (L, D_MODEL, D_MODEL), D_MODEL ** -0.5),
        'g_norm2': gain(ks[23], (L, D_MODEL)),
        'w_route_group': nrm(ks[24], (L, D_MODEL, N_GROUPS), D_MODEL ** -0.5),
        'b_route_group': nrm(ks[25], (L, N_GROUPS), 0.01),
        'w_route_expert': nrm(ks[26], (L, D_MODEL, N_GROUPS * E_PER_GROUP), D_MODEL ** -0.5),
        'b_route_expert': nrm(ks[27], (L, N_GROUPS * E_PER_GROUP), 0.01),
        'w_exp_gate': nrm(ks[28], (L, N_GROUPS, E_PER_GROUP, D_MODEL, D_EXPERT), D_MODEL ** -0.5),
        'w_exp_up': nrm(ks[29], (L, N_GROUPS, E_PER_GROUP, D_MODEL, D_EXPERT), D_MODEL ** -0.5),
        'w_exp_down': nrm(ks[30], (L, N_GROUPS, E_PER_GROUP, D_EXPERT, D_MODEL), D_EXPERT ** -0.5),
    }

def reference(x_prompt, x_sample, state_ret, cache_fox_k, cache_fox_v, cache_fox_logf,
              cache_mem_k, cache_mem_v, mem_prompt, g_norm1, w_in, b_forget, g_fox_q, g_fox_k,
              g_mem_q, g_mem_in, w_mem_kv, g_mem_k, g_ret_out, w_br_ret, w_br_fox, w_br_mem,
              w_out, g_norm2, w_route_group, b_route_group, w_route_expert, b_route_expert,
              w_exp_gate, w_exp_up, w_exp_down):
    seq = x_prompt.shape[1]
    n_new = x_sample.shape[1]
    past = cache_fox_k.shape[2]
    pos_p = jnp.arange(seq)
    pos_s = past + jnp.arange(n_new)
    kpos_s = jnp.arange(past + n_new)
    lg = retention_log_decay()
    xp = x_prompt
    xs = x_sample
    ret_p, fk_p, fv_p, fl_p, mk_p, mv_p = [], [], [], [], [], []
    ret_s, fk_s, fv_s, fl_s = [], [], [], []
    for l in range(DEPTH):
        rq, rk, rv, rg, fq, fk, fv, logf, mq, gates = prep(
            xp, pos_p, g_norm1[l], w_in[l], b_forget[l], g_fox_q[l], g_fox_k[l], g_mem_q[l])
        s_fin, o_ret = retention_prompt(rq, rk, rv)
        o_r = retention_out(o_ret, rg, g_ret_out[l])
        o_f = fox_prompt(fq, fk, fv, logf)
        mk, mv = mem_kv(mem_prompt, g_mem_in[l], w_mem_kv[l], g_mem_k[l])
        o_m = mem_attend(mq, mk, mv)
        xp = merge_and_ffn(xp, o_r, o_f, o_m, gates, w_br_ret[l], w_br_fox[l], w_br_mem[l],
                           w_out[l], g_norm2[l], w_route_group[l], b_route_group[l],
                           w_route_expert[l], b_route_expert[l], w_exp_gate[l], w_exp_up[l],
                           w_exp_down[l])
        ret_p.append(s_fin)
        fk_p.append(fk)
        fv_p.append(fv)
        fl_p.append(logf)
        mk_p.append(mk)
        mv_p.append(mv)

        rq, rk, rv, rg, fq, fk, fv, logf, mq, gates = prep(
            xs, pos_s, g_norm1[l], w_in[l], b_forget[l], g_fox_q[l], g_fox_k[l], g_mem_q[l])
        s_new, o_ret = retention_chunk(state_ret[l].astype(F32), rq.astype(F32), rk.astype(F32),
                                       rv.astype(F32), lg)
        o_r = retention_out(o_ret, rg, g_ret_out[l])
        f_all = jnp.cumsum(jnp.concatenate([cache_fox_logf[l].astype(F32), logf], axis=1), axis=1)
        k_all = jnp.concatenate([cache_fox_k[l].astype(fk.dtype), fk], axis=1)
        v_all = jnp.concatenate([cache_fox_v[l].astype(fv.dtype), fv], axis=1)
        o_f = fox_attend(fq, f_all[:, past:], pos_s, k_all, v_all, f_all, kpos_s)
        o_f = o_f.reshape(o_f.shape[:2] + (FOX_W,))
        o_m = mem_attend(mq, cache_mem_k[l].astype(mq.dtype), cache_mem_v[l].astype(mq.dtype))
        xs = merge_and_ffn(xs, o_r, o_f, o_m, gates, w_br_ret[l], w_br_fox[l], w_br_mem[l],
                           w_out[l], g_norm2[l], w_route_group[l], b_route_group[l],
                           w_route_expert[l], b_route_expert[l], w_exp_gate[l], w_exp_up[l],
                           w_exp_down[l])
        ret_s.append(s_new)
        fk_s.append(fk)
        fv_s.append(fv)
        fl_s.append(logf)
    return (xp, xs,
            jnp.stack(ret_p), jnp.stack(fk_p), jnp.stack(fv_p), jnp.stack(fl_p),
            jnp.stack(mk_p), jnp.stack(mv_p),
            jnp.stack(ret_s), jnp.stack(fk_s), jnp.stack(fv_s), jnp.stack(fl_s))


_drawn_inputs = setup_inputs


def setup_inputs(seed=0):
    import zlib

    import numpy as np

    out = dict(_drawn_inputs(seed))
    spreads = {}
    factors = {'b_route_expert': 4.445, 'g_mem_q': 3.478, 'b_route_group': 8.0}
    for name, (base, spread) in spreads.items():
        noise = np.random.default_rng([zlib.crc32(name.encode()), seed]).standard_normal(out[name].shape)
        drawn = base * np.exp(spread * noise) if base else spread * noise
        out[name] = jnp.asarray(drawn.astype(out[name].dtype))
    for name, factor in factors.items():
        out[name] = (out[name] * factor).astype(out[name].dtype)
    return out
```

```python
from contextlib import ExitStack

import numpy as np

import concourse.bass as bass
from concourse import mybir

ALU = mybir.AluOpType
ACT = mybir.ActivationFunctionType
F32 = mybir.dt.float32
F32R = mybir.dt.float32r
AX = mybir.AxisListType.X

P = 128
D = 1024
KT = D // P
T = 3
TOK = T * P
SEQ, NB, NI, PAST, NMEM = 256, 8, 16, 128, 256
HR, HF, HM = 4, 8, 4
NG, NE, DE = 4, 8, 256
EPS = 1e-6
BIG = 1e30
GRAN = 2 * 512

CHUNKS = ([("mem", 8, 2)] * 2 + [("in", 8, 3)] * 7 + [("gate", 8, 3)] * 6 + [("br", 4, 3)] * 6 + [("out", 8, 3)] * 2)
C_MK, C_MV, C_RQK, C_RV, C_RG, C_FQ, C_FK, C_FV, C_MQ = range(9)
C_GATE, C_BR, C_OUT = 9, 15, 21
FIRST = [sum(c[1] // 2 for c in CHUNKS[:i]) for i in range(len(CHUNKS) + 1)]
NGRAN = FIRST[-1]
NSPLIT = FIRST[C_BR]
RAW_SLOTS, PART_SLOTS = 4, 3

CONST = {}
_at = 0
for _name, _n in (("ident", P), ("upper", P), ("ones", P), ("batchwin", 240), ("maskwin", 240), ("upper_in_batch", P),
                  ("zeros_causal", 256), ("cos", T * 32), ("sin", T * 32), ("decay_s", HR * P), ("kdec", T * HR),
                  ("inbatch", NB), ("headsel", P), ("pick", NI), ("rev4", T * 4), ("rev8", T * 8)):
    CONST[_name] = (_at, _n)
    _at += _n
N_CONST = _at
GAIN = {}
_at = 0
for _name, _n in (("fox_q", 64), ("fox_k", 64), ("mem_q", 128), ("mem_k", 128), ("ret", 128), ("forget", 8), ("route", 36)):
    GAIN[_name] = (_at, _n)
    _at += _n
N_GAIN = _at


def schedule():
    s = [("prep_mem",), ("prep_x",)]
    ahead = 2
    split = 0

    def granule(g):
        nonlocal split
        while split < min(g + 1 + ahead, NSPLIT):
            s.append(("split", split))
            split += 1
        s.append(("k", g))

    for c in range(C_GATE):
        for g in range(FIRST[c], FIRST[c + 1]):
            granule(g)
            if g == FIRST[c] and c:
                s.append(("evac", c - 1))
                s.append(("post", c - 1))
    s.append(("forget",))
    s.append(("evac", C_GATE - 1))
    s.append(("post", C_GATE - 1))
    units = [("foxp", hp * 2 + hl, t) for t in range(2) for hp in range(4) for hl in range(2)]
    units += [("memp", h, t) for h in range(HM) for t in range(2)] + [("foxs", b, 0) for b in range(NB)]
    early = len(units)
    units += [("mems", bp, 0) for bp in range(NB // 2)]
    pieces = [("turn", i) for i in range(20)] + [("decay_sums",)]
    pieces += [("ret_s", 0), ("ret_s", 1), ("decay_query",), ("ret_o", 0), ("ret_s", 2), ("ret_o", 1), ("ret_t", 0),
               ("ret_s", 3), ("ret_o", 2), ("ret_t", 1), ("ret_o", 3), ("ret_t", 2), ("ret_t", 3), ("ret_state",)]
    tail = []
    for i in range(len(units) + 2):
        into = pieces if i < early else tail
        if i < len(units):
            into.append(("unit_s", i))
        if 1 <= i <= len(units):
            into.append(("unit_p", i - 1))
        if i >= 2:
            into.append(("unit_v", i - 2))
    gates = range(FIRST[C_GATE], FIRST[C_BR])
    placed = 0
    for i, piece in enumerate(pieces):
        s.append(piece)
        while placed < len(gates) and (placed + 0.5) * len(pieces) <= (i + 1) * len(gates):
            granule(gates[placed])
            placed += 1
            if placed % 4 == 0:
                s.append(("evac", C_GATE + placed // 4 - 1))
    assert placed == len(gates)
    s.append(("mem_caches",))
    s += tail
    s.append(("gates",))
    for c in range(C_BR, C_OUT):
        s += [("k", g) for g in range(FIRST[c], FIRST[c + 1])] + [("merge", c)]
    s.append(("turn_merged",))
    for c in range(C_OUT, C_OUT + 2):
        s += [("k", g) for g in range(FIRST[c], FIRST[c + 1])] + [("residual", c)]
    s += [("norm2",), ("turn_x2",), ("route",)]
    return s, units


def program(nc, io):
    steps, units = schedule()
    NU = len(units)
    ctx = ExitStack()
    with ctx:
        base = (nc.sbuf_base + 31) // 32 * 32

        def at(name, shape, offset, dt=F32):
            return nc.alloc_sbuf_tensor_at(name, shape, dt, offset=base + offset)

        def sem(name):
            return ctx.enter_context(nc.semaphore(name))

        KB = 1024
        o_const = 0
        o_gain = o_const + 4 * N_CONST
        o_small = (o_gain + 4 * N_GAIN + 31) // 32 * 32
        o_h = (o_small + 4 * 560 + 31) // 32 * 32
        o_ot = o_h + 24 * KB
        o_raw = o_ot + 18 * KB
        o_z = o_raw + 4 * GRAN * (RAW_SLOTS + 2 * PART_SLOTS)
        o_mkv = o_z + 42 * KB
        o_turned = o_mkv + 8 * KB
        o_sums = o_turned + 28 * KB
        o_work = o_sums + 5632
        end = o_work + 29 * KB
        assert end <= 212863, end

        const = at("const", [P, N_CONST], o_const)
        gain = at("gain", [P, N_GAIN], o_gain)
        small = at("small", [P, 560], o_small)

        def cst(name):
            a, n = CONST[name]
            return const[:, a:a + n]

        def gn(name):
            a, n = GAIN[name]
            return gain[:, a:a + n]

        used = [0]

        def sm(n):
            a = used[0]
            used[0] += n
            assert used[0] <= 560
            return small[:, a:a + n]

        ident = cst("ident")
        gk = sm(24)
        ss, rstd = sm(5), sm(5)
        ffw = sm(64)
        zf, zneg, ze, zl, logf = (sm(24) for _ in range(5))
        logc = sm(64)
        fq_col = sm(16)
        fq_s = sm(8)
        pick8 = sm(P)
        hs, hr = sm(24), sm(24)
        nmax, rsum, rinv = sm(2), sm(2), sm(2)
        rss, rrs = sm(3), sm(3)
        ss2, rstd2, newton = sm(3), sm(3), sm(24)

        hT_hi = at("hT_hi", [P, KT, TOK], o_h, F32R)
        hT_lo = at("hT_lo", [P, KT, TOK], o_h + 12 * KB, F32R)
        mT = at("mT", [P, KT, TOK], o_h)
        x2 = at("x2", [P, T, D], o_h + 12 * KB)
        memk = [at(f"memk{i}", [P, 1024], o_h + 4 * KB * i) for i in range(4)]
        memv = [at(f"memv{i}", [P, 1024], (o_h, o_work)[i // 2] + 16 * KB + 4 * KB * (i % 2)) for i in range(4)]
        memT_hi = at("memT_hi", [P, KT, NMEM], o_ot, F32R)
        memT_lo = at("memT_lo", [P, KT, NMEM], o_ot + 8 * KB, F32R)
        oT = at("oT", [P, 12, TOK], o_ot)
        h2T = at("h2T", [P, KT, TOK], o_ot)
        qtab = at("qtab", [P, HR, 4, P], o_ot + 6 * KB)
        dtab = at("dtab", [P, HR, 256], o_ot + 14 * KB)
        raw = at("raw", [P, RAW_SLOTS, GRAN], o_raw)
        w_hi = at("w_hi", [P, PART_SLOTS, GRAN], o_raw + 4 * GRAN * RAW_SLOTS, F32R)
        w_lo = at("w_lo", [P, PART_SLOTS, GRAN], o_raw + 4 * GRAN * (RAW_SLOTS + PART_SLOTS), F32R)
        z = at("z", [P, 7, T, 512], o_z)
        xT = at("xT", [P, KT, TOK], o_z)
        memT = at("memT", [P, KT, NMEM], o_z + 12 * KB)
        xtok = at("xtok", [P, T, D], o_z + 20 * KB)
        memtok = at("memtok", [P, 2, D], o_z + 32 * KB)
        mk = at("mk", [P, 2, 512], o_mkv)
        mv = at("mv", [P, 2, 512], o_mkv + 4 * KB)
        rqkT = at("rqkT", [P, 4, TOK], o_turned)
        fqT = at("fqT", [P, 4, TOK], o_turned + 6 * KB)
        fkT = at("fkT", [P, 4, TOK], o_turned + 12 * KB)
        mqT = at("mqT", [P, 4, TOK], o_turned + 18 * KB)
        mkT = at("mkT", [P, 4, NMEM], o_turned + 24 * KB)
        nf_p = at("nf_p", [8, 256], o_sums)
        nf_n = at("nf_n", [8, P], o_sums + 1024)
        nf_c = at("nf_c", [8, NB, P], o_sums + 1536)
        state = at("state", [P, 4, HR, P], o_work)
        kmask = at("kmask", [P, 4, HR, 2, 64], o_work + 8 * KB)
        qmask = at("qmask", [P, 2, 4, P], o_work + 16 * KB)
        sT = at("sT", [P, 2, 512], o_work + 20 * KB)
        osq = at("osq", [P, TOK], o_work + 24 * KB)
        orow = at("orow", [P, TOK], o_work + 24 * KB + 1536)
        qdup = at("qdup", [P, HR, P], o_work + 27 * KB)
        stp = at("stp", [P, 2, P], o_work + 24 * KB)
        s_sb = at("s_sb", [P, 2, 256], o_work)
        p_sb = at("p_sb", [P, 2, 256], o_work + 2 * KB)
        pT = at("pT", [P, 2, 256], o_work + 4 * KB)
        qb_f = at("qb_f", [P, 2, 640], o_work + 6 * KB)
        qb_m = at("qb_m", [P, 4, 320], o_work + 11 * KB)
        foxc = at("foxc", [P, 3, 1024], o_work + 16 * KB)
        ewt = at("ewt", [P, 2, 6144], o_z)
        rt = at("rt", [P, 1024], o_z + 48 * KB)
        act_g = at("act_g", [P, 2, DE], o_z + 52 * KB)
        act_h = at("act_h", [P, 2, DE], o_z + 54 * KB)
        act_T = at("act_T", [P, 2, 256], o_z + 56 * KB)
        wr = at("wr", [P, KT, 36], o_z + 58 * KB)
        ysb = at("ysb", [P, T, D], o_z + 60 * KB)

        ps = ctx.enter_context(nc.psum_tensor("banks", [P, 8, 512], F32))

        s_gk, s_xT, s_memT, s_xtok, s_memtok, s_const, s_gain, s_ffw = (sem(n) for n in ("s_gk", "s_xT", "s_memT", "s_xtok", "s_memtok", "s_const", "s_gain", "s_ffw"))
        s_logc, s_qtab, s_dtab, s_state, s_x2, s_wr, s_y, s_out = (sem(n) for n in ("s_logc", "s_qtab", "s_dtab", "s_state", "s_x2", "s_wr", "s_y", "s_out"))
        s_fk_out, s_state_out, s_stp_out, hi_ready, lo_ready, gran_used, ss_ready, rstd_ready = (sem(n) for n in ("s_fk_out", "s_state_out", "s_stp_out", "hi_ready", "lo_ready", "gran_used", "ss_ready", "rstd_ready"))
        act_hi, act_lo, acc_evac, post_done, sq_ready, hr_ready, ff_ready, zneg_ready = (sem(n) for n in ("act_hi", "act_lo", "acc_evac", "post_done", "sq_ready", "hr_ready", "ff_ready", "zneg_ready"))
        ln_ready, logf_ready, turn_ready, even_turned, odd_turned, sums_ready, sums_evac, fqs_psum = (sem(n) for n in ("ln_ready", "logf_ready", "turn_ready", "even_turned", "odd_turned", "sums_ready", "sums_evac", "fqs_psum"))
        fqs_ready, qdup_ready, kmask_ready, ret_s, ret_m, ret_q, ret_o, ret_sq = (sem(n) for n in ("fqs_ready", "qdup_ready", "kmask_ready", "ret_s", "ret_m", "ret_q", "ret_o", "ret_sq"))
        ret_rows, ret_t, ret_te, st_ready, st_done, work_zero, qb_ready, u_s = (sem(n) for n in ("ret_rows", "ret_t", "ret_te", "st_ready", "st_done", "work_zero", "qb_ready", "u_s"))
        u_max, u_exp, u_p, u_T, u_Te, u_v, u_oe, gate_ready = (sem(n) for n in ("u_max", "u_exp", "u_p", "u_T", "u_Te", "u_v", "u_oe", "gate_ready"))
        br_mul, br_add, mt_ready, mt_evac, x2_ready, ss2_ready, rstd2_ready, x2t_ready = (sem(n) for n in ("br_mul", "br_add", "mt_ready", "mt_evac", "x2_ready", "ss2_ready", "rstd2_ready", "x2t_ready"))
        x2t_evac, lg_ready, route_in, route_exp, comb_ready, gu_ready, silu_ready, h_ready = (sem(n) for n in ("x2t_evac", "lg_ready", "route_in", "route_exp", "comb_ready", "gu_ready", "silu_ready", "h_ready"))
        hT_ready, hT_evac, dn_done, y_ready, dve_step, pool_step, act_step = (sem(n) for n in ("hT_ready", "hT_evac", "dn_done", "y_ready", "dve_step", "pool_step", "act_step"))
        raw_in = [sem(f"raw_in{i}") for i in range(RAW_SLOTS)]
        foxc_in = [sem(f"foxc_in{i}") for i in range(3)]
        memk_in = [sem(f"memk_in{i}") for i in range(4)]
        memv_in = [sem(f"memv_in{i}") for i in range(4)]
        ewt_in = [sem(f"ewt_in{i}") for i in range(2)]

        class Chain:

            def __init__(self, eng, s):
                self.eng, self.s, self.n = eng, s, 0

            def __call__(self, ins):
                self.n += 1
                ins.then_inc(self.s, 1)
                self.eng.wait_ge(self.s, self.n)

        I32 = mybir.dt.int32

        def rsqrt(dve, chain, out, x, n):
            tmp = newton[:, 0:n]
            chain(dve.tensor_scalar(tmp.bitcast(I32), x.bitcast(I32), 1, None, ALU.logical_shift_right))
            chain(dve.tensor_scalar(out.bitcast(I32), tmp.bitcast(I32), -1.0, float(0x5F3759DF), ALU.mult, ALU.add))
            for step in range(3):
                chain(dve.tensor_tensor(tmp, out, out, ALU.mult))
                chain(dve.scalar_tensor_tensor(tmp, tmp, -0.5, x, ALU.mult, ALU.mult))
                ins = dve.scalar_tensor_tensor(out, tmp, 1.5, out, ALU.add, ALU.mult)
                if step < 2:
                    chain(ins)
            return ins

        def bank_of(c, t):
            if c < C_GATE:
                return 3 * (c % 2) + t
            if c < C_BR:
                return t
            return 3 * ((c - C_BR) % 2) + t

        def last_user(c):
            for b in range(c - 1, -1, -1):
                if bank_of(b, 0) == bank_of(c, 0):
                    return b
            return None

        chunk_of = [c for c in range(len(CHUNKS)) for _ in range(FIRST[c], FIRST[c + 1])]
        Z_OF = {C_RQK: 0, C_RV: 1, C_RG: 2, C_FQ: 3, C_FK: 4, C_FV: 5, C_MQ: 6}
        GATE_SLOT = [3, 4, 6, 0, 1, 2]
        turns = [(name, j) for name in ("rqk", "fq", "fk", "mq", "mk") for j in range(4)]
        GAMMA_N = [float((1.0 - 2.0 ** (-5.0 - h)) ** NI) for h in range(HR)]

        def group_of(i):
            return i // 2 if i < 16 else i - 8

        def last_of(i):
            return i >= 16 or i % 2 == 1

        NGROUP = group_of(NU - 1) + 1
        rqk, rv, rg, fq, fk, fv, mq = (z[:, i, :, :] for i in range(7))
        POSTED = {C_MK: 1, C_RQK: 2, C_RG: 3, C_FQ: 4, C_FK: 5, C_MQ: 6}
        NORMS = {C_MK: (mk[:, :, :], 8, P, "mem_k", 0), C_FQ: (fq, 24, 64, "fox_q", 1), C_FK: (fk, 24, 64, "fox_k", 2), C_MQ: (mq, 12, P, "mem_q", 3)}
        last_norm = [C_MK, C_FQ, C_FK, C_MQ]

        def keys(i):
            return P if units[i][0] == "foxp" and units[i][2] == 0 else 256

        def turn_wait(eng, j):
            eng.wait_ge(odd_turned if j % 2 else even_turned, j // 2 + 1)

        def turn_out(eng, copy, i):
            name, j = turns[i]
            eng.wait_ge(turn_ready, i + 1)
            dst = {"rqk": rqkT, "fq": fqT, "fk": fkT, "mq": mqT, "mk": mkT}[name]
            n = NMEM if name == "mk" else TOK
            scale = {"fq": 64 ** -0.5, "mq": P ** -0.5}.get(name, 1.0)
            copy(dst[:, j, :], ps[:, 3 + i % 5, 0:n], scale).then_inc(odd_turned if i % 2 else even_turned, 1)

        zq = at("zq", [P, T * 512], o_work + 16 * KB)
        scratch = at("scratch", [P, 2, D], o_work)
        ffw_hi = at("ffw_hi", [P, 64], o_work + 8 * KB, F32R)
        ffw_lo = at("ffw_lo", [P, 64], o_work + 8 * KB + 256, F32R)
        block = ctx.enter_context(nc.Block())

        rt_used = [0]

        def R(n):
            a = rt_used[0]
            rt_used[0] += n
            return rt[:, a:a + n]

        r_l, r_d4, r_e4, r_t4, r_oh = R(108), R(12), R(12), R(12), R(12)
        r_m4, r_x4, r_m1, r_m2, r_x1, r_d2, r_e2, r_s4, r_w1, r_w2 = (R(3) for _ in range(10))
        r_x, r_le, r_le2, r_t8, r_oh1, r_oh2, r_we, comb = R(96), R(24), R(24), R(24), R(24), R(24), R(24), R(96)

        def route(dve, chain):
            def v(a, n):
                return a.rearrange("p (t n) -> p t n", t=T) if n else a

            def wide(a, n):
                return a.unsqueeze(2).to_broadcast([P, T, n])

            def first_best(values, n, mx, tmp, tmp_mx, onehot, rev):
                chain(dve.tensor_reduce(mx, values, AX, ALU.max))
                chain(dve.tensor_tensor(v(tmp, n), values, wide(mx, n), ALU.is_equal))
                chain(dve.tensor_tensor(v(tmp, n), v(tmp, n), v(cst(rev), n), ALU.mult))
                chain(dve.tensor_reduce(tmp_mx, v(tmp, n), AX, ALU.max))
                chain(dve.tensor_tensor(v(onehot, n), v(tmp, n), wide(tmp_mx, n), ALU.is_equal))

            dve.wait_ge(lg_ready, 1)
            L = v(r_l, 36)
            for t in range(T):
                ins = dve.scalar_tensor_tensor(L[:, t, :], ps[:, 7, 64 * t:64 * t + 36], rstd2[:, t:t + 1], gn("route"), ALU.mult, ALU.add)
            chain(ins)
            first_best(L[:, :, 0:4], 4, r_m4, r_t4, r_x4, r_oh, "rev4")
            chain(dve.tensor_tensor(v(r_d4, 4), L[:, :, 0:4], wide(r_m4, 4), ALU.subtract))
            x4 = r_x.rearrange("p (t e g) -> p t e g", t=T, e=NE)
            chain(dve.tensor_tensor(x4, L[:, :, 4:36].rearrange("p t (g e) -> p t e g", g=NG), v(r_oh, 4).unsqueeze(2).to_broadcast([P, T, NE, NG]), ALU.mult))
            chain(dve.tensor_reduce(v(r_le, 8), x4, AX, ALU.add))
            first_best(v(r_le, 8), 8, r_m1, r_t8, r_x1, r_oh1, "rev8")
            chain(dve.scalar_tensor_tensor(r_le2, r_oh1, -BIG, r_le, ALU.mult, ALU.add))
            first_best(v(r_le2, 8), 8, r_m2, r_t8, r_x1, r_oh2, "rev8")
            dve.tensor_tensor(r_d2, r_m2, r_m1, ALU.subtract).then_inc(route_in, 1)
            dve.wait_ge(route_exp, 1)
            chain(dve.tensor_reduce(r_s4, v(r_e4, 4), AX, ALU.add))
            chain(dve.tensor_scalar(r_w2, r_e2, 1.0, None, ALU.add))
            chain(dve.tensor_tensor(r_w1, r_w2, r_s4, ALU.mult))
            chain(dve.reciprocal(r_w1, r_w1))
            chain(dve.tensor_tensor(r_w1, r_w1, rstd2, ALU.mult))
            chain(dve.tensor_tensor(r_w2, r_e2, r_w1, ALU.mult))
            chain(dve.tensor_tensor(v(r_we, 8), v(r_oh1, 8), wide(r_w1, 8), ALU.mult))
            chain(dve.tensor_tensor(v(r_t8, 8), v(r_oh2, 8), wide(r_w2, 8), ALU.mult))
            chain(dve.tensor_tensor(r_we, r_we, r_t8, ALU.add))
            dve.tensor_tensor(comb.rearrange("p (t g e) -> p t g e", t=T, g=NG), v(r_oh, 4).unsqueeze(3).to_broadcast([P, T, NG, NE]),
                              v(r_we, 8).unsqueeze(2).to_broadcast([P, T, NG, NE]), ALU.mult).then_inc(comb_ready, 1)
            dve.wait_ge(comb_ready, 1)

        @block.sync
        def _(sp):
            def load(dst, src, s):
                sp.dma_start(dst, src).then_inc(s, 16)

            def granule(g):
                old = g - RAW_SLOTS
                if old >= NSPLIT:
                    sp.wait_ge(gran_used, old + 1)
                elif old >= 0:
                    sp.wait_ge(lo_ready, old + 1)
                load(raw[:, g % RAW_SLOTS, :], io["wstream"][g], raw_in[g % RAW_SLOTS])

            load(memT[:, :, :], io["memT"], s_memT)
            load(gk, io["gk"], s_gk)
            for g in range(RAW_SLOTS):
                granule(g)
            load(memtok[:, :, :], io["memtok"], s_memtok)
            load(xT[:, :, :], io["xT"], s_xT)
            load(xtok[:, :, :], io["xtok"], s_xtok)
            load(const[:, :], io["const"], s_const)
            load(gain[:, :], io["gain"], s_gain)
            load(ffw, io["ffw"], s_ffw)
            load(logc, io["logc"], s_logc)
            for kind, *arg in steps:
                i = arg[0] if arg else 0
                if kind == "k" and i + RAW_SLOTS < NGRAN:
                    granule(i + RAW_SLOTS)
                elif kind == "post" and i == C_MV:
                    sp.wait_ge(gran_used, FIRST[2])
                    sp.wait_ge(ss_ready, 5)
                    sp.wait_ge(act_lo, 17)
                    load(qtab[:, :, :, :], io["qtab"], s_qtab)
                    load(dtab[:, :, :], io["dtab"], s_dtab)
                elif kind == "forget":
                    sp.wait_ge(ff_ready, 1)
                    load(state[:, :, :, :], io["state"], s_state)
                elif kind == "mem_caches":
                    sp.wait_ge(gran_used, NSPLIT)
                    for b in range(4):
                        load(memk[b][:, :], io["memc"][b, :, 0:1024], memk_in[b])
                    for b in range(2):
                        load(memv[b][:, :], io["memc"][b, :, 1024:2048], memv_in[b])
                elif kind == "unit_v" and units[i][0] == "foxs" and units[i][1] == NB - 1:
                    sp.wait_ge(u_v, i + 1)
                    for b in range(2, 4):
                        load(memv[b][:, :], io["memc"][b, :, 1024:2048], memv_in[b])
                elif kind == "unit_v" and units[i][0] == "mems" and units[i][1] < 2:
                    a = units[i][1]
                    sp.wait_ge(u_v, i + 1)
                    for b in (2 * a + 4, 2 * a + 5):
                        load(memv[b % 4][:, :], io["memc"][b, :, 1024:2048], memv_in[b % 4])
                elif kind == "unit_s" and units[i][0] == "mems" and units[i][1] < 2:
                    a = units[i][1]
                    sp.wait_ge(u_s, i + 1)
                    for b in (2 * a + 4, 2 * a + 5):
                        load(memk[b % 4][:, :], io["memc"][b, :, 0:1024], memk_in[b % 4])
                elif kind == "gates":
                    sp.wait_ge(u_v, NU)
                    load(x2[:, :, :], io["xtok"], s_x2)
                    sp.wait_ge(u_oe, NGROUP)
                    load(wr[:, :, :], io["wr"], s_wr)
            sp.wait_ge(mt_ready, 8)
            for e in range(NG * NE):
                if e >= 2:
                    sp.wait_ge(dn_done, T * (e - 1))
                load(ewt[:, e % 2, :], io["wexp"][e], ewt_in[e % 2])
            sp.wait_ge(y_ready, 1)
            sp.dma_start(io["y"], ysb[:, :, :]).then_inc(s_y, 16)
            sp.wait_ge(s_y, 16)

        @block.scalar
        def _(act):
            chain = Chain(act, act_step)
            for kind, *arg in steps:
                i = arg[0] if arg else 0
                if kind == "prep_mem":
                    act.wait_ge(s_memT, 16)
                    act.wait_ge(s_gk, 16)
                    for k in range(KT):
                        act.activation(memT_hi[:, k, :], memT[:, k, :], ACT.Copy, scale=gk[:, 8 + k:9 + k]).then_inc(act_hi, 1)
                elif kind == "prep_x":
                    act.wait_ge(s_memtok, 16)
                    for t in range(2):
                        act.activation(scratch[:, t, :], memtok[:, t, :], ACT.Square, accum_out=ss[:, 3 + t:4 + t]).then_inc(ss_ready, 1)
                    act.wait_ge(s_xT, 16)
                    for k in range(KT):
                        act.activation(hT_hi[:, k, :], xT[:, k, :], ACT.Copy, scale=gk[:, k:k + 1]).then_inc(act_hi, 1)
                    act.wait_ge(s_ffw, 16)
                    act.activation(ffw_hi[:, :], ffw, ACT.Copy).then_inc(act_hi, 1)
                    act.wait_ge(s_xtok, 16)
                    for t in range(T):
                        if t < 2:
                            act.wait_ge(ss_ready, 1 + t)
                        else:
                            act.wait_ge(ss_ready, 3)
                        act.activation(scratch[:, t % 2, :], xtok[:, t, :], ACT.Square, accum_out=ss[:, t:t + 1]).then_inc(ss_ready, 1)
                elif kind == "split":
                    act.wait_ge(raw_in[i % RAW_SLOTS], 16 * (i // RAW_SLOTS + 1))
                    if i >= PART_SLOTS:
                        act.wait_ge(gran_used, i - PART_SLOTS + 1)
                    act.activation(w_hi[:, i % PART_SLOTS, :], raw[:, i % RAW_SLOTS, :], ACT.Copy).then_inc(hi_ready, 1)
                elif kind == "evac":
                    act.wait_ge(rstd_ready, 1)
                    act.wait_ge(gran_used, FIRST[i + 1])
                    if i < C_RQK:
                        dst = (mk, mv)[i][:, :, :]
                    elif i < C_GATE:
                        dst = z[:, Z_OF[i], :, :]
                    else:
                        dst = z[:, GATE_SLOT[i - C_GATE], :, :]
                    if i == C_RQK:
                        act.wait_ge(act_lo, 17)
                    elif i == C_GATE:
                        act.wait_ge(turn_ready, 8)
                    elif i == C_GATE + 1:
                        act.wait_ge(turn_ready, 12)
                        act.wait_ge(s_fk_out, 16)
                    elif i == C_GATE + 2:
                        act.wait_ge(turn_ready, 16)
                    elif i >= C_GATE + 3:
                        act.wait_ge(st_ready, 5)
                        act.wait_ge(kmask_ready, 1)
                        act.wait_ge(ret_rows, HR)
                    f = ACT.Silu if i == C_RG else ACT.Copy
                    for t in range(CHUNKS[i][2]):
                        sc = rstd[:, 3 + t:4 + t] if i < C_RQK else rstd[:, t:t + 1]
                        ins = act.activation(dst[:, t, :], ps[:, bank_of(i, t), :], f, scale=sc)
                    ins.then_inc(acc_evac, 1)
                elif kind == "forget":
                    act.wait_ge(zneg_ready, 1)
                    chain(act.activation(ze, zneg, ACT.Exp))
                    act.activation(zl, ze, ACT.Ln, bias=1.0).then_inc(ln_ready, 1)
                elif kind == "turn":
                    if i % 2 == 0:
                        turn_out(act, lambda o, a, m: act.activation(o, a, ACT.Copy, scale=m), i)
                    if i == 2:
                        act.wait_ge(even_turned, 1)
                        act.wait_ge(odd_turned, 1)
                        for hl in range(2):
                            for b2 in range(2):
                                ins = act.activation(qdup[64 * b2:64 * b2 + 64, hl::2, :], rqkT[64 * hl:64 * hl + 64, 0:2, SEQ:TOK], ACT.Copy)
                        ins.then_inc(qdup_ready, 1)
                elif kind == "decay_sums":
                    act.wait_ge(sums_ready, 1)
                    act.activation(nf_p[:, :], ps[0:8, 3, 0:256], ACT.Copy, scale=-1.0)
                    act.activation(nf_n[:, :], ps[0:8, 3, 256:384], ACT.Copy, scale=-1.0)
                    for q in range(2):
                        act.activation(nf_c[:, 4 * q:4 * q + 4, :], ps[0:8, 4 + q, :].rearrange("p (b j) -> p b j", b=4), ACT.Copy, scale=-1.0)
                    act.activation(fq_col, ps[:, 6, 0:16], ACT.Copy).then_inc(sums_evac, 1)
                elif kind == "ret_o":
                    act.wait_ge(ret_o, i + 1)
                    if i:
                        act.wait_ge(ret_rows, i)
                    act.activation(osq[:, :], ps[:, 6, 0:TOK], ACT.Square, scale=float(P) ** -0.5).then_inc(ret_sq, 1)
                elif kind == "ret_t":
                    act.wait_ge(ret_t, i + 1)
                    act.activation(oT[:, i, :], ps[:, 7, 0:TOK], ACT.Copy).then_inc(ret_te, 1)
                elif kind == "unit_s":
                    act.wait_ge(u_max, i + 1)
                    n = keys(i)
                    src = s_sb[:, i % 2, 0:n] if units[i][0][:3] == "fox" else ps[:, 3 + i % 2, 0:n]
                    if i >= 2:
                        act.wait_ge(u_T, i - 1)
                    act.activation(p_sb[:, i % 2, 0:n], src, ACT.Exp, bias=nmax[:, i % 2:i % 2 + 1],
                                   accum_out=rsum[:, i % 2:i % 2 + 1]).then_inc(u_exp, 1)
                elif kind == "unit_p":
                    n = keys(i)
                    act.wait_ge(u_T, i + 1)
                    if i >= 2:
                        act.wait_ge(u_v, i - 1)
                    act.activation(pT[:, i % 2, 0:n], ps[:, 5, 0:n], ACT.Copy).then_inc(u_Te, 1)
                elif kind == "unit_v" and last_of(i):
                    act.wait_ge(u_v, i + 1)
                    o = ps[:, 6 + group_of(i) % 2, 0:P]
                    what, a, t = units[i]
                    if what == "foxp":
                        ins = act.activation(oT[:, 4 + a // 2, t * P:(t + 1) * P], o, ACT.Copy)
                    elif what == "memp":
                        ins = act.activation(oT[:, 8 + a, t * P:(t + 1) * P], o, ACT.Copy)
                    elif what == "foxs":
                        cols = slice(SEQ + a * NI, SEQ + (a + 1) * NI)
                        for hl in range(2):
                            half = slice(64 * hl, 64 * hl + 64)
                            ins = act.activation(oT[half, 4:8, cols],
                                                 o[half, :].rearrange("p (g i) -> p g i", i=2 * NI)[:, :, hl * NI:(hl + 1) * NI], ACT.Copy)
                    else:
                        for b2 in range(2):
                            b = 2 * a + b2
                            ins = act.activation(oT[:, 8:12, SEQ + b * NI:SEQ + (b + 1) * NI],
                                                 o[:, 64 * b2:64 * b2 + 64].rearrange("p (h i) -> p h i", h=HM), ACT.Copy)
                    ins.then_inc(u_oe, 1)
                elif kind == "gates":
                    act.wait_ge(acc_evac, C_BR)
                    for c in range(6):
                        act.activation(z[:, GATE_SLOT[c], :, :], z[:, GATE_SLOT[c], :, :], ACT.Sigmoid).then_inc(gate_ready, 1)
                elif kind == "turn_merged":
                    for j in range(8):
                        act.wait_ge(mt_ready, j + 1)
                        act.activation(mT[:, j, :], ps[:, 6 + j % 2, 0:TOK], ACT.Copy).then_inc(mt_evac, 1)
                elif kind == "norm2":
                    act.wait_ge(x2_ready, 2)
                    for t in range(T):
                        act.activation(ysb[:, t, :], x2[:, t, :], ACT.Square, accum_out=ss2[:, t:t + 1]).then_inc(ss2_ready, 1)
                elif kind == "turn_x2":
                    for j in range(8):
                        act.wait_ge(x2t_ready, j + 1)
                        act.activation(h2T[:, j, :], ps[:, 6 + j % 2, 0:TOK], ACT.Copy, scale=gk[:, 16 + j:17 + j]).then_inc(x2t_evac, 1)
                elif kind == "route":
                    act.wait_ge(route_in, 1)
                    act.activation(r_e4, r_d4, ACT.Exp)
                    act.activation(r_e2, r_d2, ACT.Exp).then_inc(route_exp, 1)
            act.wait_ge(rstd2_ready, 1)
            for n in range(NG * NE * T):
                t = n % T
                act.wait_ge(gu_ready, n + 1)
                if n >= 2:
                    act.wait_ge(h_ready, n - 1)
                act.activation(act_g[:, n % 2, :], ps[:, 6, 0:DE], ACT.Silu, scale=rstd2[:, t:t + 1]).then_inc(silu_ready, 1)

        @block.vector
        def _(dve):
            chain = Chain(dve, dve_step)
            for kind, *arg in steps:
                i = arg[0] if arg else 0
                if kind == "prep_mem":
                    dve.wait_ge(s_gk, 16)
                    for k in range(KT):
                        dve.wait_ge(act_hi, k + 1)
                        dve.scalar_tensor_tensor(memT_lo[:, k, :], memT[:, k, :], gk[:, 8 + k:9 + k], memT_hi[:, k, :].bitcast(F32),
                                                 ALU.mult, ALU.subtract).then_inc(act_lo, 1)
                elif kind == "prep_x":
                    for k in range(KT):
                        dve.wait_ge(act_hi, KT + k + 1)
                        dve.scalar_tensor_tensor(hT_lo[:, k, :], xT[:, k, :], gk[:, k:k + 1], hT_hi[:, k, :].bitcast(F32),
                                                 ALU.mult, ALU.subtract).then_inc(act_lo, 1)
                    dve.wait_ge(act_hi, 2 * KT + 1)
                    dve.tensor_tensor(ffw_lo[:, :], ffw, ffw_hi[:, :].bitcast(F32), ALU.subtract).then_inc(act_lo, 1)
                    dve.wait_ge(ss_ready, 5)
                    chain(dve.tensor_scalar(ss, ss, 1.0 / D, EPS, ALU.mult, ALU.add))
                    rsqrt(dve, chain, rstd, ss, 5).then_inc(rstd_ready, 1)
                elif kind == "split":
                    dve.wait_ge(hi_ready, i + 1)
                    if i >= PART_SLOTS:
                        dve.wait_ge(gran_used, i - PART_SLOTS + 1)
                    dve.tensor_tensor(w_lo[:, i % PART_SLOTS, :], raw[:, i % RAW_SLOTS, :], w_hi[:, i % PART_SLOTS, :].bitcast(F32),
                                      ALU.subtract).then_inc(lo_ready, 1)
                elif kind == "post" and i in NORMS:
                    _, rows, n, g, order = NORMS[i]
                    dve.wait_ge(sq_ready, order + 1)
                    chain(dve.tensor_reduce(hs[:, 0:rows], zq[:, 0:rows * n].rearrange("p (r n) -> p r n", n=n), AX, ALU.add))
                    chain(dve.tensor_scalar(hs[:, 0:rows], hs[:, 0:rows], 1.0 / n, EPS, ALU.mult, ALU.add))
                    if order:
                        dve.wait_ge(post_done, POSTED[last_norm[order - 1]])
                    rsqrt(dve, chain, hr[:, 0:rows], hs[:, 0:rows], rows).then_inc(hr_ready, 1)
                elif kind == "forget":
                    dve.wait_ge(ff_ready, 1)
                    dve.wait_ge(s_gain, 16)
                    for t in range(T):
                        ins = dve.scalar_tensor_tensor(zf[:, 8 * t:8 * t + 8], ps[:, 6, 8 * t:8 * t + 8], rstd[:, t:t + 1], gn("forget"), ALU.mult, ALU.add)
                    chain(ins)
                    dve.scalar_tensor_tensor(zneg, zf, -1.0, zf, ALU.mult, ALU.min).then_inc(zneg_ready, 1)
                    dve.wait_ge(ln_ready, 1)
                    dve.scalar_tensor_tensor(logf, zf, 0.0, zl, ALU.min, ALU.subtract).then_inc(logf_ready, 1)
                elif kind == "turn" and i % 2 == 1:
                    turn_out(dve, lambda o, a, m: dve.tensor_scalar(o, a, m, None, ALU.mult), i)
                elif kind == "ret_s":
                    dve.wait_ge(ret_s, i + 1)
                    dve.wait_ge(post_done, 6)
                    dve.wait_ge(s_dtab, 16)
                    if i >= 2:
                        dve.wait_ge(ret_o, i - 1)
                    b = 3 + i % 2
                    dve.tensor_tensor(sT[:, i % 2, 0:256], ps[:, b, 0:256], dtab[:, i, :], ALU.mult)
                    dve.tensor_tensor(sT[:, i % 2, 256:384], ps[:, b, 256:384], dtab[:, i, 0:P], ALU.mult)
                    dve.tensor_tensor(sT[:, i % 2, 384:512], ps[:, b, 384:512], cst("decay_s")[:, i * P:(i + 1) * P], ALU.mult).then_inc(ret_m, 1)
                    dve.wait_ge(qdup_ready, 1)
                    dve.wait_ge(s_qtab, 16)
                    dve.tensor_tensor(qmask[:, i % 2, :, :], qdup[:, i, :].unsqueeze(1).to_broadcast([P, 4, P]), qtab[:, i, :, :],
                                      ALU.mult).then_inc(ret_q, 1)
                elif kind == "decay_query":
                    dve.wait_ge(fqs_psum, 1)
                    chain(dve.tensor_tensor(pick8.rearrange("p (b i) -> p b i", b=NB), ps[:, 5, 0:P].rearrange("p (b i) -> p b i", b=NB),
                                            cst("pick").unsqueeze(1).to_broadcast([P, NB, NI]), ALU.mult))
                    dve.tensor_reduce(fq_s, pick8.rearrange("p (b i) -> p b i", b=NB), AX, ALU.add, negate=True).then_inc(fqs_ready, 1)
                elif kind == "ret_o":
                    dve.wait_ge(ret_sq, i + 1)
                    chain(dve.tensor_reduce(rss, osq[:, :].rearrange("p (t v) -> p t v", t=T), AX, ALU.add))
                    chain(dve.tensor_scalar(rss, rss, EPS, None, ALU.add))
                    chain(rsqrt(dve, chain, rrs, rss, T))
                    if i:
                        dve.wait_ge(ret_t, i)
                    rows = orow[:, :].rearrange("p (t v) -> p t v", t=T)
                    chain(dve.tensor_tensor(rows, ps[:, 6, 0:TOK].rearrange("p (t v) -> p t v", t=T), rg[:, :, i * P:(i + 1) * P], ALU.mult))
                    dve.tensor_tensor(rows, rows, rrs.unsqueeze(2).to_broadcast([P, T, P]), ALU.mult).then_inc(ret_rows, 1)
                elif kind == "ret_state":
                    dve.wait_ge(s_state, 16)
                    for h in range(HR):
                        dve.wait_ge(st_ready, h + 1)
                        dve.scalar_tensor_tensor(state[:, :, h, :], state[:, :, h, :], GAMMA_N[h], ps[:, 3 + h, :].rearrange("p (b v) -> p b v", b=4),
                                                 ALU.mult, ALU.add).then_inc(st_done, 1)
                    dve.wait_ge(st_ready, 5)
                    dve.tensor_copy(stp[:, :, :], ps[:, 7, 0:256].rearrange("p (g v) -> p g v", g=2)).then_inc(st_done, 1)
                elif kind == "unit_s":
                    what, a, t = units[i]
                    n = keys(i)
                    dve.wait_ge(u_s, i + 1)
                    if i == 0:
                        dve.wait_ge(sums_evac, 1)
                        dve.wait_ge(work_zero, 1)
                    if i >= 2:
                        dve.wait_ge(u_exp, i - 1)
                    row = s_sb[:, i % 2, :]
                    psc = ps[:, 3 + i % 2, :]
                    if what == "foxp":
                        m = cst("zeros_causal")[:, 256 - n:256]
                        chain(dve.scalar_tensor_tensor(row[:, 0:n], psc[:, 0:n], fq_col[:, 8 * t + a:8 * t + a + 1], m, ALU.add, ALU.add))
                    elif what == "foxs":
                        dve.tensor_scalar(row[:, 0:P], psc[:, 0:P], fq_s[:, a:a + 1], None, ALU.add)
                        m = cst("maskwin")[:, (NB - 1 - a) * NI:(NB - 1 - a) * NI + P]
                        chain(dve.scalar_tensor_tensor(row[:, P:256], psc[:, P:256], fq_s[:, a:a + 1], m, ALU.add, ALU.add))
                    src = row if what[:3] == "fox" else psc
                    dve.tensor_reduce(nmax[:, i % 2:i % 2 + 1], src[:, 0:n], AX, ALU.max, negate=True).then_inc(u_max, 1)
                elif kind == "unit_p":
                    n = keys(i)
                    dve.wait_ge(u_exp, i + 1)
                    chain(dve.reciprocal(rinv[:, i % 2:i % 2 + 1], rsum[:, i % 2:i % 2 + 1]))
                    dve.tensor_scalar(p_sb[:, i % 2, 0:n], p_sb[:, i % 2, 0:n], rinv[:, i % 2:i % 2 + 1], None, ALU.mult).then_inc(u_p, 1)
                elif kind == "merge":
                    c = i - C_BR
                    dve.wait_ge(gran_used, FIRST[i + 1])
                    dve.wait_ge(gate_ready, c + 1)
                    for t in range(T):
                        ins = dve.tensor_tensor(z[:, GATE_SLOT[c], t, :], ps[:, bank_of(i, t), :], z[:, GATE_SLOT[c], t, :], ALU.mult)
                    ins.then_inc(br_mul, 1)
                elif kind == "residual":
                    n = i - C_OUT
                    dve.wait_ge(gran_used, FIRST[i + 1])
                    dve.wait_ge(s_x2, 16)
                    for t in range(T):
                        ins = dve.tensor_tensor(x2[:, t, 512 * n:512 * n + 512], ps[:, bank_of(i, t), :], x2[:, t, 512 * n:512 * n + 512], ALU.add)
                    ins.then_inc(x2_ready, 1)
                elif kind == "norm2":
                    dve.wait_ge(ss2_ready, T)
                    chain(dve.tensor_scalar(ss2, ss2, 1.0 / D, EPS, ALU.mult, ALU.add))
                    rsqrt(dve, chain, rstd2, ss2, T).then_inc(rstd2_ready, 1)
                    dve.wait_ge(rstd2_ready, 1)
                elif kind == "route":
                    route(dve, chain)
            for n in range(NG * NE * T):
                e, t = divmod(n, T)
                dve.wait_ge(silu_ready, n + 1)
                if n >= 2:
                    dve.wait_ge(hT_ready, n - 1)
                dve.scalar_tensor_tensor(act_h[:, n % 2, :], ps[:, 6, DE:2 * DE], comb[:, t * 32 + e:t * 32 + e + 1], act_g[:, n % 2, :],
                                         ALU.mult, ALU.mult).then_inc(h_ready, 1)
                dve.wait_ge(hT_ready, n + 1)
                if n >= 2:
                    dve.wait_ge(dn_done, n - 1)
                dve.tensor_copy(act_T[:, n % 2, :], ps[:, 7, 0:256]).then_inc(hT_evac, 1)
            dve.wait_ge(dn_done, NG * NE * T)
            for t in range(T):
                for n in range(2):
                    ins = dve.tensor_tensor(ysb[:, t, 512 * n:512 * n + 512], ps[:, 2 * t + n, :], x2[:, t, 512 * n:512 * n + 512], ALU.add)
            ins.then_inc(y_ready, 1)

        @block.gpsimd
        def _(pool):
            chain = Chain(pool, pool_step)

            def store(dst, src, s):
                pool.dma_start(dst, src).then_inc(s, 16)

            for kind, *arg in steps:
                i = arg[0] if arg else 0
                if kind == "post":
                    pool.wait_ge(acc_evac, i + 1)
                    if POSTED.get(i, 1) > 1:
                        pool.wait_ge(post_done, POSTED[i] - 1)
                    if i in NORMS:
                        rows_ap, rows, n, g, order = NORMS[i]
                        x = rows_ap.rearrange("p t (h n) -> p (t h) n", n=n)
                        sq = zq[:, 0:rows * n].rearrange("p (r n) -> p r n", n=n)
                        if order:
                            pool.wait_ge(hr_ready, order)
                        pool.tensor_tensor(sq, x, x, ALU.mult).then_inc(sq_ready, 1)
                        pool.wait_ge(hr_ready, order + 1)
                        pool.wait_ge(s_gain, 16)
                        chain(pool.tensor_tensor(x, x, hr[:, 0:rows].unsqueeze(2).to_broadcast([P, rows, n]), ALU.mult))
                        pool.tensor_tensor(x, x, gn(g).unsqueeze(1).to_broadcast([P, rows, n]), ALU.mult).then_inc(post_done, 1)
                        if i == C_MK:
                            pool.wait_ge(post_done, POSTED[i])
                            store(io["mem_k"], mk[:, :, :], s_out)
                        if i == C_FK:
                            pool.wait_ge(post_done, POSTED[i])
                            store(io["fox_k"], fk, s_fk_out)
                    elif i == C_RQK:
                        pool.wait_ge(s_const, 16)
                        rows = rqk.rearrange("p t (h f) -> p t h f", f=64)
                        a, b = rows[:, :, :, 0:32], rows[:, :, :, 32:64]
                        cos = cst("cos").rearrange("p (t f) -> p t f", t=T).unsqueeze(2).to_broadcast([P, T, 8, 32])
                        sin = cst("sin").rearrange("p (t f) -> p t f", t=T).unsqueeze(2).to_broadcast([P, T, 8, 32])
                        ra = zq[:, 0:768].rearrange("p (t h f) -> p t h f", t=T, f=32)
                        rb = zq[:, 768:1536].rearrange("p (t h f) -> p t h f", t=T, f=32)
                        chain(pool.tensor_tensor(ra, a, cos, ALU.mult))
                        chain(pool.tensor_tensor(rb, b, sin, ALU.mult))
                        chain(pool.tensor_tensor(ra, ra, rb, ALU.subtract))
                        chain(pool.tensor_tensor(rb, a, sin, ALU.mult))
                        chain(pool.tensor_tensor(b, b, cos, ALU.mult))
                        chain(pool.tensor_tensor(b, b, rb, ALU.add))
                        pool.tensor_copy(a, ra).then_inc(post_done, 1)
                    elif i == C_RG:
                        rows = rg.rearrange("p t (h v) -> p (t h) v", v=P)
                        pool.tensor_tensor(rows, rows, gn("ret").unsqueeze(1).to_broadcast([P, T * HR, P]), ALU.mult).then_inc(post_done, 1)
                    else:
                        if i == C_MV:
                            store(io["mem_v"], mv[:, :, :], s_out)
                        if i == C_FV:
                            store(io["fox_v"], fv, s_out)
                elif kind == "forget":
                    pool.wait_ge(logf_ready, 1)
                    store(io["logf"], logf, s_out)
                elif kind == "turn" and i == 4:
                    pool.wait_ge(turn_ready, 4)
                    k4 = rqk[:, :, 256:512].rearrange("p t (h f) -> p t h f", f=64)
                    kd = cst("kdec").rearrange("p (t h) -> p t h", t=T).unsqueeze(3).to_broadcast([P, T, HR, 64])
                    chain(pool.tensor_tensor(k4, k4, kd, ALU.mult))
                    for b in range(NB):
                        ins = pool.tensor_tensor(kmask[:, b // 2, :, b % 2, :], rqk[:, 2, 256:512].rearrange("p (h f) -> p h f", f=64),
                                                 cst("inbatch")[:, b:b + 1].unsqueeze(2).to_broadcast([P, HR, 64]), ALU.mult)
                    ins.then_inc(kmask_ready, 1)
                elif kind == "ret_state":
                    pool.wait_ge(st_done, 5)
                    store(io["state_s"], state[:, :, :, :], s_state_out)
                    store(io["state_p"], stp[:, :, :], s_stp_out)
                    pool.wait_ge(s_state_out, 16)
                    pool.wait_ge(s_stp_out, 16)
                    for b in range(3):
                        store(foxc[:, b, :], io["foxc"][b], foxc_in[b])
                    pool.memset(qb_f[:, :, :], 0.0)
                    pool.memset(qb_m[:, :, :], 0.0).then_inc(work_zero, 1)
                    pool.wait_ge(work_zero, 1)
                elif kind == "unit_s":
                    what, a, t = units[i]
                    if what == "foxs":
                        if a >= 2:
                            pool.wait_ge(u_s, i - 1)
                        cols = slice(SEQ + a * NI, SEQ + (a + 1) * NI)
                        pool.wait_ge(even_turned, 4)
                        pool.wait_ge(odd_turned, 4)
                        if a:
                            pool.wait_ge(qb_ready, a)
                        for hl in range(2):
                            half = slice(64 * hl, 64 * hl + 64)
                            if hl:
                                chain(ins)
                            ins = pool.tensor_copy(qb_f[half, a % 2, :].rearrange("p (g c) -> p g c", c=160)[:, :, hl * NI:(hl + 1) * NI],
                                                   fqT[half, :, cols])
                        ins.then_inc(qb_ready, 1)
                    elif what == "mems":
                        if a >= 2:
                            pool.wait_ge(u_s, i - 1)
                        pool.wait_ge(qb_ready, NB + a)
                        for b2 in range(2):
                            b = 2 * a + b2
                            if b2:
                                chain(ins)
                            ins = pool.tensor_copy(qb_m[:, b % 4, :].rearrange("p (h c) -> p h c", c=80)[:, :, 0:NI],
                                                   mqT[:, :, SEQ + b * NI:SEQ + (b + 1) * NI])
                        ins.then_inc(qb_ready, 1)
                elif kind == "unit_v" and units[i][0] == "foxs" and units[i][1] + 3 < NB:
                    b = units[i][1] + 3
                    pool.wait_ge(u_v, i + 1)
                    store(foxc[:, b % 3, :], io["foxc"][b], foxc_in[b % 3])
                elif kind == "merge" and i >= C_BR + 2:
                    c = i - C_BR
                    pool.wait_ge(br_mul, c + 1)
                    if c >= 4:
                        pool.wait_ge(br_add, c - 3)
                    pool.tensor_tensor(z[:, GATE_SLOT[c % 2], :, :], z[:, GATE_SLOT[c % 2], :, :], z[:, GATE_SLOT[c], :, :], ALU.add).then_inc(br_add, 1)
            pool.wait_ge(s_out, 16 * 4)
            pool.wait_ge(s_fk_out, 16)

        @block.tensor
        def _(pe):
            mm = nc.tensor.matmul

            def parts(out, xh, xl, wh, wl, start, stop):
                mm(out, xh, wh, start=start, stop=False, skip_group_check=True)
                mm(out, xh, wl, start=False, stop=False, skip_group_check=True)
                return mm(out, xl, wh, start=False, stop=stop, skip_group_check=True)

            for kind, *arg in steps:
                i = arg[0] if arg else 0
                if kind == "k":
                    c = chunk_of[i]
                    what, kt, nt = CHUNKS[c]
                    if i == FIRST[c]:
                        u = last_user(c)
                        if c == C_BR + 1:
                            pe.wait_ge(u_exp, NU)
                            pe.wait_ge(u_Te, NU)
                        elif u is not None and u < C_BR:
                            pe.wait_ge(acc_evac, u + 1)
                        elif u is not None and u < C_OUT:
                            pe.wait_ge(br_mul, u - C_BR + 1)
                        if c == C_BR:
                            pe.wait_ge(ret_te, HR)
                            pe.wait_ge(u_oe, NGROUP)
                        if what == "out":
                            pe.wait_ge(mt_evac, 8)
                        if c == 0:
                            pe.wait_ge(act_lo, KT)
                        if c == C_RQK:
                            pe.wait_ge(act_lo, 2 * KT)
                    if i < NSPLIT:
                        pe.wait_ge(lo_ready, i + 1)
                    else:
                        pe.wait_ge(raw_in[i % RAW_SLOTS], 16 * (i // RAW_SLOTS + 1))
                    for kk in range(2):
                        k = 2 * (i - FIRST[c]) + kk
                        first, last = k == 0, k == kt - 1
                        cols = slice(512 * kk, 512 * kk + 512)
                        for t in range(nt):
                            tok = slice(t * P, t * P + P)
                            acc = ps[:, bank_of(c, t), :]
                            if i < NSPLIT:
                                xh, xl = (memT_hi, memT_lo) if what == "mem" else (hT_hi, hT_lo)
                                ins = parts(acc, xh[:, k, tok], xl[:, k, tok], w_hi[:, i % PART_SLOTS, cols], w_lo[:, i % PART_SLOTS, cols], first, last)
                            else:
                                x = oT[:, 4 * ((c - C_BR) // 2) + k, tok] if what == "br" else mT[:, k, tok]
                                ins = mm(acc, x, raw[:, i % RAW_SLOTS, cols], start=first, stop=last, skip_group_check=True)
                    ins.then_inc(gran_used, 1)
                elif kind == "forget":
                    pe.wait_ge(act_lo, 2 * KT + 1)
                    for t in range(T):
                        for k in range(KT):
                            tok = slice(t * P, t * P + P)
                            ins = parts(ps[:, 6, 8 * t:8 * t + 8], hT_hi[:, k, tok], hT_lo[:, k, tok], ffw_hi[:, 8 * k:8 * k + 8], ffw_lo[:, 8 * k:8 * k + 8],
                                        k == 0, k == KT - 1)
                    ins.then_inc(ff_ready, 1)
                elif kind == "turn":
                    name, j = turns[i]
                    if i == 0:
                        pe.wait_ge(s_const, 16)
                        pe.wait_ge(acc_evac, C_GATE)
                        pe.wait_ge(zneg_ready, 1)
                    pe.wait_ge(post_done, POSTED[{"rqk": C_RQK, "fq": C_FQ, "fk": C_FK, "mq": C_MQ, "mk": C_MK}[name]])
                    if i >= 5:
                        turn_wait(pe, i - 5)
                    rows = {"rqk": rqk, "fq": fq, "fk": fk, "mq": mq, "mk": mk[:, :, :]}[name]
                    for t in range(2 if name == "mk" else T):
                        ins = nc.tensor.transpose(ps[:, 3 + i % 5, t * P:(t + 1) * P], rows[:, t, j * P:(j + 1) * P], ident)
                    ins.then_inc(turn_ready, 1)
                elif kind == "decay_sums":
                    for j in range(15, 20):
                        turn_wait(pe, j)
                    pe.wait_ge(logf_ready, 1)
                    pe.wait_ge(s_logc, 16)
                    up1 = const[:, CONST["upper"][0]:CONST["upper"][0] + 256]
                    lf = [logf[:, 8 * t:8 * t + 8] for t in range(T)]
                    kw = dict(skip_group_check=True)
                    mm(ps[0:8, 3, 0:256], lf[0], up1, start=True, stop=False, **kw)
                    mm(ps[0:8, 3, 128:256], lf[1], cst("upper"), start=False, stop=True, **kw)
                    for b in range(NB):
                        win = cst("batchwin")[:, (NB - 1 - b) * NI:(NB - 1 - b) * NI + P]
                        mm(ps[0:8, 3, 256:384], logc[:, 8 * b:8 * b + 8], win, start=b == 0, stop=False, **kw)
                    mm(ps[0:8, 3, 256:384], lf[2], cst("upper_in_batch"), start=False, stop=True, **kw)
                    for b in range(NB):
                        mm(ps[0:8, 4 + b // 4, (b % 4) * P:(b % 4) * P + P], logc[:, 8 * b:8 * b + 8], cst("upper"), start=True, stop=True, **kw)
                    mm(ps[:, 6, 0:8], cst("upper"), lf[0], start=True, stop=True, **kw)
                    mm(ps[:, 6, 8:16], cst("ones"), lf[0], start=True, stop=False, **kw)
                    mm(ps[:, 6, 8:16], cst("upper"), lf[1], start=False, stop=True, **kw).then_inc(sums_ready, 1)
                elif kind == "decay_query":
                    pe.wait_ge(sums_evac, 1)
                    sel = cst("headsel")[0:8, :]
                    mm(ps[:, 5, 0:P], sel, nf_n[:, :], start=True, stop=True).then_inc(fqs_psum, 1)
                elif kind == "ret_s":
                    h, b = i, 3 + i % 2
                    pe.wait_ge(sums_evac, 1)
                    if h >= 2:
                        pe.wait_ge(ret_m, h - 1)
                    half = slice(64 * (h % 2), 64 * (h % 2) + 64)
                    q, k = rqkT[half, h // 2, :], rqkT[half, 2 + h // 2, :]
                    mm(ps[:, b, 0:256], k[:, 0:P], q[:, 0:256], start=True, stop=True, skip_group_check=True)
                    mm(ps[:, b, 256:384], k[:, P:256], q[:, P:256], start=True, stop=True, skip_group_check=True)
                    mm(ps[:, b, 384:512], k[:, SEQ:TOK], q[:, SEQ:TOK], start=True, stop=True, skip_group_check=True).then_inc(ret_s, 1)
                elif kind == "ret_o":
                    h = i
                    pe.wait_ge(ret_m, h + 1)
                    pe.wait_ge(ret_q, h + 1)
                    pe.wait_ge(s_state, 16)
                    if h:
                        pe.wait_ge(ret_rows, h)
                    s, v = sT[:, h % 2, :], rv[:, :, h * P:(h + 1) * P]
                    kw = dict(skip_group_check=True)
                    mm(ps[:, 6, 0:P], s[:, 0:P], v[:, 0, :], start=True, stop=True, **kw)
                    mm(ps[:, 6, P:2 * P], s[:, P:2 * P], v[:, 0, :], start=True, stop=False, **kw)
                    mm(ps[:, 6, P:2 * P], s[:, 2 * P:3 * P], v[:, 1, :], start=False, stop=True, **kw)
                    mm(ps[:, 6, 2 * P:3 * P], s[:, 3 * P:4 * P], v[:, 2, :], start=True, stop=False, **kw)
                    for bp in range(4):
                        ins = mm(ps[:, 6, 2 * P:3 * P], qmask[:, h % 2, bp, :], state[:, bp, h, :], start=False, stop=bp == 3, **kw)
                    ins.then_inc(ret_o, 1)
                elif kind == "ret_t":
                    pe.wait_ge(ret_rows, i + 1)
                    if i:
                        pe.wait_ge(ret_te, i)
                    for t in range(T):
                        ins = nc.tensor.transpose(ps[:, 7, t * P:(t + 1) * P], orow[:, t * P:(t + 1) * P], ident)
                    ins.then_inc(ret_t, 1)
                elif kind == "ret_state":
                    pe.wait_ge(kmask_ready, 1)
                    pe.wait_ge(fqs_ready, 1)
                    pe.wait_ge(ret_te, HR)
                    pe.wait_ge(ret_m, HR)
                    for h in range(HR):
                        for bp in range(4):
                            ins = mm(ps[:, 3 + h, bp * P:(bp + 1) * P], kmask[:, bp, h, :, :].rearrange("p a f -> p (a f)"), rv[:, 2, h * P:(h + 1) * P],
                                     start=True, stop=True, skip_group_check=True)
                        ins.then_inc(st_ready, 1)
                    for h in range(HR):
                        half = slice(64 * (h % 2), 64 * (h % 2) + 64)
                        for t in range(2):
                            ins = mm(ps[half, 7, (h // 2) * P:(h // 2) * P + P], rqk[:, t, 256 + h * 64:256 + h * 64 + 64], rv[:, t, h * P:(h + 1) * P],
                                     start=t == 0, stop=t == 1, skip_group_check=True)
                    ins.then_inc(st_ready, 1)
                elif kind == "unit_s":
                    what, a, t = units[i]
                    bank = ps[:, 3 + i % 2, :]
                    kw = dict(skip_group_check=True)
                    if i == 0:
                        pe.wait_ge(st_done, 5)
                    if i >= 2:
                        pe.wait_ge(u_exp, i - 1)
                    if what == "foxp":
                        n, half = keys(i), slice(64 * (a % 2), 64 * (a % 2) + 64)
                        mm(bank[:, 0:n], fqT[half, a // 2, t * P:(t + 1) * P], fkT[half, a // 2, 0:n], start=True, stop=False, **kw)
                        ins = mm(bank[:, 0:n], ident[0:8, a:a + 1].to_broadcast([8, P]), nf_p[:, 0:n], start=False, stop=True, **kw)
                    elif what == "memp":
                        ins = mm(bank[:, 0:256], mqT[:, a, t * P:(t + 1) * P], mkT[:, a, :], start=True, stop=True, **kw)
                    elif what == "foxs":
                        pe.wait_ge(qb_ready, a + 1)
                        pe.wait_ge(foxc_in[a % 3], 16 * (a // 3 + 1))
                        sel = cst("headsel")[0:8, :]
                        for hp in range(4):
                            mm(bank[:, 0:P], qb_f[:, a % 2, hp * P:(hp + 1) * P], foxc[:, a % 3, hp * P:(hp + 1) * P], start=hp == 0, stop=False, **kw)
                        mm(bank[:, 0:P], sel, nf_c[:, a, :], start=False, stop=True, **kw)
                        for hp in range(4):
                            mm(bank[:, P:256], qb_f[:, a % 2, hp * P:(hp + 1) * P], fkT[:, hp, SEQ:TOK], start=hp == 0, stop=False, **kw)
                        ins = mm(bank[:, P:256], sel, nf_n[:, :], start=False, stop=True, **kw)
                    else:
                        pe.wait_ge(qb_ready, NB + a + 1)
                        for b2 in range(2):
                            b = 2 * a + b2
                            pe.wait_ge(memk_in[b % 4], 16 * (b // 4 + 1))
                            for h in range(HM):
                                ins = mm(ps[64 * b2:64 * b2 + 64, 3 + i % 2, 0:256], qb_m[:, b % 4, 64 * h:64 * h + 64], memk[b % 4][:, 256 * h:256 * h + 256],
                                         start=h == 0, stop=h == 3, **kw)
                    ins.then_inc(u_s, 1)
                elif kind == "unit_p":
                    pe.wait_ge(u_p, i + 1)
                    if i:
                        pe.wait_ge(u_Te, i)
                    for k in range(keys(i) // P):
                        ins = nc.tensor.transpose(ps[:, 5, k * P:(k + 1) * P], p_sb[:, i % 2, k * P:(k + 1) * P], ident)
                    ins.then_inc(u_T, 1)
                elif kind == "unit_v":
                    what, a, t = units[i]
                    nk = keys(i) // P
                    g = group_of(i)
                    bank = ps[:, 6 + g % 2, :]
                    pr = pT[:, i % 2, :]
                    kw = dict(skip_group_check=True)
                    pe.wait_ge(u_Te, i + 1)
                    if g >= 2:
                        pe.wait_ge(u_oe, g - 1)
                    if what == "foxp":
                        for k in range(nk):
                            ins = mm(ps[64 * (a % 2):64 * (a % 2) + 64, 6 + g % 2, 0:P], fv[:, k, 64 * a:64 * a + 64], pr[:, k * P:(k + 1) * P],
                                     start=k == 0, stop=k == nk - 1, **kw)
                    elif what == "memp":
                        for k in range(nk):
                            ins = mm(bank[:, 0:P], mv[:, k, a * P:(a + 1) * P], pr[:, k * P:(k + 1) * P], start=k == 0, stop=k == 1, **kw)
                    elif what == "foxs":
                        for hp in range(4):
                            cols = slice(32 * hp, 32 * hp + 32)
                            mm(bank[:, cols], foxc[:, a % 3, 512 + hp * P:512 + (hp + 1) * P], pr[:, cols], start=True, stop=False, **kw)
                            ins = mm(bank[:, cols], fv[:, 2, hp * P:(hp + 1) * P], pr[:, P + 32 * hp:P + 32 * hp + 32], start=False, stop=True, **kw)
                    else:
                        for b2 in range(2):
                            b = 2 * a + b2
                            pe.wait_ge(memv_in[b % 4], 16 * (b // 4 + 1))
                            for h in range(HM):
                                c0 = 64 * b2 + NI * h
                                for k in range(2):
                                    v0 = 512 * k + P * h
                                    ins = mm(bank[:, c0:c0 + NI], memv[b % 4][:, v0:v0 + P], pr[:, k * P + c0:k * P + c0 + NI],
                                             start=k == 0, stop=k == 1, **kw)
                    ins.then_inc(u_v, 1)
                elif kind == "turn_merged":
                    for j in range(8):
                        pe.wait_ge(br_add, 3 + j // 4)
                        if j >= 2:
                            pe.wait_ge(mt_evac, j - 1)
                        for t in range(T):
                            ins = nc.tensor.transpose(ps[:, 6 + j % 2, t * P:(t + 1) * P], z[:, GATE_SLOT[j // 4], t, (j % 4) * P:(j % 4 + 1) * P], ident)
                        ins.then_inc(mt_ready, 1)
                elif kind == "turn_x2":
                    pe.wait_ge(x2_ready, 2)
                    for j in range(8):
                        if j >= 2:
                            pe.wait_ge(x2t_evac, j - 1)
                        for t in range(T):
                            ins = nc.tensor.transpose(ps[:, 6 + j % 2, t * P:(t + 1) * P], x2[:, t, j * P:(j + 1) * P], ident)
                        ins.then_inc(x2t_ready, 1)
                elif kind == "route":
                    pe.wait_ge(x2t_evac, 8)
                    pe.wait_ge(s_wr, 16)
                    for t in range(T):
                        for k in range(KT):
                            ins = mm(ps[:, 7, 64 * t:64 * t + 36], h2T[:, k, t * P:(t + 1) * P], wr[:, k, :], start=k == 0, stop=k == KT - 1, skip_group_check=True)
                    ins.then_inc(lg_ready, 1)
            pe.wait_ge(comb_ready, 1)
            N = NG * NE * T
            for n in range(N + 1):
                if n < N:
                    e, t = divmod(n, T)
                    if n:
                        pe.wait_ge(h_ready, n)
                    pe.wait_ge(ewt_in[e % 2], 16 * (e // 2 + 1))
                    for k in range(KT):
                        ins = mm(ps[:, 6, :], h2T[:, k, t * P:(t + 1) * P], ewt[:, e % 2, 512 * k:512 * k + 512], start=k == 0, stop=k == KT - 1, skip_group_check=True)
                    ins.then_inc(gu_ready, 1)
                if n:
                    m = n - 1
                    e, t = divmod(m, T)
                    pe.wait_ge(h_ready, m + 1)
                    if m:
                        pe.wait_ge(hT_evac, m)
                    for f in range(2):
                        ins = nc.tensor.transpose(ps[:, 7, f * P:(f + 1) * P], act_h[:, m % 2, f * P:(f + 1) * P], ident)
                    ins.then_inc(hT_ready, 1)
                    pe.wait_ge(hT_evac, m + 1)
                    for f in range(2):
                        for q in range(2):
                            o = 4096 + D * f + 512 * q
                            ins = mm(ps[:, 2 * t + q, :], act_T[:, m % 2, f * P:(f + 1) * P], ewt[:, e % 2, o:o + 512], start=e == 0 and f == 0,
                                     stop=e == NG * NE - 1 and f == 1, skip_group_check=True)
                    ins.then_inc(dn_done, 1)


def constants():
    a = np.zeros((P, N_CONST), np.float64)
    p = np.arange(P)

    def put(name, x):
        o, n = CONST[name]
        a[:, o:o + n] = x.reshape(P, n)

    i16, b16 = p % NI, p // NI
    put("ident", np.eye(P))
    put("upper", (p[None, :] >= p[:, None]).astype(float))
    put("ones", np.ones((P, P)))
    win = np.zeros((P, 240))
    win[:, 112:128] = 1.0
    put("batchwin", win)
    win = np.full((P, 240), -BIG)
    win[:, 112:128] = np.where(np.arange(NI)[None, :] <= i16[:, None], 0.0, -BIG)
    put("maskwin", win)
    put("upper_in_batch", ((p[None, :] >= p[:, None]) & (b16[None, :] == b16[:, None])).astype(float))
    zc = np.zeros((P, 256))
    zc[:, 128:] = np.where(p[None, :] <= p[:, None], 0.0, -BIG)
    put("zeros_causal", zc)
    pos = np.concatenate([np.arange(SEQ), PAST + i16]).astype(np.float32)
    inv = (np.float32(10000.0) ** (-np.arange(32, dtype=np.float32) / np.float32(32))).astype(np.float32)
    ang = (pos[:, None] * inv[None, :]).astype(np.float32).astype(np.float64).reshape(T, P, 32).transpose(1, 0, 2)
    put("cos", np.cos(ang))
    put("sin", np.sin(ang))
    lg = np.log1p(-2.0 ** (-5.0 - np.arange(HR)))
    scale = 64 ** -0.5
    diff = p[None, :] - p[:, None]
    dec = np.where((diff >= 0)[:, None, :] & (b16[:, None] == b16[None, :])[:, None, :], np.exp(diff[:, None, :] * lg[None, :, None]), 0.0) * scale
    put("decay_s", dec)
    kd = np.concatenate([SEQ - 1 - np.arange(SEQ), NI - 1 - i16]).reshape(T, P).T
    put("kdec", np.exp(kd[:, :, None] * lg[None, None, :]) * scale)
    put("inbatch", (b16[:, None] == np.arange(NB)[None, :]).astype(float))
    put("headsel", (b16[None, :] == p[:, None]).astype(float))
    put("pick", (i16[:, None] == np.arange(NI)[None, :]).astype(float))
    put("rev4", np.tile(4.0 - np.arange(4), (P, T)))
    put("rev8", np.tile(8.0 - np.arange(8), (P, T)))
    i = np.arange(256)
    d2 = i[None, :] - p[:, None]
    dtab = np.where((d2 >= 0)[:, None, :], np.exp(np.maximum(d2, 0)[:, None, :] * lg[None, :, None]), 0.0) * scale
    qt = np.exp((i16[None, :] + 1.0) * lg[:, None])
    own = (2 * np.arange(4)[None, :, None] + (p // 64)[:, None, None]) == b16[None, None, :]
    qtab = qt[None, :, None, :] * own[:, None, :, :]
    f = np.float32
    return a.astype(f), dtab.astype(f), qtab.astype(f)


OUTS = [("y", (P, T, D)), ("fox_k", (P, T, 512)), ("fox_v", (P, T, 512)), ("logf", (P, T * 8)), ("mem_k", (P, 2, 512)), ("mem_v", (P, 2, 512)),
        ("state_s", (P, 4, HR, P)), ("state_p", (P, 2, P))]


def kernel(**inputs):
    from concourse import bacc
    from concourse.bass_utils import run_bass_kernel_spmd

    g = {k: np.ascontiguousarray(v) for k, v in inputs.items()}
    c = np.ascontiguousarray
    x = np.concatenate([g["x_prompt"].reshape(SEQ, D), g["x_sample"].reshape(P, D)])
    mem = g["mem_prompt"].reshape(NMEM, D)

    def by_token(a, t):
        return c(a.reshape(t, P, -1).transpose(1, 0, 2))

    def turned(a):
        return c(a.reshape(-1, KT, P).transpose(2, 1, 0))

    def granules(w):
        k, n = w.shape
        return w.reshape(k // 256, 2, P, n // 512, 512).transpose(3, 0, 2, 1, 4).reshape(-1, P, GRAN)

    w = g["w_in"][0]
    sizes = [256, 256, 512, 512, 512, 512, 512, 8, 512, 3072]
    cut = np.cumsum([0] + sizes)
    parts = [w[:, cut[i]:cut[i + 1]] for i in range(10)]
    wff = parts[7]
    win = np.concatenate(parts[:7] + parts[8:], axis=1)
    stream = [granules(g["w_mem_kv"][0]), granules(win), granules(g["w_br_ret"][0]), granules(g["w_br_fox"][0]), granules(g["w_br_mem"][0]),
              granules(g["w_out"][0])]
    const, dtab, qtab = constants()
    gk = np.concatenate([g[n].reshape(KT, P).T for n in ("g_norm1", "g_mem_in", "g_norm2")], axis=1)
    gain = np.concatenate([g["g_fox_q"][0], g["g_fox_k"][0], g["g_mem_q"][0], g["g_mem_k"][0], g["g_ret_out"][0], g["b_forget"][0],
                           g["b_route_group"][0], g["b_route_expert"][0]])
    fk = g["cache_fox_k"][0].transpose(0, 2, 3, 1).reshape(NB, 4, P, P).transpose(0, 2, 1, 3).reshape(NB, P, 512)
    foxc = np.concatenate([fk, g["cache_fox_v"][0].reshape(NB, P, 512)], axis=2)
    mkc = g["cache_mem_k"][0].transpose(0, 3, 2, 1).reshape(NB, P, 1024)
    mvc = g["cache_mem_v"][0].reshape(NB, 2, P, 512).transpose(0, 2, 1, 3).reshape(NB, P, 1024)
    gu = np.concatenate([g["w_exp_gate"].reshape(32, KT, P, DE), g["w_exp_up"].reshape(32, KT, P, DE)], axis=3).transpose(0, 2, 1, 3).reshape(32, P, 4096)
    dn = g["w_exp_down"].reshape(32, 2, P, D).transpose(0, 2, 1, 3).reshape(32, P, 2048)
    arrays = {
        "xT": turned(x), "xtok": by_token(x, T), "memT": turned(mem), "memtok": by_token(mem, 2), "gk": c(gk), "gain": c(np.tile(gain, (P, 1))),
        "const": const, "dtab": dtab, "qtab": qtab, "ffw": c(wff.reshape(KT, P, 8).transpose(1, 0, 2).reshape(P, 64)),
        "logc": c(g["cache_fox_logf"][0].transpose(1, 0, 2).reshape(P, 64)), "wstream": c(np.concatenate(stream)),
        "state": c(g["state_ret"][0].reshape(4, 2, HR, 64, P).transpose(1, 3, 0, 2, 4).reshape(P, 4, HR, P)),
        "foxc": c(foxc), "memc": c(np.concatenate([mkc, mvc], axis=2)),
        "wr": c(np.concatenate([g["w_route_group"][0], g["w_route_expert"][0]], axis=1).reshape(KT, P, 36).transpose(1, 0, 2)),
        "wexp": c(np.concatenate([gu, dn], axis=2)),
    }
    nc = bacc.Bacc("TRN2", target_bir_lowering=False, num_devices=1)
    io = {k: nc.dram_tensor(f"in_{k}", v.shape, mybir.dt.from_np(v.dtype), kind="ExternalInput").ap() for k, v in arrays.items()}
    io.update({k: nc.dram_tensor(f"out_{k}", s, F32, kind="ExternalOutput").ap() for k, s in OUTS})
    program(nc, io)
    r = run_bass_kernel_spmd(nc, [{f"in_{k}": v for k, v in arrays.items()}], core_ids=[0]).results[0]
    o = {k: np.asarray(r[f"out_{k}"]).reshape(s) for k, s in OUTS}

    def rows(a):
        return a.transpose(1, 0, 2).reshape(a.shape[0] * a.shape[1], -1)

    y, fk, fv = rows(o["y"]), rows(o["fox_k"]), rows(o["fox_v"])
    lf = rows(o["logf"].reshape(P, T, 8))
    mk, mv = rows(o["mem_k"]), rows(o["mem_v"])
    st_s = o["state_s"].reshape(2, 64, 4, HR, P).transpose(2, 0, 3, 1, 4).reshape(1, NB, HR, 64, P)
    st_p = o["state_p"].reshape(2, 64, 2, P).transpose(2, 0, 1, 3).reshape(1, 1, HR, 64, P)
    return (y[:SEQ].reshape(1, SEQ, D), y[SEQ:].reshape(NB, NI, D), st_p, fk[:SEQ].reshape(1, 1, SEQ, HF, 64), fv[:SEQ].reshape(1, 1, SEQ, HF, 64),
            lf[:SEQ].reshape(1, 1, SEQ, HF), mk.reshape(1, 1, NMEM, HM, P), mv.reshape(1, 1, NMEM, HM, P), st_s,
            fk[SEQ:].reshape(1, NB, NI, HF, 64), fv[SEQ:].reshape(1, NB, NI, HF, 64), lf[SEQ:].reshape(1, NB, NI, HF))
```

```python
from contextlib import ExitStack

import numpy as np

import concourse.bass as bass
from concourse import mybir

ALU = mybir.AluOpType
ACT = mybir.ActivationFunctionType
F32 = mybir.dt.float32
F32R = mybir.dt.float32r
AX = mybir.AxisListType.X

P = 128
D = 1024
KT = D // P
T = 3
TOK = T * P
SEQ, NB, NI, PAST, NMEM = 256, 8, 16, 128, 256
HR, HF, HM = 4, 8, 4
NG, NE, DE = 4, 8, 256
EPS = 1e-6
BIG = 1e30
GRAN = 2 * 512

CHUNKS = ([("mem", 8, 2)] * 2 + [("in", 8, 3)] * 7 + [("gate", 8, 3)] * 6 + [("br", 4, 3)] * 6 + [("out", 8, 3)] * 2)
C_MK, C_MV, C_RQK, C_RV, C_RG, C_FQ, C_FK, C_FV, C_MQ = range(9)
C_GATE, C_BR, C_OUT = 9, 15, 21
FIRST = [sum(c[1] // 2 for c in CHUNKS[:i]) for i in range(len(CHUNKS) + 1)]
NGRAN = FIRST[-1]
NSPLIT = FIRST[C_BR]
RAW_SLOTS, PART_SLOTS = 4, 3

CONST = {}
_at = 0
for _name, _n in (("ident", P), ("upper", P), ("ones", P), ("batchwin", 240), ("maskwin", 240), ("upper_in_batch", P),
                  ("zeros_causal", 256), ("cos", T * 32), ("sin", T * 32), ("decay_s", HR * P), ("kdec", T * HR),
                  ("inbatch", NB), ("headsel", P), ("pick", NI), ("rev4", T * 4), ("rev8", T * 8)):
    CONST[_name] = (_at, _n)
    _at += _n
N_CONST = _at
CONST2 = {}
_at = 0
for _name, _n in (("before", P), ("iota", 256), ("slot", 16), ("first_slot", T * 32), ("quad_slot", 8 * T)):
    CONST2[_name] = (_at, _n)
    _at += _n
N_CONST2 = _at
CAP = 64
PAIRS = 16
QUADS = 8
GAIN = {}
_at = 0
for _name, _n in (("fox_q", 64), ("fox_k", 64), ("mem_q", 128), ("mem_k", 128), ("ret", 128), ("forget", 8), ("route", 36)):
    GAIN[_name] = (_at, _n)
    _at += _n
N_GAIN = _at


def schedule():
    s = []
    ahead = 2
    for g in range(ahead + 1):
        s += [("prep_mem", 2 * g), ("prep_mem", 2 * g + 1), ("split", g)]
    s += [("prep_mem", 6), ("prep_mem", 7)]
    split = ahead + 1
    prep = {1: [("prep_x", k) for k in range(3)], 2: [("prep_x", k) for k in range(3, 6)], 3: [("prep_x", 6), ("prep_x", 7), ("prep_ff",)], 4: [("norm1",)]}

    def granule(g):
        nonlocal split
        while split < min(g + 1 + ahead, NSPLIT):
            s.append(("split", split))
            split += 1
        s.append(("k", g))
        s.extend(prep.get(g, []))

    for c in range(C_GATE):
        for g in range(FIRST[c], FIRST[c + 1]):
            granule(g)
            if g == FIRST[c] and c:
                s.append(("evac", c - 1))
                s.append(("post", c - 1))
    s.append(("forget",))
    s.append(("evac", C_GATE - 1))
    s.append(("post", C_GATE - 1))
    units = [("foxp", hp * 2 + hl, t) for t in range(2) for hp in range(4) for hl in range(2)]
    units += [("memp", h, t) for h in range(HM) for t in range(2)] + [("foxs", b, 0) for b in range(NB)]
    early = len(units)
    units += [("mems", bp, 0) for bp in range(NB // 2)]
    pieces = [("turn", i) for i in range(20)] + [("decay_sums",)]
    pieces += [("ret_s", 0), ("ret_s", 1), ("decay_query",), ("ret_o", 0), ("ret_s", 2), ("ret_o", 1), ("ret_t", 0),
               ("ret_s", 3), ("ret_o", 2), ("ret_t", 1), ("ret_o", 3), ("ret_t", 2), ("ret_t", 3), ("ret_state",)]
    tail = []
    for i in range(len(units) + 2):
        into = pieces if i < early else tail
        if i < len(units):
            into.append(("unit_s", i))
        if 1 <= i <= len(units):
            into.append(("unit_p", i - 1))
        if i >= 2:
            into.append(("unit_v", i - 2))
    weight = {"turn": 0.5, "decay_sums": 3, "ret_s": 2, "ret_o": 4, "ret_t": 1, "ret_state": 0, "decay_query": 1}
    total = sum(weight.get(piece[0], 1) for piece in pieces)
    gates = range(FIRST[C_GATE], FIRST[C_BR])
    placed = passed = 0
    for piece in pieces:
        s.append(piece)
        passed += weight.get(piece[0], 1)
        while placed < len(gates) and (placed + 0.5) * total <= passed * len(gates):
            granule(gates[placed])
            placed += 1
            if placed % 4 == 0:
                s.append(("evac", C_GATE + placed // 4 - 1))
    assert placed == len(gates)
    s += [("mem_caches",), ("gates",)]
    branch = []
    for c in range(C_BR, C_BR + 4):
        branch += [[("k", g)] for g in range(FIRST[c], FIRST[c + 1])]
        branch[-1].append(("merge", c))
    placed = 0
    for i, piece in enumerate(tail):
        s.append(piece)
        while placed < len(branch) and placed * len(tail) < (i + 1) * len(branch):
            s += branch[placed]
            placed += 1
    s.append(("attention_done",))
    for c in range(C_BR + 4, C_OUT):
        s += [("k", g) for g in range(FIRST[c], FIRST[c + 1])] + [("merge", c)]
    s.append(("turn_merged",))
    for c in range(C_OUT, C_OUT + 2):
        s += [("k", g) for g in range(FIRST[c], FIRST[c + 1])] + [("residual", c)]
    s += [("norm2",), ("turn_x2",), ("x_parts",), ("route",)]
    return s, units


MISC = (0, 1, 7)


def moe_schedule():
    s, misc = [], []

    def step(what, a, j):
        s.append((what, a, j, len(misc)))
        misc.append((what, a, j))

    s += [("rank", 0), ("rows_out", 0), ("pick", 0)]
    for k in range(KT):
        step("gather", 0, k)
    for p in range(PAIRS + 2):
        if p >= 2:
            s.append(("y_out", p - 2))
        if p < PAIRS:
            s.append(("slot_weight", p))
            if p % 2 == 0 and p // 2 + 1 < QUADS:
                s.append(("pick", p // 2 + 1))
            s.append(("gu", p))
        if 1 <= p <= PAIRS:
            s.append(("hT_out", p - 1))
        if p < PAIRS:
            s += [("silu", p), ("h", p)]
            if p // 2 + 1 < QUADS:
                for k in range(4 * (p % 2), 4 * (p % 2) + 4):
                    step("gather", p // 2 + 1, k)
        if 1 <= p <= PAIRS:
            s += [("back", p - 1), ("down", p - 1)]
        if p >= 2:
            for j in range(6):
                step("scatter", p - 2, j)
    return s, misc


def program(nc, io):
    steps, units = schedule()
    moe, misc_steps = moe_schedule()
    NU = len(units)
    ctx = ExitStack()
    with ctx:
        base = (nc.sbuf_base + 31) // 32 * 32

        def at(name, shape, offset, dt=F32):
            return nc.alloc_sbuf_tensor_at(name, shape, dt, offset=base + offset)

        def sem(name):
            return ctx.enter_context(nc.semaphore(name))

        KB = 1024
        o_const = 0
        o_gain = o_const + 4 * N_CONST
        o_small = (o_gain + 4 * N_GAIN + 31) // 32 * 32
        o_h = (o_small + 4 * 560 + 31) // 32 * 32
        o_ot = o_h + 24 * KB
        o_raw = o_ot + 18 * KB
        o_z = o_raw + 4 * GRAN * (RAW_SLOTS + 2 * PART_SLOTS)
        o_mkv = o_z + 42 * KB
        o_turned = o_mkv + 8 * KB
        o_sums = o_turned + 28 * KB
        o_work = o_sums + 5632
        end = o_work + 29 * KB
        assert end <= 212863, end

        const = at("const", [P, N_CONST], o_const)
        gain = at("gain", [P, N_GAIN], o_gain)
        small = at("small", [P, 560], o_small)

        def cst(name):
            a, n = CONST[name]
            return const[:, a:a + n]

        def gn(name):
            a, n = GAIN[name]
            return gain[:, a:a + n]

        used = [0]

        def sm(n):
            a = used[0]
            used[0] += n
            assert used[0] <= 560
            return small[:, a:a + n]

        ident = cst("ident")
        gk = sm(24)
        ss, rstd = sm(5), sm(5)
        ffw = sm(64)
        zf, zneg, ze, zl, logf = (sm(24) for _ in range(5))
        logc = sm(64)
        fq_col = sm(16)
        fq_s = sm(8)
        pick8 = sm(P)
        hs, hr = sm(24), sm(24)
        nmax, rsum, rinv = sm(2), sm(2), sm(2)
        rss, rrs = sm(3), sm(3)
        ss2, rstd2, newton = sm(3), sm(3), sm(24)

        hT_hi = at("hT_hi", [P, KT, TOK], o_h, F32R)
        hT_lo = at("hT_lo", [P, KT, TOK], o_h + 12 * KB, F32R)
        mT = at("mT", [P, KT, TOK], o_h)
        x2 = at("x2", [P, T, D], o_h + 12 * KB)
        memk = [at(f"memk{i}", [P, 1024], o_h + 4 * KB * i) for i in range(4)]
        memv = [at(f"memv{i}", [P, 1024], (o_h + 16 * KB, o_work)[i // 2] + 4 * KB * (i % 2)) for i in range(4)]
        memT_hi = at("memT_hi", [P, KT, NMEM], o_ot, F32R)
        memT_lo = at("memT_lo", [P, KT, NMEM], o_ot + 8 * KB, F32R)
        oT = at("oT", [P, 12, TOK], o_ot)
        h2T = at("h2T", [P, KT, TOK], o_ot)
        qtab = at("qtab", [P, HR, 4, P], o_ot + 6 * KB)
        dtab = at("dtab", [P, HR, 256], o_ot + 14 * KB)
        raw = at("raw", [P, RAW_SLOTS, GRAN], o_raw)
        w_hi = at("w_hi", [P, PART_SLOTS, GRAN], o_raw + 4 * GRAN * RAW_SLOTS, F32R)
        w_lo = at("w_lo", [P, PART_SLOTS, GRAN], o_raw + 4 * GRAN * (RAW_SLOTS + PART_SLOTS), F32R)
        z = at("z", [P, 7, T, 512], o_z)
        xT = at("xT", [P, KT, TOK], o_z)
        memT = at("memT", [P, KT, NMEM], o_z + 12 * KB)
        xtok = at("xtok", [P, T, D], o_z + 20 * KB)
        memtok = at("memtok", [P, 2, D], o_z + 32 * KB)
        mk = at("mk", [P, 2, 512], o_mkv)
        mv = at("mv", [P, 2, 512], o_mkv + 4 * KB)
        rqkT = at("rqkT", [P, 4, TOK], o_turned)
        fqT = at("fqT", [P, 4, TOK], o_turned + 6 * KB)
        fkT = at("fkT", [P, 4, TOK], o_turned + 12 * KB)
        mqT = at("mqT", [P, 4, TOK], o_turned + 18 * KB)
        mkT = at("mkT", [P, 4, NMEM], o_turned + 24 * KB)
        nf_p = at("nf_p", [8, 256], o_sums)
        nf_n = at("nf_n", [8, P], o_sums + 1024)
        nf_c = at("nf_c", [8, NB, P], o_sums + 1536)
        state = at("state", [P, 4, HR, P], o_work)
        kmask = at("kmask", [P, 4, HR, 2, 64], o_work + 8 * KB)
        qmask = at("qmask", [P, 2, 4, P], o_work + 16 * KB)
        sT = at("sT", [P, 2, 512], o_work + 20 * KB)
        osq = at("osq", [P, TOK], o_work + 24 * KB)
        orow = at("orow", [P, TOK], o_work + 24 * KB + 1536)
        qdup = at("qdup", [P, HR, P], o_work + 27 * KB)
        stp = at("stp", [P, 2, P], o_work + 24 * KB)
        foxc = [at(f"foxc{i}", [P, 1024], (o_work + 4 * KB * i) if i < 3 else o_mkv) for i in range(4)]
        qb_f = at("qb_f", [P, 2, 640], o_work + 12 * KB)
        s_sb = at("s_sb", [P, 2, 256], o_work + 17 * KB)
        p_sb = at("p_sb", [P, 2, 256], o_work + 19 * KB)
        pT = at("pT", [P, 2, 256], o_work + 21 * KB)
        qb_m = at("qb_m", [P, 4, 320], o_work + 23 * KB)
        wgu = [at(f"wgu{i}", [P, 4096], o_z + 24 * KB * i) for i in range(4)]
        wdn = [at(f"wdn{i}", [P, 2048], o_z + 24 * KB * i + 16 * KB) for i in range(4)]
        wgu_o = [at(f"wgu_o{i}", [P, 6144], o_z + 24 * KB * i) for i in range(2)]
        y_hi = at("y_hi", [P, 2, D], o_z + 96 * KB, F32R)
        y_lo = at("y_lo", [P, 2, D], o_z + 104 * KB, F32R)
        assert o_z + 112 * KB <= end
        x_hi = at("x_hi", [P, T, D], o_raw, F32R)
        x_lo = at("x_lo", [P, T, D], o_raw + 12 * KB, F32R)
        xs = at("xs", [P, 2, KT, 256], o_raw + 24 * KB)
        sq_scratch = at("sq_scratch", [P, D], o_raw + 24 * KB)
        slotrow = at("slotrow", [P, 4, TOK], o_h)
        pick = at("pick_rows", [P, 2, T, 256], o_h + 6 * KB, F32R)
        rt = at("rt", [P, 896], o_ot + 12 * KB)
        const2 = at("const2", [P, N_CONST2], o_ot + 12 * KB + 3584)
        overflow = at("overflow", [1, 8], o_ot + 12 * KB + 3584 + 4 * N_CONST2, mybir.dt.int32)
        assert 12 * KB + 3584 + 4 * N_CONST2 + 32 <= 18 * KB
        act_g = at("act_g", [P, 2, DE], o_ot)
        act_h = at("act_h", [P, 2, DE], o_ot + 2 * KB)
        act_T = at("act_T", [P, 2, 256], o_ot + 4 * KB)
        back = at("back", [P, 2, TOK], o_ot + 6 * KB, F32R)
        back_a = at("back_a", [P, TOK], o_ot + 9 * KB)
        back_b = at("back_b", [P, TOK], o_ot + 9 * KB + 1536)
        wr = at("wr", [P, KT, 36], o_const + 4 * CONST["decay_s"][0])

        ov_h2T = at("ov_h2T", [P, KT, TOK], o_raw + 24 * KB)
        ov_g = at("ov_g", [P, T, DE], o_h)
        ov_h = at("ov_h", [P, T, DE], o_h + 3 * KB)
        ov_hT = at("ov_hT", [P, T, DE], o_h + 6 * KB)

        def cst2(name):
            a, n = CONST2[name]
            return const2[:, a:a + n]

        ps = ctx.enter_context(nc.psum_tensor("banks", [P, 8, 512], F32))

        s_gk, s_xT, s_xtok, s_memtok, s_const, s_gain, s_ffw = (sem(n) for n in ("s_gk", "s_xT", "s_xtok", "s_memtok", "s_const", "s_gain", "s_ffw"))
        s_memT = [sem(f"s_memT{i}") for i in range(2)]
        s_logc, s_qtab, s_dtab, s_state, s_x2, s_wr, s_const2, s_y = (sem(n) for n in ("s_logc", "s_qtab", "s_dtab", "s_state", "s_x2", "s_wr", "s_const2", "s_y"))
        s_out, s_fk_out, s_state_out, s_stp_out, hi_ready, lo_ready, gran_used, ss_ready = (sem(n) for n in ("s_out", "s_fk_out", "s_state_out", "s_stp_out", "hi_ready", "lo_ready", "gran_used", "ss_ready"))
        rstd_ready, act_hi, act_lo, acc_evac, post_done, sq_ready, hr_ready, ff_ready = (sem(n) for n in ("rstd_ready", "act_hi", "act_lo", "acc_evac", "post_done", "sq_ready", "hr_ready", "ff_ready"))
        zneg_ready, ln_ready, logf_ready, turn_ready, even_turned, odd_turned, sums_ready, sums_evac = (sem(n) for n in ("zneg_ready", "ln_ready", "logf_ready", "turn_ready", "even_turned", "odd_turned", "sums_ready", "sums_evac"))
        fqs_psum, fqs_ready, qdup_ready, kmask_ready, ret_s, ret_m, ret_q, ret_o = (sem(n) for n in ("fqs_psum", "fqs_ready", "qdup_ready", "kmask_ready", "ret_s", "ret_m", "ret_q", "ret_o"))
        ret_sq, ret_rows, ret_t, ret_te, st_ready, st_done, work_zero, qb_ready = (sem(n) for n in ("ret_sq", "ret_rows", "ret_t", "ret_te", "st_ready", "st_done", "work_zero", "qb_ready"))
        u_s, u_max, u_exp, u_p, u_T, u_Te, u_v, u_oe = (sem(n) for n in ("u_s", "u_max", "u_exp", "u_p", "u_T", "u_Te", "u_v", "u_oe"))
        gate_ready, br_mul, br_add, mt_ready, mt_evac, x2_ready, ss2_ready, rstd2_ready = (sem(n) for n in ("gate_ready", "br_mul", "br_add", "mt_ready", "mt_evac", "x2_ready", "ss2_ready", "rstd2_ready"))
        x2t_ready, x2t_evac, lg_ready, route_in, route_exp, taken_ready, rank_ready, slots_ready = (sem(n) for n in ("x2t_ready", "x2t_evac", "lg_ready", "route_in", "route_exp", "taken_ready", "rank_ready", "slots_ready"))
        rows_ready, rows_out, xhi_ready, xparts_ready, pick_ready, xg_ready, xs_ready, gu_ready = (sem(n) for n in ("rows_ready", "rows_out", "xhi_ready", "xparts_ready", "pick_ready", "xg_ready", "xs_ready", "gu_ready"))
        silu_ready, h_ready, hT_ready, hT_evac, dn_ready, yhi_ready, ylo_ready, back_ready = (sem(n) for n in ("silu_ready", "h_ready", "hT_ready", "hT_evac", "dn_ready", "yhi_ready", "ylo_ready", "back_ready"))
        overflow_ready, ov_x, ov_xT, ov_gu, ov_silu, ov_hd, ov_tr = (sem(n) for n in ("overflow_ready", "ov_x", "ov_xT", "ov_gu", "ov_silu", "ov_hd", "ov_tr"))
        ov_hTe, ov_down, ov_acc = (sem(n) for n in ("ov_hTe", "ov_down", "ov_acc"))
        ov_w = [sem(f"ov_w{i}") for i in range(2)]
        sc_ready, acc_done, dve_step, pool_step, act_step = (sem(n) for n in ("sc_ready", "acc_done", "dve_step", "pool_step", "act_step"))
        raw_in = [sem(f"raw_in{i}") for i in range(RAW_SLOTS)]
        foxc_in = [sem(f"foxc_in{i}") for i in range(4)]
        memk_in = [sem(f"memk_in{i}") for i in range(4)]
        memv_in = [sem(f"memv_in{i}") for i in range(4)]
        wgu_in = [sem(f"wgu_in{i}") for i in range(4)]
        wdn_in = [sem(f"wdn_in{i}") for i in range(4)]

        class Chain:

            def __init__(self, eng, s):
                self.eng, self.s, self.n = eng, s, 0

            def __call__(self, ins):
                self.n += 1
                ins.then_inc(self.s, 1)
                self.eng.wait_ge(self.s, self.n)

        I32 = mybir.dt.int32

        def rsqrt(dve, chain, out, x, n):
            tmp = newton[:, 0:n]
            chain(dve.tensor_scalar(tmp.bitcast(I32), x.bitcast(I32), 1, None, ALU.logical_shift_right))
            chain(dve.tensor_scalar(out.bitcast(I32), tmp.bitcast(I32), -1.0, float(0x5F3759DF), ALU.mult, ALU.add))
            for step in range(3):
                chain(dve.tensor_tensor(tmp, out, out, ALU.mult))
                chain(dve.scalar_tensor_tensor(tmp, tmp, -0.5, x, ALU.mult, ALU.mult))
                ins = dve.scalar_tensor_tensor(out, tmp, 1.5, out, ALU.add, ALU.mult)
                if step < 2:
                    chain(ins)
            return ins

        def bank_of(c, t):
            if c < C_GATE:
                return 3 * (c % 2) + t
            if c < C_BR + 4:
                return t
            return 3 * ((c - C_BR) % 2) + t

        def last_user(c):
            for b in range(c - 1, -1, -1):
                if bank_of(b, 0) == bank_of(c, 0):
                    return b
            return None

        chunk_of = [c for c in range(len(CHUNKS)) for _ in range(FIRST[c], FIRST[c + 1])]
        Z_OF = {C_RQK: 0, C_RV: 1, C_RG: 2, C_FQ: 3, C_FK: 4, C_FV: 5, C_MQ: 6}
        GATE_SLOT = [3, 4, 6, 0, 1, 2]
        turns = [(name, j) for name in ("rqk", "fq", "fk", "mq", "mk") for j in range(4)]
        GAMMA_N = [float((1.0 - 2.0 ** (-5.0 - h)) ** NI) for h in range(HR)]

        def group_of(i):
            return i // 2 if i < 16 else i - 8

        def last_of(i):
            return i >= 16 or i % 2 == 1

        NGROUP = group_of(NU - 1) + 1
        rqk, rv, rg, fq, fk, fv, mq = (z[:, i, :, :] for i in range(7))
        POSTED = {C_MK: 1, C_RQK: 2, C_RG: 3, C_FQ: 4, C_FK: 5, C_MQ: 6}
        NORMS = {C_MK: (mk[:, :, :], 8, P, "mem_k", 0), C_FQ: (fq, 24, 64, "fox_q", 1), C_FK: (fk, 24, 64, "fox_k", 2), C_MQ: (mq, 12, P, "mem_q", 3)}
        last_norm = [C_MK, C_FQ, C_FK, C_MQ]

        def keys(i):
            return P if units[i][0] == "foxp" and units[i][2] == 0 else 256

        def turn_wait(eng, j):
            eng.wait_ge(odd_turned if j % 2 else even_turned, j // 2 + 1)

        def turn_out(eng, copy, i):
            name, j = turns[i]
            eng.wait_ge(turn_ready, i + 1)
            dst = {"rqk": rqkT, "fq": fqT, "fk": fkT, "mq": mqT, "mk": mkT}[name]
            n = NMEM if name == "mk" else TOK
            scale = {"fq": 64 ** -0.5, "mq": P ** -0.5}.get(name, 1.0)
            copy(dst[:, j, :], ps[:, 3 + i % 5, 0:n], scale).then_inc(odd_turned if i % 2 else even_turned, 1)

        zq = at("zq", [P, T * 512], o_work + 16 * KB)
        scratch = at("scratch", [P, 2, D], o_work)
        ffw_hi = at("ffw_hi", [P, 64], o_work + 8 * KB, F32R)
        ffw_lo = at("ffw_lo", [P, 64], o_work + 8 * KB + 256, F32R)
        block = ctx.enter_context(nc.Block())

        rt_used = [0]

        def R(n):
            a = rt_used[0]
            rt_used[0] += n
            return rt[:, a:a + n]

        r_l, r_d4, r_e4, r_t4, r_oh = R(108), R(12), R(12), R(12), R(12)
        r_m4, r_x4, r_m1, r_m2, r_x1, r_d2, r_e2, r_s4, r_w1, r_w2 = (R(3) for _ in range(10))
        r_le, r_le2, r_t8, r_oh1, r_oh2 = (R(24) for _ in range(5))
        r_s1, r_s2, r_full = R(3), R(3), R(1)
        r_x, r_m1e, r_m2e, r_m = R(96), R(96), R(96), R(96)
        r_over = R(96)
        r_q1, r_q2 = R(24), R(24)
        r_wa, r_wb = R(16), R(16)

        def route(dve, chain):
            def v(a, n):
                return a.rearrange("p (t n) -> p t n", t=T) if n else a

            def wide(a, n):
                return a.unsqueeze(2).to_broadcast([P, T, n])

            def first_best(values, n, mx, tmp, tmp_mx, onehot, rev):
                chain(dve.tensor_reduce(mx, values, AX, ALU.max))
                chain(dve.tensor_tensor(v(tmp, n), values, wide(mx, n), ALU.is_equal))
                chain(dve.tensor_tensor(v(tmp, n), v(tmp, n), v(cst(rev), n), ALU.mult))
                chain(dve.tensor_reduce(tmp_mx, v(tmp, n), AX, ALU.max))
                chain(dve.tensor_tensor(v(onehot, n), v(tmp, n), wide(tmp_mx, n), ALU.is_equal))

            dve.wait_ge(lg_ready, 1)
            L = v(r_l, 36)
            for t in range(T):
                ins = dve.scalar_tensor_tensor(L[:, t, :], ps[:, 7, 64 * t:64 * t + 36], rstd2[:, t:t + 1], gn("route"), ALU.mult, ALU.add)
            chain(ins)
            first_best(L[:, :, 0:4], 4, r_m4, r_t4, r_x4, r_oh, "rev4")
            chain(dve.tensor_tensor(v(r_d4, 4), L[:, :, 0:4], wide(r_m4, 4), ALU.subtract))
            x4 = r_x.rearrange("p (t e g) -> p t e g", t=T, e=NE)
            chain(dve.tensor_tensor(x4, L[:, :, 4:36].rearrange("p t (g e) -> p t e g", g=NG), v(r_oh, 4).unsqueeze(2).to_broadcast([P, T, NE, NG]), ALU.mult))
            chain(dve.tensor_reduce(v(r_le, 8), x4, AX, ALU.add))
            first_best(v(r_le, 8), 8, r_m1, r_t8, r_x1, r_oh1, "rev8")
            chain(dve.scalar_tensor_tensor(r_le2, r_oh1, -BIG, r_le, ALU.mult, ALU.add))
            first_best(v(r_le2, 8), 8, r_m2, r_t8, r_x1, r_oh2, "rev8")
            dve.tensor_tensor(r_d2, r_m2, r_m1, ALU.subtract).then_inc(route_in, 1)
            for oh_e, m_e in ((r_oh1, r_m1e), (r_oh2, r_m2e)):
                chain(dve.tensor_tensor(m_e.rearrange("p (t g e) -> p t g e", t=T, g=NG), v(r_oh, 4).unsqueeze(3).to_broadcast([P, T, NG, NE]),
                                        v(oh_e, 8).unsqueeze(2).to_broadcast([P, T, NG, NE]), ALU.mult))
            dve.tensor_tensor(r_m, r_m1e, r_m2e, ALU.add).then_inc(taken_ready, 1)
            dve.wait_ge(route_exp, 1)
            chain(dve.tensor_reduce(r_s4, v(r_e4, 4), AX, ALU.add))
            chain(dve.tensor_scalar(r_w2, r_e2, 1.0, None, ALU.add))
            chain(dve.tensor_tensor(r_w1, r_w2, r_s4, ALU.mult))
            chain(dve.reciprocal(r_w1, r_w1))
            chain(dve.tensor_tensor(r_w2, r_e2, r_w1, ALU.mult))
            dve.wait_ge(rank_ready, 1)
            dve.wait_ge(s_const2, 16)
            rank, pos, over = ps[:, 6, 0:96], r_x, r_l[:, 0:96]
            chain(dve.tensor_scalar(over, rank, float(CAP), None, ALU.is_ge))
            chain(dve.tensor_tensor(pos, rank, cst2("first_slot"), ALU.add))
            chain(dve.scalar_tensor_tensor(pos, over, 1.0e6, pos, ALU.mult, ALU.add))
            chain(dve.tensor_tensor(r_m, r_m1e, pos, ALU.mult))
            chain(dve.tensor_reduce(r_s1, v(r_m, 32), AX, ALU.add))
            chain(dve.tensor_tensor(pos, r_m2e, pos, ALU.mult))
            chain(dve.tensor_reduce(r_s2, v(pos, 32), AX, ALU.add))
            chain(dve.tensor_reduce(r_full[0:1, :], ps[0:1, 6, 96:128], AX, ALU.max))
            dve.tensor_scalar(overflow[0:1, 0:1], r_full[0:1, :], float(CAP), None, ALU.is_gt).then_inc(overflow_ready, 1)
            q = cst2("quad_slot").rearrange("p (q t) -> p q t", t=T)
            for r_q, r_s in ((r_q1, r_s1), (r_q2, r_s2)):
                ins = dve.tensor_tensor(r_q.rearrange("p (q t) -> p q t", t=T), r_s.unsqueeze(1).to_broadcast([P, QUADS, T]), q, ALU.subtract)
                if r_q is r_q1:
                    chain(ins)
            ins.then_inc(slots_ready, 1)
            dve.wait_ge(slots_ready, 1)

        def overflow_weights(dve, chain):
            for m_e, r_w in ((r_m1e, r_w1), (r_m2e, r_w2)):
                chain(dve.tensor_tensor(m_e, m_e, r_l[:, 0:96], ALU.mult))
                chain(dve.tensor_tensor(m_e.rearrange("p (t n) -> p t n", t=T), m_e.rearrange("p (t n) -> p t n", t=T),
                                        r_w.unsqueeze(2).to_broadcast([P, T, NG * NE]), ALU.mult))
            chain(dve.tensor_tensor(r_over, r_m1e, r_m2e, ALU.add))

        def if_overflow(eng):
            eng.wait_ge(overflow_ready, 1)
            return eng.If(eng.value_load(overflow[0:1, 0:1], min_val=0, max_val=1))

        @block.sync
        def _(sp):
            def load(dst, src, s):
                sp.dma_start(dst, src).then_inc(s, 16)

            def granule(g):
                old = g - RAW_SLOTS
                if old >= NSPLIT:
                    sp.wait_ge(gran_used, old + 1)
                elif old >= 0:
                    sp.wait_ge(lo_ready, old + 1)
                load(raw[:, g % RAW_SLOTS, :], io["wstream"][g], raw_in[g % RAW_SLOTS])

            def load_pair(p):
                if p >= 2:
                    sp.wait_ge(gu_ready, p - 1)
                for e in (2 * p, 2 * p + 1):
                    load(wgu[e % 4][:, :], io["wexp"][e, :, 0:4096], wgu_in[e % 4])
                if p >= 2:
                    sp.wait_ge(dn_ready, p - 1)
                for e in (2 * p, 2 * p + 1):
                    load(wdn[e % 4][:, :], io["wexp"][e, :, 4096:6144], wdn_in[e % 4])

            load(gk, io["gk"], s_gk)
            load(memT[:, 0:4, :], io["memT"][:, 0:4, :], s_memT[0])
            granule(0)
            load(memT[:, 4:8, :], io["memT"][:, 4:8, :], s_memT[1])
            for g in range(1, RAW_SLOTS):
                granule(g)
            load(xT[:, :, :], io["xT"], s_xT)
            load(ffw, io["ffw"], s_ffw)
            load(memtok[:, :, :], io["memtok"], s_memtok)
            load(xtok[:, :, :], io["xtok"], s_xtok)
            for kind, *arg in steps:
                i = arg[0] if arg else 0
                if kind == "k" and i + RAW_SLOTS < NGRAN:
                    granule(i + RAW_SLOTS)
                    if i == 2:
                        load(const[:, :], io["const"], s_const)
                        load(gain[:, :], io["gain"], s_gain)
                        load(logc, io["logc"], s_logc)
                elif kind == "post" and i == C_MV:
                    sp.wait_ge(gran_used, FIRST[2])
                    sp.wait_ge(ss_ready, 5)
                    sp.wait_ge(act_lo, 17)
                    load(qtab[:, :, :, :], io["qtab"], s_qtab)
                    load(dtab[:, :, :], io["dtab"], s_dtab)
                elif kind == "forget":
                    sp.wait_ge(ff_ready, 1)
                    load(state[:, :, :, :], io["state"], s_state)
                elif kind == "mem_caches":
                    sp.wait_ge(gran_used, NSPLIT)
                    for b in range(4):
                        load(memk[b][:, :], io["memc"][b, :, 0:1024], memk_in[b])
                    for b in range(2):
                        load(memv[b][:, :], io["memc"][b, :, 1024:2048], memv_in[b])
                elif kind == "unit_v" and units[i][0] == "foxs" and units[i][1] == NB - 1:
                    sp.wait_ge(u_v, i + 1)
                    for b in range(2, 4):
                        load(memv[b][:, :], io["memc"][b, :, 1024:2048], memv_in[b])
                elif kind == "unit_v" and units[i][0] == "mems" and units[i][1] < 2:
                    a = units[i][1]
                    sp.wait_ge(u_v, i + 1)
                    for b in (2 * a + 4, 2 * a + 5):
                        load(memv[b % 4][:, :], io["memc"][b, :, 1024:2048], memv_in[b % 4])
                elif kind == "unit_s" and units[i][0] == "mems" and units[i][1] < 2:
                    a = units[i][1]
                    sp.wait_ge(u_s, i + 1)
                    for b in (2 * a + 4, 2 * a + 5):
                        load(memk[b % 4][:, :], io["memc"][b, :, 0:1024], memk_in[b % 4])
                elif kind == "attention_done":
                    sp.wait_ge(u_v, NU)
                    load(x2[:, :, :], io["xtok"], s_x2)
                    sp.wait_ge(u_oe, NGROUP)
                    load_pair(1)
                elif kind == "turn_merged":
                    sp.wait_ge(gran_used, FIRST[C_OUT])
                    load(wr[:, :, :], io["wr"], s_wr)
                    load(const2[:, :], io["const2"], s_const2)
            sp.wait_ge(mt_ready, 8)
            for p in [0] + list(range(2, PAIRS)):
                load_pair(p)
            with if_overflow(sp):
                for b in range(2):
                    sp.wait_ge(dn_ready, PAIRS)
                    load(wgu_o[b][:, :], io["wexp"][b], ov_w[b])
                with sp.Fori(0, NG * NE // 2 - 1) as i:
                    for b in range(2):
                        sp.wait_ge(ov_down, 12 * i + 6 * b + 6)
                        load(wgu_o[b][:, :], io["wexp"][bass.ds(2 * i + b + 2, 1)].rearrange("a p c -> p (a c)"), ov_w[b])
                sp.wait_ge(ov_acc, 6 * NG * NE)
            with sp.Else():
                pass
            for t in range(T):
                sp.wait_ge(acc_done, 6 * (PAIRS - 1) + 2 * t + 2)
                sp.dma_start(io["y"][:, t, :], x2[:, t, :]).then_inc(s_y, 16)
            sp.wait_ge(s_y, 16 * T)

        @block.scalar
        def _(act):
            chain = Chain(act, act_step)
            for kind, *arg in steps:
                i = arg[0] if arg else 0
                if kind == "prep_mem":
                    act.wait_ge(s_memT[i // 4], 16)
                    act.wait_ge(s_gk, 16)
                    act.activation(memT_hi[:, i, :], memT[:, i, :], ACT.Copy, scale=gk[:, 8 + i:9 + i]).then_inc(act_hi, 1)
                elif kind == "prep_x":
                    act.wait_ge(s_xT, 16)
                    act.activation(hT_hi[:, i, :], xT[:, i, :], ACT.Copy, scale=gk[:, i:i + 1]).then_inc(act_hi, 1)
                elif kind == "prep_ff":
                    act.wait_ge(s_ffw, 16)
                    act.activation(ffw_hi[:, :], ffw, ACT.Copy).then_inc(act_hi, 1)
                elif kind == "norm1":
                    act.wait_ge(s_memtok, 16)
                    for t in range(2):
                        act.activation(scratch[:, t, :], memtok[:, t, :], ACT.Square, accum_out=ss[:, 3 + t:4 + t]).then_inc(ss_ready, 1)
                    act.wait_ge(s_xtok, 16)
                    for t in range(T):
                        act.wait_ge(ss_ready, 1 + t)
                        act.activation(scratch[:, t % 2, :], xtok[:, t, :], ACT.Square, accum_out=ss[:, t:t + 1]).then_inc(ss_ready, 1)
                elif kind == "split":
                    act.wait_ge(raw_in[i % RAW_SLOTS], 16 * (i // RAW_SLOTS + 1))
                    if i >= PART_SLOTS:
                        act.wait_ge(gran_used, i - PART_SLOTS + 1)
                    act.activation(w_hi[:, i % PART_SLOTS, :], raw[:, i % RAW_SLOTS, :], ACT.Copy).then_inc(hi_ready, 1)
                elif kind == "evac":
                    act.wait_ge(rstd_ready, 1)
                    act.wait_ge(gran_used, FIRST[i + 1])
                    if i < C_RQK:
                        dst = (mk, mv)[i][:, :, :]
                    elif i < C_GATE:
                        dst = z[:, Z_OF[i], :, :]
                    else:
                        dst = z[:, GATE_SLOT[i - C_GATE], :, :]
                    if i == C_RQK:
                        act.wait_ge(act_lo, 17)
                    elif i == C_GATE:
                        act.wait_ge(turn_ready, 8)
                    elif i == C_GATE + 1:
                        act.wait_ge(turn_ready, 12)
                        act.wait_ge(s_fk_out, 16)
                    elif i == C_GATE + 2:
                        act.wait_ge(turn_ready, 16)
                    elif i >= C_GATE + 3:
                        act.wait_ge(st_ready, 5)
                        act.wait_ge(kmask_ready, 1)
                        act.wait_ge(ret_rows, HR)
                    f = ACT.Silu if i == C_RG else ACT.Copy
                    for t in range(CHUNKS[i][2]):
                        sc = rstd[:, 3 + t:4 + t] if i < C_RQK else rstd[:, t:t + 1]
                        ins = act.activation(dst[:, t, :], ps[:, bank_of(i, t), :], f, scale=sc)
                    ins.then_inc(acc_evac, 1)
                elif kind == "forget":
                    act.wait_ge(zneg_ready, 1)
                    chain(act.activation(ze, zneg, ACT.Exp))
                    act.activation(zl, ze, ACT.Ln, bias=1.0).then_inc(ln_ready, 1)
                elif kind == "turn":
                    if i % 2 == 0:
                        turn_out(act, lambda o, a, m: act.activation(o, a, ACT.Copy, scale=m), i)
                    if i == 2:
                        act.wait_ge(even_turned, 1)
                        act.wait_ge(odd_turned, 1)
                        for hl in range(2):
                            for b2 in range(2):
                                ins = act.activation(qdup[64 * b2:64 * b2 + 64, hl::2, :], rqkT[64 * hl:64 * hl + 64, 0:2, SEQ:TOK], ACT.Copy)
                        ins.then_inc(qdup_ready, 1)
                elif kind == "decay_sums":
                    act.wait_ge(sums_ready, 1)
                    act.activation(nf_p[:, :], ps[0:8, 3, 0:256], ACT.Copy, scale=-1.0)
                    act.activation(nf_n[:, :], ps[0:8, 3, 256:384], ACT.Copy, scale=-1.0)
                    for q in range(2):
                        act.activation(nf_c[:, 4 * q:4 * q + 4, :], ps[0:8, 4 + q, :].rearrange("p (b j) -> p b j", b=4), ACT.Copy, scale=-1.0)
                    act.activation(fq_col, ps[:, 6, 0:16], ACT.Copy).then_inc(sums_evac, 1)
                elif kind == "ret_o":
                    act.wait_ge(ret_o, i + 1)
                    if i:
                        act.wait_ge(ret_rows, i)
                    act.activation(osq[:, :], ps[:, 6, 0:TOK], ACT.Square, scale=float(P) ** -0.5).then_inc(ret_sq, 1)
                elif kind == "ret_t":
                    act.wait_ge(ret_t, i + 1)
                    act.activation(oT[:, i, :], ps[:, 7, 0:TOK], ACT.Copy).then_inc(ret_te, 1)
                elif kind == "unit_s":
                    act.wait_ge(u_max, i + 1)
                    n = keys(i)
                    src = s_sb[:, i % 2, 0:n] if units[i][0][:3] == "fox" else ps[:, 3 + i % 2, 0:n]
                    if i >= 2:
                        act.wait_ge(u_T, i - 1)
                    act.activation(p_sb[:, i % 2, 0:n], src, ACT.Exp, bias=nmax[:, i % 2:i % 2 + 1],
                                   accum_out=rsum[:, i % 2:i % 2 + 1]).then_inc(u_exp, 1)
                elif kind == "unit_p":
                    n = keys(i)
                    act.wait_ge(u_T, i + 1)
                    if i >= 2:
                        act.wait_ge(u_v, i - 1)
                    act.activation(pT[:, i % 2, 0:n], ps[:, 5, 0:n], ACT.Copy).then_inc(u_Te, 1)
                elif kind == "unit_v" and last_of(i):
                    act.wait_ge(u_v, i + 1)
                    o = ps[:, 6 + group_of(i) % 2, 0:P]
                    what, a, t = units[i]
                    if what == "foxp":
                        ins = act.activation(oT[:, 4 + a // 2, t * P:(t + 1) * P], o, ACT.Copy)
                    elif what == "memp":
                        ins = act.activation(oT[:, 8 + a, t * P:(t + 1) * P], o, ACT.Copy)
                    elif what == "foxs":
                        cols = slice(SEQ + a * NI, SEQ + (a + 1) * NI)
                        for hl in range(2):
                            half = slice(64 * hl, 64 * hl + 64)
                            ins = act.activation(oT[half, 4:8, cols],
                                                 o[half, :].rearrange("p (g i) -> p g i", i=2 * NI)[:, :, hl * NI:(hl + 1) * NI], ACT.Copy)
                    else:
                        for b2 in range(2):
                            b = 2 * a + b2
                            ins = act.activation(oT[:, 8:12, SEQ + b * NI:SEQ + (b + 1) * NI],
                                                 o[:, 64 * b2:64 * b2 + 64].rearrange("p (h i) -> p h i", h=HM), ACT.Copy)
                    ins.then_inc(u_oe, 1)
                elif kind == "gates":
                    act.wait_ge(acc_evac, C_BR)
                    for c in range(6):
                        act.activation(z[:, GATE_SLOT[c], :, :], z[:, GATE_SLOT[c], :, :], ACT.Sigmoid).then_inc(gate_ready, 1)
                elif kind == "turn_merged":
                    for j in range(8):
                        act.wait_ge(mt_ready, j + 1)
                        act.activation(mT[:, j, :], ps[:, 6 + j % 2, 0:TOK], ACT.Copy).then_inc(mt_evac, 1)
                elif kind == "norm2":
                    act.wait_ge(x2_ready, 2)
                    for t in range(T):
                        if t:
                            act.wait_ge(ss2_ready, t)
                        act.activation(sq_scratch[:, :], x2[:, t, :], ACT.Square, accum_out=ss2[:, t:t + 1]).then_inc(ss2_ready, 1)
                elif kind == "x_parts":
                    act.wait_ge(rstd2_ready, 1)
                    for t in range(T):
                        act.activation(x_hi[:, t, :], x2[:, t, :], ACT.Copy, scale=rstd2[:, t:t + 1]).then_inc(xhi_ready, 1)
                elif kind == "turn_x2":
                    for j in range(8):
                        act.wait_ge(x2t_ready, j + 1)
                        act.activation(h2T[:, j, :], ps[:, 6 + j % 2, 0:TOK], ACT.Copy, scale=gk[:, 16 + j:17 + j]).then_inc(x2t_evac, 1)
                elif kind == "route":
                    act.wait_ge(route_in, 1)
                    act.activation(r_e4, r_d4, ACT.Exp)
                    act.activation(r_e2, r_d2, ACT.Exp).then_inc(route_exp, 1)
            for what, a, *m in moe:
                if what == "rows_out":
                    act.wait_ge(rows_ready, 1)
                    for j in range(4):
                        act.activation(slotrow[:, j, :], ps[:, j, 0:TOK], ACT.Copy).then_inc(rows_out, 1)
                elif what == "gather":
                    act.wait_ge(xg_ready, 8 * a + m[0] + 1)
                    act.activation(xs[:, a % 2, m[0], :], ps[:, MISC[m[1] % 3], 0:256], ACT.Copy, scale=gk[:, 16 + m[0]:17 + m[0]]).then_inc(xs_ready, 1)
                elif what == "silu":
                    act.wait_ge(gu_ready, a + 1)
                    if a >= 2:
                        act.wait_ge(h_ready, a - 1)
                    act.activation(act_g[:, a % 2, :], ps[:, 2 + a % 2, 0:DE], ACT.Silu).then_inc(silu_ready, 1)
                elif what == "y_out":
                    act.wait_ge(dn_ready, a + 1)
                    if a >= 2:
                        act.wait_ge(acc_done, 6 * (a - 1))
                    for n in range(2):
                        act.activation(y_hi[:, a % 2, 512 * n:512 * n + 512], ps[:, 5 + n, :], ACT.Copy).then_inc(yhi_ready, 1)
            with if_overflow(act):
                for k in range(KT):
                    act.wait_ge(ov_x, k + 1)
                    act.activation(ov_h2T[:, k, :], ps[:, k, 0:TOK], ACT.Copy, scale=gk[:, 16 + k:17 + k]).then_inc(ov_xT, 1)
                with act.Fori(0, NG * NE) as e:
                    for t in range(T):
                        act.wait_ge(ov_gu, 3 * e + t + 1)
                        act.activation(ov_g[:, t, :], ps[:, t, 0:DE], ACT.Silu).then_inc(ov_silu, 1)
                    for t in range(T):
                        act.wait_ge(ov_tr, 3 * e + t + 1)
                        act.activation(ov_hT[:, t, :], ps[:, 3 + t, 0:DE], ACT.Copy).then_inc(ov_hTe, 1)
            with act.Else():
                pass

        @block.vector
        def _(dve):
            chain = Chain(dve, dve_step)
            for kind, *arg in steps:
                i = arg[0] if arg else 0
                if kind == "prep_mem":
                    dve.wait_ge(act_hi, i + 1)
                    dve.scalar_tensor_tensor(memT_lo[:, i, :], memT[:, i, :], gk[:, 8 + i:9 + i], memT_hi[:, i, :].bitcast(F32),
                                             ALU.mult, ALU.subtract).then_inc(act_lo, 1)
                elif kind == "prep_x":
                    dve.wait_ge(act_hi, KT + i + 1)
                    dve.scalar_tensor_tensor(hT_lo[:, i, :], xT[:, i, :], gk[:, i:i + 1], hT_hi[:, i, :].bitcast(F32),
                                             ALU.mult, ALU.subtract).then_inc(act_lo, 1)
                elif kind == "prep_ff":
                    dve.wait_ge(act_hi, 2 * KT + 1)
                    dve.tensor_tensor(ffw_lo[:, :], ffw, ffw_hi[:, :].bitcast(F32), ALU.subtract).then_inc(act_lo, 1)
                elif kind == "norm1":
                    dve.wait_ge(ss_ready, 5)
                    chain(dve.tensor_scalar(ss, ss, 1.0 / D, EPS, ALU.mult, ALU.add))
                    rsqrt(dve, chain, rstd, ss, 5).then_inc(rstd_ready, 1)
                elif kind == "split":
                    dve.wait_ge(hi_ready, i + 1)
                    if i >= PART_SLOTS:
                        dve.wait_ge(gran_used, i - PART_SLOTS + 1)
                    dve.tensor_tensor(w_lo[:, i % PART_SLOTS, :], raw[:, i % RAW_SLOTS, :], w_hi[:, i % PART_SLOTS, :].bitcast(F32),
                                      ALU.subtract).then_inc(lo_ready, 1)
                elif kind == "post" and i in NORMS:
                    _, rows, n, g, order = NORMS[i]
                    dve.wait_ge(sq_ready, order + 1)
                    chain(dve.tensor_reduce(hs[:, 0:rows], zq[:, 0:rows * n].rearrange("p (r n) -> p r n", n=n), AX, ALU.add))
                    chain(dve.tensor_scalar(hs[:, 0:rows], hs[:, 0:rows], 1.0 / n, EPS, ALU.mult, ALU.add))
                    if order:
                        dve.wait_ge(post_done, POSTED[last_norm[order - 1]])
                    rsqrt(dve, chain, hr[:, 0:rows], hs[:, 0:rows], rows).then_inc(hr_ready, 1)
                elif kind == "forget":
                    dve.wait_ge(ff_ready, 1)
                    dve.wait_ge(s_gain, 16)
                    for t in range(T):
                        ins = dve.scalar_tensor_tensor(zf[:, 8 * t:8 * t + 8], ps[:, 6, 8 * t:8 * t + 8], rstd[:, t:t + 1], gn("forget"), ALU.mult, ALU.add)
                    chain(ins)
                    dve.scalar_tensor_tensor(zneg, zf, -1.0, zf, ALU.mult, ALU.min).then_inc(zneg_ready, 1)
                    dve.wait_ge(ln_ready, 1)
                    dve.scalar_tensor_tensor(logf, zf, 0.0, zl, ALU.min, ALU.subtract).then_inc(logf_ready, 1)
                elif kind == "turn" and i % 2 == 1:
                    turn_out(dve, lambda o, a, m: dve.tensor_scalar(o, a, m, None, ALU.mult), i)
                elif kind == "ret_s":
                    dve.wait_ge(ret_s, i + 1)
                    dve.wait_ge(post_done, 6)
                    dve.wait_ge(s_dtab, 16)
                    if i >= 2:
                        dve.wait_ge(ret_o, i - 1)
                    b = 3 + i % 2
                    dve.tensor_tensor(sT[:, i % 2, 0:256], ps[:, b, 0:256], dtab[:, i, :], ALU.mult)
                    dve.tensor_tensor(sT[:, i % 2, 256:384], ps[:, b, 256:384], dtab[:, i, 0:P], ALU.mult)
                    dve.tensor_tensor(sT[:, i % 2, 384:512], ps[:, b, 384:512], cst("decay_s")[:, i * P:(i + 1) * P], ALU.mult).then_inc(ret_m, 1)
                    dve.wait_ge(qdup_ready, 1)
                    dve.wait_ge(s_qtab, 16)
                    dve.tensor_tensor(qmask[:, i % 2, :, :], qdup[:, i, :].unsqueeze(1).to_broadcast([P, 4, P]), qtab[:, i, :, :],
                                      ALU.mult).then_inc(ret_q, 1)
                elif kind == "decay_query":
                    dve.wait_ge(fqs_psum, 1)
                    chain(dve.tensor_tensor(pick8.rearrange("p (b i) -> p b i", b=NB), ps[:, 5, 0:P].rearrange("p (b i) -> p b i", b=NB),
                                            cst("pick").unsqueeze(1).to_broadcast([P, NB, NI]), ALU.mult))
                    dve.tensor_reduce(fq_s, pick8.rearrange("p (b i) -> p b i", b=NB), AX, ALU.add, negate=True).then_inc(fqs_ready, 1)
                elif kind == "ret_o":
                    dve.wait_ge(ret_sq, i + 1)
                    chain(dve.tensor_reduce(rss, osq[:, :].rearrange("p (t v) -> p t v", t=T), AX, ALU.add))
                    chain(dve.tensor_scalar(rss, rss, EPS, None, ALU.add))
                    chain(rsqrt(dve, chain, rrs, rss, T))
                    if i:
                        dve.wait_ge(ret_t, i)
                    rows = orow[:, :].rearrange("p (t v) -> p t v", t=T)
                    chain(dve.tensor_tensor(rows, ps[:, 6, 0:TOK].rearrange("p (t v) -> p t v", t=T), rg[:, :, i * P:(i + 1) * P], ALU.mult))
                    dve.tensor_tensor(rows, rows, rrs.unsqueeze(2).to_broadcast([P, T, P]), ALU.mult).then_inc(ret_rows, 1)
                elif kind == "ret_state":
                    dve.wait_ge(s_state, 16)
                    for h in range(HR):
                        dve.wait_ge(st_ready, h + 1)
                        dve.scalar_tensor_tensor(state[:, :, h, :], state[:, :, h, :], GAMMA_N[h], ps[:, 3 + h, :].rearrange("p (b v) -> p b v", b=4),
                                                 ALU.mult, ALU.add).then_inc(st_done, 1)
                    dve.wait_ge(st_ready, 5)
                    dve.tensor_copy(stp[:, :, :], ps[:, 7, 0:256].rearrange("p (g v) -> p g v", g=2)).then_inc(st_done, 1)
                elif kind == "unit_s":
                    what, a, t = units[i]
                    n = keys(i)
                    dve.wait_ge(u_s, i + 1)
                    if i == 0:
                        dve.wait_ge(sums_evac, 1)
                    if i >= 2:
                        dve.wait_ge(u_exp, i - 1)
                    row = s_sb[:, i % 2, :]
                    psc = ps[:, 3 + i % 2, :]
                    if what == "foxp":
                        m = cst("zeros_causal")[:, 256 - n:256]
                        chain(dve.scalar_tensor_tensor(row[:, 0:n], psc[:, 0:n], fq_col[:, 8 * t + a:8 * t + a + 1], m, ALU.add, ALU.add))
                    elif what == "foxs":
                        dve.tensor_scalar(row[:, 0:P], psc[:, 0:P], fq_s[:, a:a + 1], None, ALU.add)
                        m = cst("maskwin")[:, (NB - 1 - a) * NI:(NB - 1 - a) * NI + P]
                        chain(dve.scalar_tensor_tensor(row[:, P:256], psc[:, P:256], fq_s[:, a:a + 1], m, ALU.add, ALU.add))
                    src = row if what[:3] == "fox" else psc
                    dve.tensor_reduce(nmax[:, i % 2:i % 2 + 1], src[:, 0:n], AX, ALU.max, negate=True).then_inc(u_max, 1)
                elif kind == "unit_p":
                    n = keys(i)
                    dve.wait_ge(u_exp, i + 1)
                    chain(dve.reciprocal(rinv[:, i % 2:i % 2 + 1], rsum[:, i % 2:i % 2 + 1]))
                    dve.tensor_scalar(p_sb[:, i % 2, 0:n], p_sb[:, i % 2, 0:n], rinv[:, i % 2:i % 2 + 1], None, ALU.mult).then_inc(u_p, 1)
                elif kind == "merge":
                    c = i - C_BR
                    dve.wait_ge(gran_used, FIRST[i + 1])
                    dve.wait_ge(gate_ready, c + 1)
                    for t in range(T):
                        ins = dve.tensor_tensor(z[:, GATE_SLOT[c], t, :], ps[:, bank_of(i, t), :], z[:, GATE_SLOT[c], t, :], ALU.mult)
                    ins.then_inc(br_mul, 1)
                elif kind == "residual":
                    n = i - C_OUT
                    dve.wait_ge(gran_used, FIRST[i + 1])
                    dve.wait_ge(s_x2, 16)
                    for t in range(T):
                        ins = dve.tensor_tensor(x2[:, t, 512 * n:512 * n + 512], ps[:, bank_of(i, t), :], x2[:, t, 512 * n:512 * n + 512], ALU.add)
                    ins.then_inc(x2_ready, 1)
                elif kind == "norm2":
                    dve.wait_ge(ss2_ready, T)
                    chain(dve.tensor_scalar(ss2, ss2, 1.0 / D, EPS, ALU.mult, ALU.add))
                    rsqrt(dve, chain, rstd2, ss2, T).then_inc(rstd2_ready, 1)
                    dve.wait_ge(rstd2_ready, 1)
                elif kind == "x_parts":
                    for t in range(T):
                        dve.wait_ge(xhi_ready, t + 1)
                        dve.scalar_tensor_tensor(x_lo[:, t, :], x2[:, t, :], rstd2[:, t:t + 1], x_hi[:, t, :].bitcast(F32), ALU.mult, ALU.subtract).then_inc(xparts_ready, 1)
                elif kind == "route":
                    route(dve, chain)
            overflow_weights(dve, chain)
            for what, a, *m in moe:
                if what == "pick":
                    if a >= 2:
                        dve.wait_ge(xs_ready, 8 * (a - 1))
                    for t in range(T):
                        col = 3 * a + t
                        chain(dve.tensor_scalar(pick[:, a % 2, t, :], cst2("iota"), r_q1[:, col:col + 1], None, ALU.is_equal))
                        dve.scalar_tensor_tensor(pick[:, a % 2, t, :], cst2("iota"), r_q2[:, col:col + 1], pick[:, a % 2, t, :].bitcast(F32),
                                                 ALU.is_equal, ALU.add).then_inc(pick_ready, 1)
                elif what == "slot_weight":
                    if a == 0:
                        dve.wait_ge(rows_out, 4)
                    sid = cst2("slot")[:, a:a + 1]
                    chain(dve.scalar_tensor_tensor(back_a[:, :], slotrow[:, 0, :], sid, slotrow[:, 2, :], ALU.is_equal, ALU.mult, accum_out=r_wa[:, a:a + 1]))
                    chain(dve.scalar_tensor_tensor(back_a[:, :], slotrow[:, 1, :], sid, slotrow[:, 3, :], ALU.is_equal, ALU.mult, accum_out=r_wb[:, a:a + 1]))
                    chain(dve.tensor_tensor(r_wa[:, a:a + 1], r_wa[:, a:a + 1], r_wb[:, a:a + 1], ALU.add))
                elif what == "y_out":
                    for n in range(2):
                        dve.wait_ge(yhi_ready, 2 * a + n + 1)
                        if a >= 2:
                            dve.wait_ge(acc_done, 6 * (a - 1))
                        cols = slice(512 * n, 512 * n + 512)
                        dve.tensor_tensor(y_lo[:, a % 2, cols], ps[:, 5 + n, :], y_hi[:, a % 2, cols].bitcast(F32), ALU.subtract).then_inc(ylo_ready, 1)
                elif what == "hT_out":
                    dve.wait_ge(hT_ready, a + 1)
                    if a >= 2:
                        dve.wait_ge(dn_ready, a - 1)
                    dve.tensor_copy(act_T[:, a % 2, :], ps[:, 4, 0:256]).then_inc(hT_evac, 1)
                elif what == "h":
                    dve.wait_ge(silu_ready, a + 1)
                    if a >= 2:
                        dve.wait_ge(hT_ready, a - 1)
                    dve.scalar_tensor_tensor(act_h[:, a % 2, :], ps[:, 2 + a % 2, DE:2 * DE], r_wa[:, a:a + 1], act_g[:, a % 2, :],
                                             ALU.mult, ALU.mult).then_inc(h_ready, 1)
                elif what == "scatter":
                    j = m[0]
                    t, n = divmod(j, 2)
                    dve.wait_ge(sc_ready, 6 * a + j + 1)
                    cols = slice(512 * n, 512 * n + 512)
                    if a:
                        dve.wait_ge(acc_done, 6 * (a - 1) + j + 1)
                    dve.tensor_tensor(x2[:, t, cols], ps[:, MISC[m[1] % 3], :], x2[:, t, cols], ALU.add).then_inc(acc_done, 1)
            with if_overflow(dve):
                dve.wait_ge(acc_done, 6 * PAIRS)
                with dve.Fori(0, NG * NE) as e:
                    for t in range(T):
                        dve.wait_ge(ov_silu, 3 * e + t + 1)
                        dve.scalar_tensor_tensor(ov_h[:, t, :], ps[:, t, DE:2 * DE], r_over[:, bass.ds(e + 32 * t, 1)], ov_g[:, t, :],
                                                 ALU.mult, ALU.mult).then_inc(ov_hd, 1)
                    dve.wait_ge(ov_acc, 6 * e)
                    for j in range(6):
                        t, n = divmod(j, 2)
                        cols = slice(512 * n, 512 * n + 512)
                        dve.wait_ge(ov_down, 6 * e + j + 1)
                        dve.tensor_tensor(x2[:, t, cols], ps[:, j, :], x2[:, t, cols], ALU.add).then_inc(ov_acc, 1)
            with dve.Else():
                pass

        @block.gpsimd
        def _(pool):
            chain = Chain(pool, pool_step)

            def store(dst, src, s):
                pool.dma_start(dst, src).then_inc(s, 16)

            for kind, *arg in steps:
                i = arg[0] if arg else 0
                if kind == "post":
                    pool.wait_ge(acc_evac, i + 1)
                    if POSTED.get(i, 1) > 1:
                        pool.wait_ge(post_done, POSTED[i] - 1)
                    if i in NORMS:
                        rows_ap, rows, n, g, order = NORMS[i]
                        x = rows_ap.rearrange("p t (h n) -> p (t h) n", n=n)
                        sq = zq[:, 0:rows * n].rearrange("p (r n) -> p r n", n=n)
                        if order:
                            pool.wait_ge(hr_ready, order)
                        pool.tensor_tensor(sq, x, x, ALU.mult).then_inc(sq_ready, 1)
                        pool.wait_ge(hr_ready, order + 1)
                        pool.wait_ge(s_gain, 16)
                        chain(pool.tensor_tensor(x, x, hr[:, 0:rows].unsqueeze(2).to_broadcast([P, rows, n]), ALU.mult))
                        pool.tensor_tensor(x, x, gn(g).unsqueeze(1).to_broadcast([P, rows, n]), ALU.mult).then_inc(post_done, 1)
                        if i == C_MK:
                            pool.wait_ge(post_done, POSTED[i])
                            store(io["mem_k"], mk[:, :, :], s_out)
                        if i == C_FK:
                            pool.wait_ge(post_done, POSTED[i])
                            store(io["fox_k"], fk, s_fk_out)
                    elif i == C_RQK:
                        pool.wait_ge(s_const, 16)
                        rows = rqk.rearrange("p t (h f) -> p t h f", f=64)
                        a, b = rows[:, :, :, 0:32], rows[:, :, :, 32:64]
                        cos = cst("cos").rearrange("p (t f) -> p t f", t=T).unsqueeze(2).to_broadcast([P, T, 8, 32])
                        sin = cst("sin").rearrange("p (t f) -> p t f", t=T).unsqueeze(2).to_broadcast([P, T, 8, 32])
                        ra = zq[:, 0:768].rearrange("p (t h f) -> p t h f", t=T, f=32)
                        rb = zq[:, 768:1536].rearrange("p (t h f) -> p t h f", t=T, f=32)
                        chain(pool.tensor_tensor(ra, a, cos, ALU.mult))
                        chain(pool.tensor_tensor(rb, b, sin, ALU.mult))
                        chain(pool.tensor_tensor(ra, ra, rb, ALU.subtract))
                        chain(pool.tensor_tensor(rb, a, sin, ALU.mult))
                        chain(pool.tensor_tensor(b, b, cos, ALU.mult))
                        chain(pool.tensor_tensor(b, b, rb, ALU.add))
                        pool.tensor_copy(a, ra).then_inc(post_done, 1)
                    elif i == C_RG:
                        rows = rg.rearrange("p t (h v) -> p (t h) v", v=P)
                        pool.tensor_tensor(rows, rows, gn("ret").unsqueeze(1).to_broadcast([P, T * HR, P]), ALU.mult).then_inc(post_done, 1)
                    else:
                        if i == C_MV:
                            store(io["mem_v"], mv[:, :, :], s_out)
                        if i == C_FV:
                            store(io["fox_v"], fv, s_out)
                elif kind == "forget":
                    pool.wait_ge(logf_ready, 1)
                    store(io["logf"], logf, s_out)
                elif kind == "turn" and i == 4:
                    pool.wait_ge(turn_ready, 4)
                    k4 = rqk[:, :, 256:512].rearrange("p t (h f) -> p t h f", f=64)
                    kd = cst("kdec").rearrange("p (t h) -> p t h", t=T).unsqueeze(3).to_broadcast([P, T, HR, 64])
                    chain(pool.tensor_tensor(k4, k4, kd, ALU.mult))
                    for b in range(NB):
                        ins = pool.tensor_tensor(kmask[:, b // 2, :, b % 2, :], rqk[:, 2, 256:512].rearrange("p (h f) -> p h f", f=64),
                                                 cst("inbatch")[:, b:b + 1].unsqueeze(2).to_broadcast([P, HR, 64]), ALU.mult)
                    ins.then_inc(kmask_ready, 1)
                elif kind == "ret_state":
                    pool.wait_ge(st_done, 5)
                    store(io["state_s"], state[:, :, :, :], s_state_out)
                    store(io["state_p"], stp[:, :, :], s_stp_out)
                    pool.wait_ge(s_state_out, 16)
                    pool.wait_ge(s_stp_out, 16)
                    pool.wait_ge(s_out, 16 * 4)
                    pool.wait_ge(even_turned, 10)
                    pool.wait_ge(odd_turned, 10)
                    for b in range(4):
                        store(foxc[b][:, :], io["foxc"][b], foxc_in[b])
                    pool.memset(qb_f[:, :, :], 0.0)
                    pool.memset(qb_m[:, :, :], 0.0).then_inc(work_zero, 1)
                    pool.wait_ge(work_zero, 1)
                elif kind == "unit_s" and i + 1 < NU:
                    what, a, t = units[i + 1]
                    if what == "foxs":
                        if a >= 2:
                            pool.wait_ge(u_s, i)
                        cols = slice(SEQ + a * NI, SEQ + (a + 1) * NI)
                        pool.wait_ge(even_turned, 4)
                        pool.wait_ge(odd_turned, 4)
                        if a:
                            pool.wait_ge(qb_ready, a)
                        for hl in range(2):
                            half = slice(64 * hl, 64 * hl + 64)
                            if hl:
                                chain(ins)
                            ins = pool.tensor_copy(qb_f[half, a % 2, :].rearrange("p (g c) -> p g c", c=160)[:, :, hl * NI:(hl + 1) * NI],
                                                   fqT[half, :, cols])
                        ins.then_inc(qb_ready, 1)
                    elif what == "mems":
                        if a >= 2:
                            pool.wait_ge(u_s, i)
                        pool.wait_ge(qb_ready, NB + a)
                        for b2 in range(2):
                            b = 2 * a + b2
                            if b2:
                                chain(ins)
                            ins = pool.tensor_copy(qb_m[:, b % 4, :].rearrange("p (h c) -> p h c", c=80)[:, :, 0:NI],
                                                   mqT[:, :, SEQ + b * NI:SEQ + (b + 1) * NI])
                        ins.then_inc(qb_ready, 1)
                elif kind == "unit_v" and units[i][0] == "foxs" and units[i][1] + 4 < NB:
                    b = units[i][1] + 4
                    pool.wait_ge(u_v, i + 1)
                    store(foxc[b % 4][:, :], io["foxc"][b], foxc_in[b % 4])
                elif kind == "merge" and i >= C_BR + 2:
                    c = i - C_BR
                    pool.wait_ge(br_mul, c + 1)
                    if c >= 4:
                        pool.wait_ge(br_add, c - 3)
                    pool.tensor_tensor(z[:, GATE_SLOT[c % 2], :, :], z[:, GATE_SLOT[c % 2], :, :], z[:, GATE_SLOT[c], :, :], ALU.add).then_inc(br_add, 1)
            for what, a, *m in moe:
                if what == "back":
                    if a == 0:
                        pool.wait_ge(rows_out, 4)
                        pool.wait_ge(s_const2, 16)
                    else:
                        pool.wait_ge(back_ready, a)
                    if a >= 2:
                        pool.wait_ge(acc_done, 6 * (a - 1))
                    sid = cst2("slot")[:, a:a + 1]
                    chain(pool.tensor_scalar(back[:, a % 2, :], slotrow[:, 0, :], sid, None, ALU.is_equal))
                    chain(pool.tensor_scalar(back_b[:, :], slotrow[:, 1, :], sid, None, ALU.is_equal))
                    pool.tensor_tensor(back[:, a % 2, :], back[:, a % 2, :].bitcast(F32), back_b[:, :], ALU.add).then_inc(back_ready, 1)
            pool.wait_ge(s_out, 16 * 4)
            pool.wait_ge(s_fk_out, 16)

        @block.tensor
        def _(pe):
            mm = nc.tensor.matmul

            def parts(out, xh, xl, wh, wl, start, stop):
                mm(out, xh, wh, start=start, stop=False, skip_group_check=True)
                mm(out, xh, wl, start=False, stop=False, skip_group_check=True)
                return mm(out, xl, wh, start=False, stop=stop, skip_group_check=True)

            for kind, *arg in steps:
                i = arg[0] if arg else 0
                if kind == "k":
                    c = chunk_of[i]
                    what, kt, nt = CHUNKS[c]
                    if i == FIRST[c]:
                        u = last_user(c)
                        if c == C_BR + 5:
                            pe.wait_ge(u_exp, NU)
                            pe.wait_ge(u_Te, NU)
                        elif u is not None and u < C_BR:
                            pe.wait_ge(acc_evac, u + 1)
                        elif u is not None and u < C_OUT:
                            pe.wait_ge(br_mul, u - C_BR + 1)
                        if c == C_BR:
                            pe.wait_ge(ret_te, HR)
                        elif c == C_BR + 2:
                            pe.wait_ge(u_oe, NGROUP - NB // 2)
                        elif c == C_BR + 4:
                            pe.wait_ge(u_oe, NGROUP)
                        if what == "out":
                            pe.wait_ge(mt_evac, 8)
                    if c in (0, C_RQK):
                        pe.wait_ge(act_lo, (KT if c else 0) + 2 * (i - FIRST[c]) + 2)
                    if i < NSPLIT:
                        pe.wait_ge(lo_ready, i + 1)
                    else:
                        pe.wait_ge(raw_in[i % RAW_SLOTS], 16 * (i // RAW_SLOTS + 1))
                    for kk in range(2):
                        k = 2 * (i - FIRST[c]) + kk
                        first, last = k == 0, k == kt - 1
                        cols = slice(512 * kk, 512 * kk + 512)
                        for t in range(nt):
                            tok = slice(t * P, t * P + P)
                            acc = ps[:, bank_of(c, t), :]
                            if i < NSPLIT:
                                xh, xl = (memT_hi, memT_lo) if what == "mem" else (hT_hi, hT_lo)
                                ins = parts(acc, xh[:, k, tok], xl[:, k, tok], w_hi[:, i % PART_SLOTS, cols], w_lo[:, i % PART_SLOTS, cols], first, last)
                            else:
                                x = oT[:, 4 * ((c - C_BR) // 2) + k, tok] if what == "br" else mT[:, k, tok]
                                ins = mm(acc, x, raw[:, i % RAW_SLOTS, cols], start=first, stop=last, skip_group_check=True)
                    ins.then_inc(gran_used, 1)
                elif kind == "forget":
                    pe.wait_ge(act_lo, 2 * KT + 1)
                    for t in range(T):
                        for k in range(KT):
                            tok = slice(t * P, t * P + P)
                            ins = parts(ps[:, 6, 8 * t:8 * t + 8], hT_hi[:, k, tok], hT_lo[:, k, tok], ffw_hi[:, 8 * k:8 * k + 8], ffw_lo[:, 8 * k:8 * k + 8],
                                        k == 0, k == KT - 1)
                    ins.then_inc(ff_ready, 1)
                elif kind == "turn":
                    name, j = turns[i]
                    if i == 0:
                        pe.wait_ge(s_const, 16)
                        pe.wait_ge(acc_evac, C_GATE)
                        pe.wait_ge(zneg_ready, 1)
                    pe.wait_ge(post_done, POSTED[{"rqk": C_RQK, "fq": C_FQ, "fk": C_FK, "mq": C_MQ, "mk": C_MK}[name]])
                    if i >= 5:
                        turn_wait(pe, i - 5)
                    rows = {"rqk": rqk, "fq": fq, "fk": fk, "mq": mq, "mk": mk[:, :, :]}[name]
                    for t in range(2 if name == "mk" else T):
                        ins = nc.tensor.transpose(ps[:, 3 + i % 5, t * P:(t + 1) * P], rows[:, t, j * P:(j + 1) * P], ident)
                    ins.then_inc(turn_ready, 1)
                elif kind == "decay_sums":
                    for j in range(15, 20):
                        turn_wait(pe, j)
                    pe.wait_ge(logf_ready, 1)
                    pe.wait_ge(s_logc, 16)
                    up1 = const[:, CONST["upper"][0]:CONST["upper"][0] + 256]
                    lf = [logf[:, 8 * t:8 * t + 8] for t in range(T)]
                    kw = dict(skip_group_check=True)
                    mm(ps[0:8, 3, 0:256], lf[0], up1, start=True, stop=False, **kw)
                    mm(ps[0:8, 3, 128:256], lf[1], cst("upper"), start=False, stop=True, **kw)
                    for b in range(NB):
                        win = cst("batchwin")[:, (NB - 1 - b) * NI:(NB - 1 - b) * NI + P]
                        mm(ps[0:8, 3, 256:384], logc[:, 8 * b:8 * b + 8], win, start=b == 0, stop=False, **kw)
                    mm(ps[0:8, 3, 256:384], lf[2], cst("upper_in_batch"), start=False, stop=True, **kw)
                    for b in range(NB):
                        mm(ps[0:8, 4 + b // 4, (b % 4) * P:(b % 4) * P + P], logc[:, 8 * b:8 * b + 8], cst("upper"), start=True, stop=True, **kw)
                    mm(ps[:, 6, 0:8], cst("upper"), lf[0], start=True, stop=True, **kw)
                    mm(ps[:, 6, 8:16], cst("ones"), lf[0], start=True, stop=False, **kw)
                    mm(ps[:, 6, 8:16], cst("upper"), lf[1], start=False, stop=True, **kw).then_inc(sums_ready, 1)
                elif kind == "decay_query":
                    pe.wait_ge(sums_evac, 1)
                    sel = cst("headsel")[0:8, :]
                    mm(ps[:, 5, 0:P], sel, nf_n[:, :], start=True, stop=True).then_inc(fqs_psum, 1)
                elif kind == "ret_s":
                    h, b = i, 3 + i % 2
                    pe.wait_ge(sums_evac, 1)
                    if h >= 2:
                        pe.wait_ge(ret_m, h - 1)
                    half = slice(64 * (h % 2), 64 * (h % 2) + 64)
                    q, k = rqkT[half, h // 2, :], rqkT[half, 2 + h // 2, :]
                    mm(ps[:, b, 0:256], k[:, 0:P], q[:, 0:256], start=True, stop=True, skip_group_check=True)
                    mm(ps[:, b, 256:384], k[:, P:256], q[:, P:256], start=True, stop=True, skip_group_check=True)
                    mm(ps[:, b, 384:512], k[:, SEQ:TOK], q[:, SEQ:TOK], start=True, stop=True, skip_group_check=True).then_inc(ret_s, 1)
                elif kind == "ret_o":
                    h = i
                    pe.wait_ge(ret_m, h + 1)
                    pe.wait_ge(ret_q, h + 1)
                    pe.wait_ge(s_state, 16)
                    if h:
                        pe.wait_ge(ret_rows, h)
                    s, v = sT[:, h % 2, :], rv[:, :, h * P:(h + 1) * P]
                    kw = dict(skip_group_check=True)
                    mm(ps[:, 6, 0:P], s[:, 0:P], v[:, 0, :], start=True, stop=True, **kw)
                    mm(ps[:, 6, P:2 * P], s[:, P:2 * P], v[:, 0, :], start=True, stop=False, **kw)
                    mm(ps[:, 6, P:2 * P], s[:, 2 * P:3 * P], v[:, 1, :], start=False, stop=True, **kw)
                    mm(ps[:, 6, 2 * P:3 * P], s[:, 3 * P:4 * P], v[:, 2, :], start=True, stop=False, **kw)
                    for bp in range(4):
                        ins = mm(ps[:, 6, 2 * P:3 * P], qmask[:, h % 2, bp, :], state[:, bp, h, :], start=False, stop=bp == 3, **kw)
                    ins.then_inc(ret_o, 1)
                elif kind == "ret_t":
                    pe.wait_ge(ret_rows, i + 1)
                    if i:
                        pe.wait_ge(ret_te, i)
                    for t in range(T):
                        ins = nc.tensor.transpose(ps[:, 7, t * P:(t + 1) * P], orow[:, t * P:(t + 1) * P], ident)
                    ins.then_inc(ret_t, 1)
                elif kind == "ret_state":
                    pe.wait_ge(kmask_ready, 1)
                    pe.wait_ge(fqs_ready, 1)
                    pe.wait_ge(ret_te, HR)
                    pe.wait_ge(ret_m, HR)
                    for h in range(HR):
                        for bp in range(4):
                            ins = mm(ps[:, 3 + h, bp * P:(bp + 1) * P], kmask[:, bp, h, :, :].rearrange("p a f -> p (a f)"), rv[:, 2, h * P:(h + 1) * P],
                                     start=True, stop=True, skip_group_check=True)
                        ins.then_inc(st_ready, 1)
                    for h in range(HR):
                        half = slice(64 * (h % 2), 64 * (h % 2) + 64)
                        for t in range(2):
                            ins = mm(ps[half, 7, (h // 2) * P:(h // 2) * P + P], rqk[:, t, 256 + h * 64:256 + h * 64 + 64], rv[:, t, h * P:(h + 1) * P],
                                     start=t == 0, stop=t == 1, skip_group_check=True)
                    ins.then_inc(st_ready, 1)
                elif kind == "unit_s":
                    what, a, t = units[i]
                    bank = ps[:, 3 + i % 2, :]
                    kw = dict(skip_group_check=True)
                    if i == 0:
                        pe.wait_ge(st_done, 5)
                    if i >= 2:
                        pe.wait_ge(u_exp, i - 1)
                    if what == "foxp":
                        n, half = keys(i), slice(64 * (a % 2), 64 * (a % 2) + 64)
                        mm(bank[:, 0:n], fqT[half, a // 2, t * P:(t + 1) * P], fkT[half, a // 2, 0:n], start=True, stop=False, **kw)
                        ins = mm(bank[:, 0:n], ident[0:8, a:a + 1].to_broadcast([8, P]), nf_p[:, 0:n], start=False, stop=True, **kw)
                    elif what == "memp":
                        ins = mm(bank[:, 0:256], mqT[:, a, t * P:(t + 1) * P], mkT[:, a, :], start=True, stop=True, **kw)
                    elif what == "foxs":
                        pe.wait_ge(qb_ready, a + 1)
                        pe.wait_ge(foxc_in[a % 4], 16 * (a // 4 + 1))
                        sel = cst("headsel")[0:8, :]
                        for hp in range(4):
                            mm(bank[:, 0:P], qb_f[:, a % 2, hp * P:(hp + 1) * P], foxc[a % 4][:, hp * P:(hp + 1) * P], start=hp == 0, stop=False, **kw)
                        mm(bank[:, 0:P], sel, nf_c[:, a, :], start=False, stop=True, **kw)
                        for hp in range(4):
                            mm(bank[:, P:256], qb_f[:, a % 2, hp * P:(hp + 1) * P], fkT[:, hp, SEQ:TOK], start=hp == 0, stop=False, **kw)
                        ins = mm(bank[:, P:256], sel, nf_n[:, :], start=False, stop=True, **kw)
                    else:
                        pe.wait_ge(qb_ready, NB + a + 1)
                        for b2 in range(2):
                            b = 2 * a + b2
                            pe.wait_ge(memk_in[b % 4], 16 * (b // 4 + 1))
                            for h in range(HM):
                                ins = mm(ps[64 * b2:64 * b2 + 64, 3 + i % 2, 0:256], qb_m[:, b % 4, 64 * h:64 * h + 64], memk[b % 4][:, 256 * h:256 * h + 256],
                                         start=h == 0, stop=h == 3, **kw)
                    ins.then_inc(u_s, 1)
                elif kind == "unit_p":
                    pe.wait_ge(u_p, i + 1)
                    if i:
                        pe.wait_ge(u_Te, i)
                    for k in range(keys(i) // P):
                        ins = nc.tensor.transpose(ps[:, 5, k * P:(k + 1) * P], p_sb[:, i % 2, k * P:(k + 1) * P], ident)
                    ins.then_inc(u_T, 1)
                elif kind == "unit_v":
                    what, a, t = units[i]
                    nk = keys(i) // P
                    g = group_of(i)
                    bank = ps[:, 6 + g % 2, :]
                    pr = pT[:, i % 2, :]
                    kw = dict(skip_group_check=True)
                    pe.wait_ge(u_Te, i + 1)
                    if g >= 2:
                        pe.wait_ge(u_oe, g - 1)
                    if what == "foxp":
                        for k in range(nk):
                            ins = mm(ps[64 * (a % 2):64 * (a % 2) + 64, 6 + g % 2, 0:P], fv[:, k, 64 * a:64 * a + 64], pr[:, k * P:(k + 1) * P],
                                     start=k == 0, stop=k == nk - 1, **kw)
                    elif what == "memp":
                        for k in range(nk):
                            ins = mm(bank[:, 0:P], mv[:, k, a * P:(a + 1) * P], pr[:, k * P:(k + 1) * P], start=k == 0, stop=k == 1, **kw)
                    elif what == "foxs":
                        for hp in range(4):
                            cols = slice(32 * hp, 32 * hp + 32)
                            mm(bank[:, cols], foxc[a % 4][:, 512 + hp * P:512 + (hp + 1) * P], pr[:, cols], start=True, stop=False, **kw)
                            ins = mm(bank[:, cols], fv[:, 2, hp * P:(hp + 1) * P], pr[:, P + 32 * hp:P + 32 * hp + 32], start=False, stop=True, **kw)
                    else:
                        for b2 in range(2):
                            b = 2 * a + b2
                            pe.wait_ge(memv_in[b % 4], 16 * (b // 4 + 1))
                            for h in range(HM):
                                c0 = 64 * b2 + NI * h
                                for k in range(2):
                                    v0 = 512 * k + P * h
                                    ins = mm(bank[:, c0:c0 + NI], memv[b % 4][:, v0:v0 + P], pr[:, k * P + c0:k * P + c0 + NI],
                                             start=k == 0, stop=k == 1, **kw)
                    ins.then_inc(u_v, 1)
                elif kind == "turn_merged":
                    for j in range(8):
                        pe.wait_ge(br_add, 3 + j // 4)
                        if j >= 2:
                            pe.wait_ge(mt_evac, j - 1)
                        for t in range(T):
                            ins = nc.tensor.transpose(ps[:, 6 + j % 2, t * P:(t + 1) * P], z[:, GATE_SLOT[j // 4], t, (j % 4) * P:(j % 4 + 1) * P], ident)
                        ins.then_inc(mt_ready, 1)
                elif kind == "turn_x2":
                    pe.wait_ge(x2_ready, 2)
                    for j in range(8):
                        if j >= 2:
                            pe.wait_ge(x2t_evac, j - 1)
                        for t in range(T):
                            ins = nc.tensor.transpose(ps[:, 6 + j % 2, t * P:(t + 1) * P], x2[:, t, j * P:(j + 1) * P], ident)
                        ins.then_inc(x2t_ready, 1)
                elif kind == "route":
                    pe.wait_ge(x2t_evac, 8)
                    pe.wait_ge(s_wr, 16)
                    for t in range(T):
                        for k in range(KT):
                            ins = mm(ps[:, 7, 64 * t:64 * t + 36], h2T[:, k, t * P:(t + 1) * P], wr[:, k, :], start=k == 0, stop=k == KT - 1, skip_group_check=True)
                    ins.then_inc(lg_ready, 1)
            kw = dict(skip_group_check=True)

            def misc_free(m):
                if m >= 3:
                    old, q, j = misc_steps[m - 3]
                    if old == "gather":
                        pe.wait_ge(xs_ready, 8 * q + j + 1)
                    else:
                        pe.wait_ge(acc_done, 6 * q + j + 1)

            for what, a, *m in moe:
                if what == "rank":
                    pe.wait_ge(taken_ready, 1)
                    pe.wait_ge(s_const2, 16)
                    for t in range(T):
                        for u in range(t + 1):
                            mm(ps[:, 6, 32 * t:32 * t + 32], cst2("before") if u == t else cst("ones"), r_m[:, 32 * u:32 * u + 32], start=u == 0, stop=u == t, **kw)
                    for u in range(T):
                        ins = mm(ps[0:1, 6, 96:128], cst("ones")[:, 0:1], r_m[:, 32 * u:32 * u + 32], start=u == 0, stop=u == 2, **kw)
                    ins.then_inc(rank_ready, 1)
                elif what == "rows_out":
                    pe.wait_ge(slots_ready, 1)
                    for j, col in enumerate((r_s1, r_s2, r_w1, r_w2)):
                        for t in range(T):
                            ins = nc.tensor.transpose(ps[:, j, t * P:(t + 1) * P], col[:, t:t + 1].to_broadcast([P, P]), ident)
                    ins.then_inc(rows_ready, 1)
                elif what == "gather":
                    k, mi = m
                    if k == 0:
                        pe.wait_ge(pick_ready, 3 * (a + 1))
                    if a == 0 and k == 0:
                        pe.wait_ge(rows_out, 4)
                        pe.wait_ge(xparts_ready, T)
                    misc_free(mi)
                    bank = ps[:, MISC[mi % 3], 0:256]
                    for t in range(T):
                        for x in (x_hi, x_lo):
                            ins = mm(bank, x[:, t, k * P:(k + 1) * P], pick[:, a % 2, t, :], start=t == 0 and x is x_hi, stop=t == 2 and x is x_lo, **kw)
                    ins.then_inc(xg_ready, 1)
                elif what == "gu":
                    pe.wait_ge(xs_ready, 8 * (a // 2 + 1))
                    if a >= 2:
                        pe.wait_ge(h_ready, a - 1)
                    for k in range(KT):
                        for e2 in range(2):
                            e = 2 * a + e2
                            if k == 0:
                                pe.wait_ge(wgu_in[e % 4], 16 * (e // 4 + 1))
                            c0 = CAP * (e % 4)
                            ins = mm(ps[64 * e2:64 * e2 + 64, 2 + a % 2, :], xs[:, (a // 2) % 2, k, c0:c0 + CAP], wgu[e % 4][:, 512 * k:512 * k + 512],
                                     start=k == 0, stop=k == KT - 1, **kw)
                    ins.then_inc(gu_ready, 1)
                elif what == "hT_out":
                    pe.wait_ge(h_ready, a + 1)
                    if a:
                        pe.wait_ge(hT_evac, a)
                    for f in range(2):
                        ins = nc.tensor.transpose(ps[:, 4, f * P:(f + 1) * P], act_h[:, a % 2, f * P:(f + 1) * P], ident)
                    ins.then_inc(hT_ready, 1)
                elif what == "down":
                    pe.wait_ge(hT_evac, a + 1)
                    if a:
                        pe.wait_ge(ylo_ready, 2 * a)
                    for n in range(2):
                        for f in range(2):
                            for e2 in range(2):
                                e = 2 * a + e2
                                if n == 0 and f == 0:
                                    pe.wait_ge(wdn_in[e % 4], 16 * (e // 4 + 1))
                                o = D * f + 512 * n
                                ins = mm(ps[64 * e2:64 * e2 + 64, 5 + n, :], act_T[:, a % 2, f * P + 64 * e2:f * P + 64 * e2 + 64], wdn[e % 4][:, o:o + 512],
                                         start=f == 0, stop=f == 1, **kw)
                    ins.then_inc(dn_ready, 1)
                elif what == "scatter":
                    j, mi = m
                    t, n = divmod(j, 2)
                    if j == 0:
                        pe.wait_ge(ylo_ready, 2 * a + 2)
                        pe.wait_ge(back_ready, a + 1)
                    misc_free(mi)
                    for y in (y_hi, y_lo):
                        ins = mm(ps[:, MISC[mi % 3], :], back[:, a % 2, t * P:(t + 1) * P], y[:, a % 2, 512 * n:512 * n + 512], start=y is y_hi, stop=y is y_lo, **kw)
                    ins.then_inc(sc_ready, 1)
            with if_overflow(pe):
                pe.wait_ge(acc_done, 6 * PAIRS)
                for k in range(KT):
                    for t in range(T):
                        for x in (x_hi, x_lo):
                            ins = mm(ps[:, k, t * P:(t + 1) * P], x[:, t, k * P:(k + 1) * P].bitcast(F32), ident, start=x is x_hi, stop=x is x_lo, **kw)
                    ins.then_inc(ov_x, 1)
                pe.wait_ge(ov_xT, KT)
                with pe.Fori(0, NG * NE // 2) as i:
                    for b in range(2):
                        pe.wait_ge(ov_w[b], 16 * i + 16)
                        pe.wait_ge(ov_acc, 12 * i + 6 * b)
                        for t in range(T):
                            for k in range(KT):
                                ins = mm(ps[:, t, :], ov_h2T[:, k, t * P:(t + 1) * P], wgu_o[b][:, 512 * k:512 * k + 512], start=k == 0, stop=k == KT - 1, **kw)
                            ins.then_inc(ov_gu, 1)
                        for t in range(T):
                            pe.wait_ge(ov_hd, 6 * i + 3 * b + t + 1)
                            for f in range(2):
                                ins = nc.tensor.transpose(ps[:, 3 + t, f * P:(f + 1) * P], ov_h[:, t, f * P:(f + 1) * P], ident)
                            ins.then_inc(ov_tr, 1)
                        pe.wait_ge(ov_hTe, 6 * i + 3 * b + 3)
                        for j in range(6):
                            t, n = divmod(j, 2)
                            for f in range(2):
                                o = 4096 + D * f + 512 * n
                                ins = mm(ps[:, j, :], ov_hT[:, t, f * P:(f + 1) * P], wgu_o[b][:, o:o + 512], start=f == 0, stop=f == 1, **kw)
                            ins.then_inc(ov_down, 1)
            with pe.Else():
                pass


def constants():
    a = np.zeros((P, N_CONST), np.float64)
    p = np.arange(P)

    def put(name, x):
        o, n = CONST[name]
        a[:, o:o + n] = x.reshape(P, n)

    i16, b16 = p % NI, p // NI
    put("ident", np.eye(P))
    put("upper", (p[None, :] >= p[:, None]).astype(float))
    put("ones", np.ones((P, P)))
    win = np.zeros((P, 240))
    win[:, 112:128] = 1.0
    put("batchwin", win)
    win = np.full((P, 240), -BIG)
    win[:, 112:128] = np.where(np.arange(NI)[None, :] <= i16[:, None], 0.0, -BIG)
    put("maskwin", win)
    put("upper_in_batch", ((p[None, :] >= p[:, None]) & (b16[None, :] == b16[:, None])).astype(float))
    zc = np.zeros((P, 256))
    zc[:, 128:] = np.where(p[None, :] <= p[:, None], 0.0, -BIG)
    put("zeros_causal", zc)
    pos = np.concatenate([np.arange(SEQ), PAST + i16]).astype(np.float32)
    inv = (np.float32(10000.0) ** (-np.arange(32, dtype=np.float32) / np.float32(32))).astype(np.float32)
    ang = (pos[:, None] * inv[None, :]).astype(np.float32).astype(np.float64).reshape(T, P, 32).transpose(1, 0, 2)
    put("cos", np.cos(ang))
    put("sin", np.sin(ang))
    lg = np.log1p(-2.0 ** (-5.0 - np.arange(HR)))
    scale = 64 ** -0.5
    diff = p[None, :] - p[:, None]
    dec = np.where((diff >= 0)[:, None, :] & (b16[:, None] == b16[None, :])[:, None, :], np.exp(diff[:, None, :] * lg[None, :, None]), 0.0) * scale
    put("decay_s", dec)
    kd = np.concatenate([SEQ - 1 - np.arange(SEQ), NI - 1 - i16]).reshape(T, P).T
    put("kdec", np.exp(kd[:, :, None] * lg[None, None, :]) * scale)
    put("inbatch", (b16[:, None] == np.arange(NB)[None, :]).astype(float))
    put("headsel", (b16[None, :] == p[:, None]).astype(float))
    put("pick", (i16[:, None] == np.arange(NI)[None, :]).astype(float))
    put("rev4", np.tile(4.0 - np.arange(4), (P, T)))
    put("rev8", np.tile(8.0 - np.arange(8), (P, T)))
    i = np.arange(256)
    d2 = i[None, :] - p[:, None]
    dtab = np.where((d2 >= 0)[:, None, :], np.exp(np.maximum(d2, 0)[:, None, :] * lg[None, :, None]), 0.0) * scale
    qt = np.exp((i16[None, :] + 1.0) * lg[:, None])
    own = (2 * np.arange(4)[None, :, None] + (p // 64)[:, None, None]) == b16[None, None, :]
    qtab = qt[None, :, None, :] * own[:, None, :, :]
    c2 = np.zeros((P, N_CONST2))
    e = np.arange(32)
    for name, x in (("before", (p[None, :] > p[:, None]).astype(float)), ("iota", np.tile(np.arange(256), (P, 1))),
                    ("slot", P * np.arange(PAIRS)[None, :] + p[:, None]), ("first_slot", np.tile(CAP * e, (P, T))),
                    ("quad_slot", np.tile(np.repeat(4 * CAP * np.arange(QUADS), T), (P, 1)))):
        o, n = CONST2[name]
        c2[:, o:o + n] = x
    f = np.float32
    return c2.astype(f), a.astype(f), dtab.astype(f), qtab.astype(f)


OUTS = [("y", (P, T, D)), ("fox_k", (P, T, 512)), ("fox_v", (P, T, 512)), ("logf", (P, T * 8)), ("mem_k", (P, 2, 512)), ("mem_v", (P, 2, 512)),
        ("state_s", (P, 4, HR, P)), ("state_p", (P, 2, P))]


def kernel(**inputs):
    from concourse import bacc
    from concourse.bass_utils import run_bass_kernel_spmd

    g = {k: np.ascontiguousarray(v) for k, v in inputs.items()}
    c = np.ascontiguousarray
    x = np.concatenate([g["x_prompt"].reshape(SEQ, D), g["x_sample"].reshape(P, D)])
    mem = g["mem_prompt"].reshape(NMEM, D)

    def by_token(a, t):
        return c(a.reshape(t, P, -1).transpose(1, 0, 2))

    def turned(a):
        return c(a.reshape(-1, KT, P).transpose(2, 1, 0))

    def granules(w):
        k, n = w.shape
        return w.reshape(k // 256, 2, P, n // 512, 512).transpose(3, 0, 2, 1, 4).reshape(-1, P, GRAN)

    w = g["w_in"][0]
    sizes = [256, 256, 512, 512, 512, 512, 512, 8, 512, 3072]
    cut = np.cumsum([0] + sizes)
    parts = [w[:, cut[i]:cut[i + 1]] for i in range(10)]
    wff = parts[7]
    win = np.concatenate(parts[:7] + parts[8:], axis=1)
    stream = [granules(g["w_mem_kv"][0]), granules(win), granules(g["w_br_ret"][0]), granules(g["w_br_fox"][0]), granules(g["w_br_mem"][0]),
              granules(g["w_out"][0])]
    const2, const, dtab, qtab = constants()
    gk = np.concatenate([g[n].reshape(KT, P).T for n in ("g_norm1", "g_mem_in", "g_norm2")], axis=1)
    gain = np.concatenate([g["g_fox_q"][0], g["g_fox_k"][0], g["g_mem_q"][0], g["g_mem_k"][0], g["g_ret_out"][0], g["b_forget"][0],
                           g["b_route_group"][0], g["b_route_expert"][0]])
    fk = g["cache_fox_k"][0].transpose(0, 2, 3, 1).reshape(NB, 4, P, P).transpose(0, 2, 1, 3).reshape(NB, P, 512)
    foxc = np.concatenate([fk, g["cache_fox_v"][0].reshape(NB, P, 512)], axis=2)
    mkc = g["cache_mem_k"][0].transpose(0, 3, 2, 1).reshape(NB, P, 1024)
    mvc = g["cache_mem_v"][0].reshape(NB, 2, P, 512).transpose(0, 2, 1, 3).reshape(NB, P, 1024)
    gu = np.concatenate([g["w_exp_gate"].reshape(32, KT, P, DE), g["w_exp_up"].reshape(32, KT, P, DE)], axis=3).transpose(0, 2, 1, 3).reshape(32, P, 4096)
    dn = g["w_exp_down"].reshape(32, 2, P, D).transpose(0, 2, 1, 3).reshape(32, P, 2048)
    arrays = {
        "xT": turned(x), "xtok": by_token(x, T), "memT": turned(mem), "memtok": by_token(mem, 2), "gk": c(gk), "gain": c(np.tile(gain, (P, 1))),
        "const": const, "const2": const2, "dtab": dtab, "qtab": qtab, "ffw": c(wff.reshape(KT, P, 8).transpose(1, 0, 2).reshape(P, 64)),
        "logc": c(g["cache_fox_logf"][0].transpose(1, 0, 2).reshape(P, 64)), "wstream": c(np.concatenate(stream)),
        "state": c(g["state_ret"][0].reshape(4, 2, HR, 64, P).transpose(1, 3, 0, 2, 4).reshape(P, 4, HR, P)),
        "foxc": c(foxc), "memc": c(np.concatenate([mkc, mvc], axis=2)),
        "wr": c(np.concatenate([g["w_route_group"][0], g["w_route_expert"][0]], axis=1).reshape(KT, P, 36).transpose(1, 0, 2)),
        "wexp": c(np.concatenate([gu, dn], axis=2)),
    }
    nc = bacc.Bacc("TRN2", target_bir_lowering=False, num_devices=1)
    io = {k: nc.dram_tensor(f"in_{k}", v.shape, mybir.dt.from_np(v.dtype), kind="ExternalInput").ap() for k, v in arrays.items()}
    io.update({k: nc.dram_tensor(f"out_{k}", s, F32, kind="ExternalOutput").ap() for k, s in OUTS})
    program(nc, io)
    r = run_bass_kernel_spmd(nc, [{f"in_{k}": v for k, v in arrays.items()}], core_ids=[0]).results[0]
    o = {k: np.asarray(r[f"out_{k}"]).reshape(s) for k, s in OUTS}

    def rows(a):
        return a.transpose(1, 0, 2).reshape(a.shape[0] * a.shape[1], -1)

    y, fk, fv = rows(o["y"]), rows(o["fox_k"]), rows(o["fox_v"])
    lf = rows(o["logf"].reshape(P, T, 8))
    mk, mv = rows(o["mem_k"]), rows(o["mem_v"])
    st_s = o["state_s"].reshape(2, 64, 4, HR, P).transpose(2, 0, 3, 1, 4).reshape(1, NB, HR, 64, P)
    st_p = o["state_p"].reshape(2, 64, 2, P).transpose(2, 0, 1, 3).reshape(1, 1, HR, 64, P)
    return (y[:SEQ].reshape(1, SEQ, D), y[SEQ:].reshape(NB, NI, D), st_p, fk[:SEQ].reshape(1, 1, SEQ, HF, 64), fv[:SEQ].reshape(1, 1, SEQ, HF, 64),
            lf[:SEQ].reshape(1, 1, SEQ, HF), mk.reshape(1, 1, NMEM, HM, P), mv.reshape(1, 1, NMEM, HM, P), st_s,
            fk[SEQ:].reshape(1, NB, NI, HF, 64), fv[SEQ:].reshape(1, NB, NI, HF, 64), lf[SEQ:].reshape(1, NB, NI, HF))
```

```python
from contextlib import ExitStack

import numpy as np

import concourse.bass as bass
from concourse import mybir

ALU = mybir.AluOpType
ACT = mybir.ActivationFunctionType
F32 = mybir.dt.float32
F32R = mybir.dt.float32r
AX = mybir.AxisListType.X

P = 128
D = 1024
KT = D // P
T = 3
TOK = T * P
SEQ, NB, NI, PAST, NMEM = 256, 8, 16, 128, 256
HR, HF, HM = 4, 8, 4
NG, NE, DE = 4, 8, 256
EPS = 1e-6
BIG = 1e30
GRAN = 2 * 512

CHUNKS = ([("mem", 8, 2)] * 2 + [("in", 8, 3)] * 7 + [("gate", 8, 3)] * 6 + [("br", 4, 3)] * 6 + [("out", 8, 3)] * 2)
C_MK, C_MV, C_RQK, C_RV, C_RG, C_FQ, C_FK, C_MQ, C_FV = range(9)
C_GATE, C_BR, C_OUT = 9, 15, 21
FIRST = [sum(c[1] // 2 for c in CHUNKS[:i]) for i in range(len(CHUNKS) + 1)]
NGRAN = FIRST[-1]
RAW_SLOTS, PART_SLOTS = 4, 3

CONST = {}
_at = 0
for _name, _n in (("ident", P), ("upper", P), ("ones", P), ("batchwin", 240), ("maskwin", 240), ("upper_in_batch", P),
                  ("zeros_causal", 256), ("cos", T * 32), ("sin", T * 32), ("decay_s", HR * P), ("kdec", T * HR),
                  ("inbatch", NB), ("headsel", P), ("pick", NI), ("rev4", T * 4), ("rev8", T * 8)):
    CONST[_name] = (_at, _n)
    _at += _n
N_CONST = _at
CONST2 = {}
_at = 0
for _name, _n in (("before", P), ("iota", 256), ("slot", 16), ("first_slot", T * 32), ("quad_slot", 8 * T)):
    CONST2[_name] = (_at, _n)
    _at += _n
N_CONST2 = _at
CAP = P // 2
PAIRS = NG * NE // 2
QUADS = NG * NE // 4
GAIN = {}
_at = 0
for _name, _n in (("fox_q", 64), ("fox_k", 64), ("mem_q", 128), ("mem_k", 128), ("ret", 128), ("forget", 8), ("route", 36)):
    GAIN[_name] = (_at, _n)
    _at += _n
N_GAIN = _at


def schedule():
    s = []
    ahead = 2
    for g in range(ahead + 1):
        s += [("prep_mem", 2 * g), ("prep_mem", 2 * g + 1), ("split", g)]
    s += [("prep_mem", 6), ("prep_mem", 7)]
    split = ahead + 1
    prep = {1: [("prep_x", k) for k in range(3)], 2: [("prep_x", k) for k in range(3, 6)], 3: [("prep_x", 6), ("prep_x", 7), ("prep_ff",)], 9: [("norm1",)]}

    def granule(g):
        nonlocal split
        while split < min(g + 1 + ahead, NGRAN):
            s.append(("split", split))
            split += 1
        s.append(("k", g))
        s.extend(prep.get(g, []))

    for c in range(C_GATE):
        for g in range(FIRST[c], FIRST[c + 1]):
            granule(g)
            if g == FIRST[C_RQK] + 2:
                s += [("evac", C_MK), ("post", C_MK), ("evac", C_MV), ("post", C_MV)]
            elif g == FIRST[c] and c > C_RQK:
                s += [("evac", c - 1), ("post", c - 1)]
    s.append(("forget",))
    s.append(("evac", C_GATE - 1))
    s.append(("post", C_GATE - 1))
    units = [("foxp", hp * 2 + hl, t) for t in range(2) for hp in range(4) for hl in range(2)]
    units += [("memp", h, t) for h in range(HM) for t in range(2)] + [("foxs", b, 0) for b in range(NB)]
    early = len(units)
    units += [("mems", bp, 0) for bp in range(NB // 2)]
    pieces = [("turn", i) for i in range(20)] + [("decay_sums",)]
    pieces += [("ret_s", 0), ("ret_s", 1), ("decay_query",), ("ret_o", 0), ("ret_s", 2), ("ret_o", 1), ("ret_t", 0),
               ("ret_s", 3), ("ret_o", 2), ("ret_t", 1), ("ret_o", 3), ("ret_t", 2), ("ret_t", 3), ("ret_state",)]
    tail = []
    for i in range(len(units) + 2):
        into = pieces if i < early else tail
        if 1 <= i <= len(units):
            into.append(("unit_w", i - 1))
        if i < len(units):
            into.append(("unit_s", i))
        into += [("unit_v", j) for j in (i - 3, i - 2) if 0 <= j and j + (3 if units[j][0] in ("foxp", "memp") else 2) == i]
        if 1 <= i <= len(units):
            into.append(("unit_p", i - 1))
    weight = {"turn": 0.3, "decay_sums": 3, "ret_s": 3, "ret_o": 6, "ret_t": 2, "ret_state": 0,
              "unit_w": 0, "unit_s": 3, "unit_v": 0, "unit_p": 0}
    total = sum(weight.get(piece[0], 1) for piece in pieces)
    gates = range(FIRST[C_GATE], FIRST[C_BR])
    placed = passed = 0
    for piece in pieces:
        s.append(piece)
        passed += weight.get(piece[0], 1)
        while placed < len(gates) and (placed + 0.5) * total <= passed * len(gates):
            granule(gates[placed])
            placed += 1
            if placed % 4 == 0:
                s.append(("evac", C_GATE + placed // 4 - 1))
    assert placed == len(gates)
    s.append(("parts", 0))
    granule(FIRST[C_BR])
    granule(FIRST[C_BR] + 1)
    s += [("mem_caches",), ("gates",), ("merge", C_BR)]
    ret_fox = range(FIRST[C_BR] + 2, FIRST[C_BR + 4] - 2)
    placed = 0
    for i, piece in enumerate(tail):
        s.append(piece)
        while placed < len(ret_fox) and placed * len(tail) < (i + 1) * len(ret_fox):
            g = ret_fox[placed]
            if g == FIRST[C_BR + 2]:
                assert ("unit_v", early - 1) in s
                s.append(("parts", 1))
            granule(g)
            if g + 1 in FIRST:
                s.append(("merge", FIRST.index(g + 1) - 1))
            placed += 1
    s += [("attention_done",), ("parts", 2)]
    c = C_BR + 4
    granule(FIRST[c] - 2)
    granule(FIRST[c] - 1)
    s.append(("merge", c - 1))
    granule(FIRST[c])
    granule(FIRST[c] + 1)
    s.append(("merge", c))
    granule(FIRST[c + 1])
    s.append(("turn_merged", 0))
    granule(FIRST[c + 1] + 1)
    s.append(("merge", c + 1))
    a, b = FIRST[C_OUT], FIRST[C_OUT + 1]
    granule(a)
    granule(a + 1)
    s.append(("turn_merged", 1))
    granule(a + 2)
    granule(a + 3)
    s.append(("residual", 0))
    granule(b)
    s.append(("squares2", 0))
    granule(b + 1)
    s.append(("turn_x2", 0))
    granule(b + 2)
    s.append(("logits", 0))
    granule(b + 3)
    s += [("residual", 1), ("squares2", 1), ("turn_x2", 1), ("norm2",), ("logits", 1), ("x_parts",), ("route",)]
    return s, units


MISC = (0, 1, 7)


def moe_schedule():
    s, misc = [], []

    def step(what, a, j):
        s.append((what, a, j, len(misc)))
        misc.append((what, a, j))

    s += [("rank", 0), ("rows_out", 0), ("pick", 0)]
    for k in range(KT):
        step("gather", 0, k)
    for p in range(PAIRS):
        q = p // 2 + 1
        s.append(("slot_weight", p))
        if p % 2 == 0 and q < QUADS:
            s.append(("pick", q))
        s.append(("gu", p))
        if p:
            s += [("y_out", p - 1), ("back", p - 1)]
        s += [("silu", p), ("h", p)]
        gathers = [("gather", q, k) for k in range(4 * (p % 2), 4 * (p % 2) + 4)] if q < QUADS else []
        scatters = [("scatter", p - 1, j) for j in range(6)] if p else []
        for i in range(4):
            for what in gathers[i:i + 1] + scatters[i:i + 1]:
                step(*what)
        s.append(("hT_out", p))
        for what in scatters[4:]:
            step(*what)
        s.append(("down", p))
    s += [("y_out", PAIRS - 1), ("back", PAIRS - 1)]
    for j in range(6):
        step("scatter", PAIRS - 1, j)
    return s, misc


def program(nc, io):
    steps, units = schedule()
    moe, misc_steps = moe_schedule()
    NU = len(units)
    ctx = ExitStack()
    with ctx:
        base = (nc.sbuf_base + 31) // 32 * 32

        def at(name, shape, offset, dt=F32):
            return nc.alloc_sbuf_tensor_at(name, shape, dt, offset=base + offset)

        def sem(name):
            return ctx.enter_context(nc.semaphore(name))

        KB = 1024
        o_const = 0
        o_gain = o_const + 4 * N_CONST
        o_small = (o_gain + 4 * N_GAIN + 31) // 32 * 32
        o_h = (o_small + 4 * 560 + 31) // 32 * 32
        o_ot = o_h + 24 * KB
        o_raw = o_ot + 18 * KB
        o_z = o_raw + 4 * GRAN * (RAW_SLOTS + 2 * PART_SLOTS)
        o_mkv = o_z + 42 * KB
        o_turned = o_mkv + 8 * KB
        o_sums = o_turned + 28 * KB
        o_work = o_sums + 5632
        end = o_work + 29 * KB
        assert end <= 212863, end

        const = at("const", [P, N_CONST], o_const)
        gain = at("gain", [P, N_GAIN], o_gain)
        small = at("small", [P, 560], o_small)

        def cst(name):
            a, n = CONST[name]
            return const[:, a:a + n]

        def gn(name):
            a, n = GAIN[name]
            return gain[:, a:a + n]

        used = [0]

        def sm(n):
            a = used[0]
            used[0] += n
            assert used[0] <= 560
            return small[:, a:a + n]

        ident = cst("ident")
        gk = sm(24)
        ss, rstd = sm(5), sm(5)
        ffw = sm(64)
        zf, zneg, ze, zl, logf = (sm(24) for _ in range(5))
        logc = sm(64)
        fq_col = sm(16)
        fq_s = sm(8)
        pick8 = sm(P)
        hs, hr = sm(24), sm(24)
        nmax, rsum, rinv = sm(2), sm(2), sm(2)
        rss, rrs = sm(3), sm(3)
        ss2, rstd2, newton = sm(6), sm(3), sm(24)

        hT_hi = at("hT_hi", [P, KT, TOK], o_h, F32R)
        hT_lo = at("hT_lo", [P, KT, TOK], o_h + 12 * KB, F32R)
        mT_hi = at("mT_hi", [P, KT, TOK], o_h, F32R)
        mT_lo = at("mT_lo", [P, KT, TOK], o_ot, F32R)
        x2 = at("x2", [P, T, D], o_h + 12 * KB)
        memk = [at(f"memk{i}", [P, 1024], o_h + 4 * KB * i) for i in range(4)]
        memv = [at(f"memv{i}", [P, 1024], (o_h + 16 * KB, o_work)[i // 2] + 4 * KB * (i % 2)) for i in range(4)]
        memT_hi = at("memT_hi", [P, KT, NMEM], o_ot, F32R)
        memT_lo = at("memT_lo", [P, KT, NMEM], o_ot + 8 * KB, F32R)
        oT = at("oT", [P, 12, TOK], o_ot)
        oT_hi = at("oT_hi", [P, 12, TOK], o_turned, F32R)
        oT_lo = at("oT_lo", [P, 12, TOK], o_ot, F32R)
        h2T = at("h2T", [P, KT, TOK], o_z + 96 * KB)
        qtab = at("qtab", [P, HR, 4, P], o_ot + 6 * KB)
        dtab = at("dtab", [P, HR, 256], o_ot + 14 * KB)
        raw = at("raw", [P, RAW_SLOTS, GRAN], o_raw)
        w_hi = at("w_hi", [P, PART_SLOTS, GRAN], o_raw + 4 * GRAN * RAW_SLOTS, F32R)
        w_lo = at("w_lo", [P, PART_SLOTS, GRAN], o_raw + 4 * GRAN * (RAW_SLOTS + PART_SLOTS), F32R)
        z = at("z", [P, 7, T, 512], o_z)
        xT = at("xT", [P, KT, TOK], o_z)
        memT = at("memT", [P, KT, NMEM], o_z + 12 * KB)
        xtok = at("xtok", [P, T, D], o_z + 20 * KB)
        memtok = at("memtok", [P, 2, D], o_z + 32 * KB)
        mk = at("mk", [P, 2, 512], o_mkv)
        mv = at("mv", [P, 2, 512], o_mkv + 4 * KB)
        rqkT = at("rqkT", [P, 4, TOK], o_turned)
        fqT = at("fqT", [P, 4, TOK], o_turned + 6 * KB)
        fkT = at("fkT", [P, 4, TOK], o_turned + 12 * KB)
        mqT = at("mqT", [P, 4, TOK], o_turned + 18 * KB)
        mkT = at("mkT", [P, 4, NMEM], o_turned + 24 * KB)
        nf_p = at("nf_p", [8, 256], o_sums)
        nf_n = at("nf_n", [8, P], o_sums + 1024)
        nf_c = at("nf_c", [8, NB, P], o_sums + 1536)
        state = at("state", [P, 4, HR, P], o_work)
        kmask = at("kmask", [P, 4, HR, 2, 64], o_work + 8 * KB)
        qmask = at("qmask", [P, 2, 4, P], o_work + 16 * KB)
        sT = at("sT", [P, 2, 512], o_work + 20 * KB)
        osq = at("osq", [P, TOK], o_work + 24 * KB)
        orow = at("orow", [P, TOK], o_work + 24 * KB + 1536)
        qdup = at("qdup", [P, HR, P], o_work + 27 * KB)
        stp = at("stp", [P, 2, P], o_work + 24 * KB)
        foxc = [at(f"foxc{i}", [P, 1024], (o_work + 4 * KB * i) if i < 3 else o_mkv) for i in range(4)]
        qb_f = at("qb_f", [P, 2, 640], o_work + 12 * KB)
        s_sb = at("s_sb", [P, 2, 256], o_work + 17 * KB)
        p_sb = at("p_sb", [P, 2, 256], o_work + 19 * KB)
        pT = at("pT", [P, 2, 256], o_work + 21 * KB)
        qb_m = at("qb_m", [P, 4, 320], o_work + 23 * KB)
        wgu = [at(f"wgu{i}", [P, 4096], o_z + 24 * KB * i) for i in range(4)]
        wdn = [at(f"wdn{i}", [P, 2048], o_z + 24 * KB * i + 16 * KB) for i in range(4)]
        wgu_o = [at(f"wgu_o{i}", [P, 6144], o_z + 24 * KB * i) for i in range(2)]
        y_hi = at("y_hi", [P, 2, D], o_z + 96 * KB, F32R)
        y_lo = at("y_lo", [P, 2, D], o_z + 104 * KB, F32R)
        assert o_z + 112 * KB <= end
        x_hi = at("x_hi", [P, T, D], o_raw, F32R)
        x_lo = at("x_lo", [P, T, D], o_raw + 12 * KB, F32R)
        xs = at("xs", [P, 2, KT, 256], o_raw + 24 * KB)
        x_scaled = at("x_scaled", [P, T, D], o_raw + 24 * KB)
        sq_scratch = at("sq_scratch", [P, 512], o_z + 108 * KB)
        slotrow = at("slotrow", [P, 4, TOK], o_h)
        pick = at("pick_rows", [P, 2, T, 256], o_h + 6 * KB, F32R)
        rt = at("rt", [P, 896], o_ot + 12 * KB)
        const2 = at("const2", [P, N_CONST2], o_ot + 12 * KB + 3584)
        overflow = at("overflow", [1, 8], o_ot + 12 * KB + 3584 + 4 * N_CONST2, mybir.dt.int32)
        assert 12 * KB + 3584 + 4 * N_CONST2 + 32 <= 18 * KB
        act_g = at("act_g", [P, 2, DE], o_ot)
        act_h = at("act_h", [P, 2, DE], o_ot + 2 * KB)
        act_T = at("act_T", [P, 2, 256], o_ot + 4 * KB)
        back = at("back", [P, 2, TOK], o_ot + 6 * KB, F32R)
        back_a = at("back_a", [P, TOK], o_ot + 9 * KB)
        back_b = at("back_b", [P, TOK], o_ot + 9 * KB + 1536)
        wr = at("wr", [P, KT, 36], o_const + 4 * CONST["decay_s"][0])

        ov_h2T = at("ov_h2T", [P, KT, TOK], o_raw + 24 * KB)
        ov_g = at("ov_g", [P, T, DE], o_h)
        ov_h = at("ov_h", [P, T, DE], o_h + 3 * KB)
        ov_hT = at("ov_hT", [P, T, DE], o_h + 6 * KB)

        def cst2(name):
            a, n = CONST2[name]
            return const2[:, a:a + n]

        ps = ctx.enter_context(nc.psum_tensor("banks", [P, 8, 512], F32))

        s_gk, s_xT, s_xtok, s_memtok, s_const, s_gain, s_ffw = (sem(n) for n in ("s_gk", "s_xT", "s_xtok", "s_memtok", "s_const", "s_gain", "s_ffw"))
        s_memT = [sem(f"s_memT{i}") for i in range(2)]
        s_logc, s_qtab, s_dtab, s_state, s_x2, s_wr, s_const2, s_y = (sem(n) for n in ("s_logc", "s_qtab", "s_dtab", "s_state", "s_x2", "s_wr", "s_const2", "s_y"))
        s_out, s_fk_out, s_state_out, s_stp_out, hi_ready, lo_ready, gran_used, ss_ready = (sem(n) for n in ("s_out", "s_fk_out", "s_state_out", "s_stp_out", "hi_ready", "lo_ready", "gran_used", "ss_ready"))
        rstd_ready, act_hi, act_lo, acc_evac, post_done, sq_ready, hr_ready, ff_ready = (sem(n) for n in ("rstd_ready", "act_hi", "act_lo", "acc_evac", "post_done", "sq_ready", "hr_ready", "ff_ready"))
        zneg_ready, ln_ready, logf_ready, turn_ready, even_turned, odd_turned, sums_ready, sums_evac = (sem(n) for n in ("zneg_ready", "ln_ready", "logf_ready", "turn_ready", "even_turned", "odd_turned", "sums_ready", "sums_evac"))
        fqs_psum, fqs_ready, qdup_ready, kmask_ready, ret_s, ret_m, ret_q, ret_o = (sem(n) for n in ("fqs_psum", "fqs_ready", "qdup_ready", "kmask_ready", "ret_s", "ret_m", "ret_q", "ret_o"))
        ret_sq, ret_rows, ret_t, ret_te, st_ready, st_done, work_zero, qb_ready = (sem(n) for n in ("ret_sq", "ret_rows", "ret_t", "ret_te", "st_ready", "st_done", "work_zero", "qb_ready"))
        u_s, u_max, u_exp, u_p, u_T, u_Te, u_v, u_oe = (sem(n) for n in ("u_s", "u_max", "u_exp", "u_p", "u_T", "u_Te", "u_v", "u_oe"))
        gate_ready, br_mul, br_add, mt_ready, mt_hi, mt_evac, x2_ready, ss2_ready, rstd2_ready = (sem(n) for n in ("gate_ready", "br_mul", "br_add", "mt_ready", "mt_hi", "mt_evac", "x2_ready", "ss2_ready", "rstd2_ready"))
        x2t_ready, x2t_even, x2t_odd, lg_ready, route_in, route_exp, taken_ready, rank_ready, slots_ready = (sem(n) for n in ("x2t_ready", "x2t_even", "x2t_odd", "lg_ready", "route_in", "route_exp", "taken_ready", "rank_ready", "slots_ready"))
        rows_ready, rows_out, xhi_ready, xparts_ready, pick_ready, xg_ready, xs_ready, gu_ready = (sem(n) for n in ("rows_ready", "rows_out", "xhi_ready", "xparts_ready", "pick_ready", "xg_ready", "xs_ready", "gu_ready"))
        silu_ready, h_ready, hT_ready, hT_evac, dn_ready, yhi_ready, ylo_ready, back_ready = (sem(n) for n in ("silu_ready", "h_ready", "hT_ready", "hT_evac", "dn_ready", "yhi_ready", "ylo_ready", "back_ready"))
        overflow_ready, ov_x, ov_xT, ov_gu, ov_silu, ov_hd, ov_tr = (sem(n) for n in ("overflow_ready", "ov_x", "ov_xT", "ov_gu", "ov_silu", "ov_hd", "ov_tr"))
        ov_hTe, ov_down, ov_acc = (sem(n) for n in ("ov_hTe", "ov_down", "ov_acc"))
        ov_w = [sem(f"ov_w{i}") for i in range(2)]
        sc_ready, acc_done, dve_step, pool_step, act_step = (sem(n) for n in ("sc_ready", "acc_done", "dve_step", "pool_step", "act_step"))
        raw_in = [sem(f"raw_in{i}") for i in range(RAW_SLOTS)]
        foxc_in = [sem(f"foxc_in{i}") for i in range(4)]
        memk_in = [sem(f"memk_in{i}") for i in range(4)]
        memv_in = [sem(f"memv_in{i}") for i in range(4)]
        tile_evac = [sem(f"tile_evac{t}") for t in range(2)]
        gu_half, ot_hi, ot_lo = sem("gu_half"), sem("ot_hi"), sem("ot_lo")
        wgu_in = [[sem(f"wgu_in{i}_{half}") for i in range(4)] for half in range(2)]
        wdn_in = [sem(f"wdn_in{i}") for i in range(4)]

        class Chain:

            def __init__(self, eng, s):
                self.eng, self.s, self.n = eng, s, 0

            def __call__(self, ins):
                self.n += 1
                ins.then_inc(self.s, 1)
                self.eng.wait_ge(self.s, self.n)

        I32 = mybir.dt.int32

        def rsqrt(dve, chain, out, x, n):
            tmp = newton[:, 0:n]
            chain(dve.tensor_scalar(tmp.bitcast(I32), x.bitcast(I32), 1, None, ALU.logical_shift_right))
            chain(dve.tensor_scalar(out.bitcast(I32), tmp.bitcast(I32), -1.0, float(0x5F3759DF), ALU.mult, ALU.add))
            for step in range(3):
                chain(dve.tensor_tensor(tmp, out, out, ALU.mult))
                chain(dve.scalar_tensor_tensor(tmp, tmp, -0.5, x, ALU.mult, ALU.mult))
                ins = dve.scalar_tensor_tensor(out, tmp, 1.5, out, ALU.add, ALU.mult)
                if step < 2:
                    chain(ins)
            return ins

        def bank_of(c, t):
            if c < C_GATE:
                return ((0, 1), (2, 3), (4, 5, 6), (7, 0, 1), (2, 3, 4), (5, 6, 7), (0, 1, 2), (3, 4, 5), (0, 1, 2))[c][t]
            if c < C_BR + 4:
                return t
            return 3 * ((c - C_BR + 1) % 2) + t

        def last_user(c, t):
            for b in range(c - 1, -1, -1):
                for u in range(CHUNKS[b][2]):
                    if bank_of(b, u) == bank_of(c, t):
                        return b, u
            return None

        def wait_bank(pe, c, t):
            if last_user(c, t) is None:
                return
            b, u = last_user(c, t)
            if b >= C_BR:
                pe.wait_ge(br_mul, 3 * (b - C_BR) + u + 1)
            elif u == CHUNKS[b][2] - 1:
                pe.wait_ge(acc_evac, b + 1)
            else:
                pe.wait_ge(tile_evac[u], b + 1 if u == 0 else b - 1)

        chunk_of = [c for c in range(len(CHUNKS)) for _ in range(FIRST[c], FIRST[c + 1])]
        Z_OF = {C_RQK: 0, C_RV: 1, C_RG: 2, C_FQ: 3, C_FK: 4, C_FV: 5, C_MQ: 6}
        GATE_SLOT = [3, 4, 6, 0, 1, 2]
        turns = [(name, j) for name in ("rqk", "fq", "fk", "mq", "mk") for j in range(4)]
        GAMMA_N = [float((1.0 - 2.0 ** (-5.0 - h)) ** NI) for h in range(HR)]

        def group_of(i):
            return i // 2 if i < 16 else i - 8

        def last_of(i):
            return i >= 16 or i % 2 == 1

        NGROUP = group_of(NU - 1) + 1
        rqk, rv, rg, fq, fk, fv, mq = (z[:, i, :, :] for i in range(7))
        POSTED = {C_MK: 1, C_RQK: 2, C_RG: 3, C_FQ: 4, C_FK: 5, C_MQ: 6}
        NORMS = {C_MK: (mk[:, :, :], 8, P, "mem_k", 0), C_FQ: (fq, 24, 64, "fox_q", 1), C_FK: (fk, 24, 64, "fox_k", 2), C_MQ: (mq, 12, P, "mem_q", 3)}
        last_norm = [C_MK, C_FQ, C_FK, C_MQ]

        def keys(i):
            return P if units[i][0] == "foxp" and units[i][2] == 0 else 256

        def turn_wait(eng, j):
            eng.wait_ge(odd_turned if j % 2 else even_turned, j // 2 + 1)

        def turn_out(eng, copy, i):
            name, j = turns[i]
            eng.wait_ge(turn_ready, i + 1)
            dst = {"rqk": rqkT, "fq": fqT, "fk": fkT, "mq": mqT, "mk": mkT}[name]
            n = NMEM if name == "mk" else TOK
            scale = {"fq": 64 ** -0.5, "mq": P ** -0.5}.get(name, 1.0)
            copy(dst[:, j, :], ps[:, 3 + i % 5, 0:n], scale).then_inc(odd_turned if i % 2 else even_turned, 1)

        zq = at("zq", [P, T * 512], o_work + 16 * KB)
        scratch = at("scratch", [P, 2, D], o_work)
        ffw_hi = at("ffw_hi", [P, 64], o_work + 8 * KB, F32R)
        ffw_lo = at("ffw_lo", [P, 64], o_work + 8 * KB + 256, F32R)
        block = ctx.enter_context(nc.Block())

        rt_used = [0]

        def R(n):
            a = rt_used[0]
            rt_used[0] += n
            return rt[:, a:a + n]

        r_l, r_d4, r_e4, r_t4, r_oh = R(108), R(12), R(12), R(12), R(12)
        r_m4, r_x4, r_m1, r_m2, r_x1, r_d2, r_e2, r_s4, r_w1, r_w2 = (R(3) for _ in range(10))
        r_le, r_le2, r_t8, r_oh1, r_oh2 = (R(24) for _ in range(5))
        r_s1, r_s2, r_full = R(3), R(3), R(1)
        r_x, r_m1e, r_m2e, r_m = R(96), R(96), R(96), R(96)
        r_over = R(96)
        r_q1, r_q2 = R(24), R(24)
        r_wa, r_wb = R(16), R(16)

        def route(dve, chain):
            def v(a, n):
                return a.rearrange("p (t n) -> p t n", t=T) if n else a

            def wide(a, n):
                return a.unsqueeze(2).to_broadcast([P, T, n])

            def first_best(values, n, mx, tmp, tmp_mx, onehot, rev):
                chain(dve.tensor_reduce(mx, values, AX, ALU.max))
                chain(dve.tensor_tensor(v(tmp, n), values, wide(mx, n), ALU.is_equal))
                chain(dve.tensor_tensor(v(tmp, n), v(tmp, n), v(cst(rev), n), ALU.mult))
                chain(dve.tensor_reduce(tmp_mx, v(tmp, n), AX, ALU.max))
                chain(dve.tensor_tensor(v(onehot, n), v(tmp, n), wide(tmp_mx, n), ALU.is_equal))

            dve.wait_ge(lg_ready, 1)
            L = v(r_l, 36)
            for t in range(T):
                ins = dve.scalar_tensor_tensor(L[:, t, :], ps[:, bank_of(C_OUT, t), 0:36], rstd2[:, t:t + 1], gn("route"), ALU.mult, ALU.add)
            chain(ins)
            first_best(L[:, :, 0:4], 4, r_m4, r_t4, r_x4, r_oh, "rev4")
            chain(dve.tensor_tensor(v(r_d4, 4), L[:, :, 0:4], wide(r_m4, 4), ALU.subtract))
            x4 = r_x.rearrange("p (t e g) -> p t e g", t=T, e=NE)
            chain(dve.tensor_tensor(x4, L[:, :, 4:36].rearrange("p t (g e) -> p t e g", g=NG), v(r_oh, 4).unsqueeze(2).to_broadcast([P, T, NE, NG]), ALU.mult))
            chain(dve.tensor_reduce(v(r_le, 8), x4, AX, ALU.add))
            first_best(v(r_le, 8), 8, r_m1, r_t8, r_x1, r_oh1, "rev8")
            chain(dve.scalar_tensor_tensor(r_le2, r_oh1, -BIG, r_le, ALU.mult, ALU.add))
            first_best(v(r_le2, 8), 8, r_m2, r_t8, r_x1, r_oh2, "rev8")
            dve.tensor_tensor(r_d2, r_m2, r_m1, ALU.subtract).then_inc(route_in, 1)
            for oh_e, m_e in ((r_oh1, r_m1e), (r_oh2, r_m2e)):
                chain(dve.tensor_tensor(m_e.rearrange("p (t g e) -> p t g e", t=T, g=NG), v(r_oh, 4).unsqueeze(3).to_broadcast([P, T, NG, NE]),
                                        v(oh_e, 8).unsqueeze(2).to_broadcast([P, T, NG, NE]), ALU.mult))
            dve.tensor_tensor(r_m, r_m1e, r_m2e, ALU.add).then_inc(taken_ready, 1)
            dve.wait_ge(route_exp, 1)
            chain(dve.tensor_reduce(r_s4, v(r_e4, 4), AX, ALU.add))
            chain(dve.tensor_scalar(r_w2, r_e2, 1.0, None, ALU.add))
            chain(dve.tensor_tensor(r_w1, r_w2, r_s4, ALU.mult))
            chain(dve.reciprocal(r_w1, r_w1))
            chain(dve.tensor_tensor(r_w2, r_e2, r_w1, ALU.mult))
            dve.wait_ge(rank_ready, 1)
            dve.wait_ge(s_const2, 16)
            rank, pos, over = ps[:, 6, 0:96], r_x, r_l[:, 0:96]
            chain(dve.tensor_scalar(over, rank, float(CAP), None, ALU.is_ge))
            chain(dve.tensor_tensor(pos, rank, cst2("first_slot"), ALU.add))
            chain(dve.scalar_tensor_tensor(pos, over, 1.0e6, pos, ALU.mult, ALU.add))
            chain(dve.tensor_tensor(r_m, r_m1e, pos, ALU.mult))
            chain(dve.tensor_reduce(r_s1, v(r_m, 32), AX, ALU.add))
            chain(dve.tensor_tensor(pos, r_m2e, pos, ALU.mult))
            chain(dve.tensor_reduce(r_s2, v(pos, 32), AX, ALU.add))
            chain(dve.tensor_reduce(r_full[0:1, :], ps[0:1, 6, 96:128], AX, ALU.max))
            dve.tensor_scalar(overflow[0:1, 0:1], r_full[0:1, :], float(CAP), None, ALU.is_gt).then_inc(overflow_ready, 1)
            q = cst2("quad_slot").rearrange("p (q t) -> p q t", t=T)
            for r_q, r_s in ((r_q1, r_s1), (r_q2, r_s2)):
                ins = dve.tensor_tensor(r_q.rearrange("p (q t) -> p q t", t=T), r_s.unsqueeze(1).to_broadcast([P, QUADS, T]), q, ALU.subtract)
                if r_q is r_q1:
                    chain(ins)
            ins.then_inc(slots_ready, 1)
            dve.wait_ge(slots_ready, 1)

        def overflow_weights(dve, chain):
            for m_e, r_w in ((r_m1e, r_w1), (r_m2e, r_w2)):
                chain(dve.tensor_tensor(m_e, m_e, r_l[:, 0:96], ALU.mult))
                chain(dve.tensor_tensor(m_e.rearrange("p (t n) -> p t n", t=T), m_e.rearrange("p (t n) -> p t n", t=T),
                                        r_w.unsqueeze(2).to_broadcast([P, T, NG * NE]), ALU.mult))
            chain(dve.tensor_tensor(r_over, r_m1e, r_m2e, ALU.add))

        def if_overflow(eng):
            eng.wait_ge(overflow_ready, 1)
            return eng.If(eng.value_load(overflow[0:1, 0:1], min_val=0, max_val=1))

        @block.sync
        def _(sp):
            def load(dst, src, s):
                sp.dma_start(dst, src).then_inc(s, 16)

            def granule(g):
                old = g - RAW_SLOTS
                if old >= 0:
                    sp.wait_ge(lo_ready, old + 1)
                load(raw[:, g % RAW_SLOTS, :], io["wstream"][g], raw_in[g % RAW_SLOTS])

            def load_pair(p):
                for half in range(2):
                    if p >= 2:
                        sp.wait_ge((gu_half, gu_ready)[half], p - 1)
                    for e in (2 * p, 2 * p + 1):
                        cols = slice(2048 * half, 2048 * half + 2048)
                        load(wgu[e % 4][:, cols], io["wexp"][e, :, cols], wgu_in[half][e % 4])
                if p >= 2:
                    sp.wait_ge(dn_ready, p - 1)
                for e in (2 * p, 2 * p + 1):
                    load(wdn[e % 4][:, :], io["wexp"][e, :, 4096:6144], wdn_in[e % 4])

            load(gk, io["gk"], s_gk)
            load(memT[:, 0:4, :], io["memT"][:, 0:4, :], s_memT[0])
            granule(0)
            load(memT[:, 4:8, :], io["memT"][:, 4:8, :], s_memT[1])
            for g in range(1, RAW_SLOTS):
                granule(g)
            load(xT[:, :, :], io["xT"], s_xT)
            load(ffw, io["ffw"], s_ffw)
            for kind, *arg in steps:
                i = arg[0] if arg else 0
                if kind == "k" and i + RAW_SLOTS < NGRAN:
                    granule(i + RAW_SLOTS)
                    if i == 3:
                        load(memtok[:, :, :], io["memtok"], s_memtok)
                    elif i == 4:
                        load(xtok[:, :, :], io["xtok"], s_xtok)
                        load(gain[:, :], io["gain"], s_gain)
                    elif i == 9:
                        load(const[:, :], io["const"], s_const)
                        load(logc, io["logc"], s_logc)
                elif kind == "post" and i == C_MV:
                    sp.wait_ge(gran_used, FIRST[2])
                    sp.wait_ge(ss_ready, 5)
                    sp.wait_ge(act_lo, 17)
                    load(qtab[:, :, :, :], io["qtab"], s_qtab)
                    load(dtab[:, :, :], io["dtab"], s_dtab)
                elif kind == "forget":
                    sp.wait_ge(ff_ready, 1)
                    load(state[:, :, :, :], io["state"], s_state)
                elif kind == "mem_caches":
                    sp.wait_ge(gran_used, FIRST[C_BR])
                    for b in range(4):
                        load(memk[b][:, :], io["memc"][b, :, 0:1024], memk_in[b])
                    for b in range(2):
                        load(memv[b][:, :], io["memc"][b, :, 1024:2048], memv_in[b])
                elif kind == "unit_v" and units[i][0] == "foxs" and units[i][1] == NB - 1:
                    sp.wait_ge(u_v, i + 1)
                    for b in range(2, 4):
                        load(memv[b][:, :], io["memc"][b, :, 1024:2048], memv_in[b])
                elif kind == "unit_v" and units[i][0] == "mems" and units[i][1] < 2:
                    a = units[i][1]
                    sp.wait_ge(u_v, i + 1)
                    for b in (2 * a + 4, 2 * a + 5):
                        load(memv[b % 4][:, :], io["memc"][b, :, 1024:2048], memv_in[b % 4])
                elif kind == "unit_s" and units[i][0] == "mems" and units[i][1] < 2:
                    a = units[i][1]
                    sp.wait_ge(u_s, i + 1)
                    for b in (2 * a + 4, 2 * a + 5):
                        load(memk[b % 4][:, :], io["memc"][b, :, 0:1024], memk_in[b % 4])
                elif kind == "attention_done":
                    sp.wait_ge(u_v, NU)
                    load(x2[:, :, :], io["xtok"], s_x2)
                elif kind == "residual" and i == 0:
                    sp.wait_ge(mt_ready, 8)
                    load_pair(0)
                    load_pair(1)
                elif kind == "turn_merged" and i == 1:
                    sp.wait_ge(gran_used, FIRST[C_OUT])
                    load(wr[:, :, :], io["wr"], s_wr)
                    load(const2[:, :], io["const2"], s_const2)
            for p in range(2, PAIRS):
                load_pair(p)
            with if_overflow(sp):
                for b in range(2):
                    sp.wait_ge(dn_ready, PAIRS)
                    load(wgu_o[b][:, :], io["wexp"][b], ov_w[b])
                with sp.Fori(0, NG * NE // 2 - 1) as i:
                    for b in range(2):
                        sp.wait_ge(ov_down, 12 * i + 6 * b + 6)
                        load(wgu_o[b][:, :], io["wexp"][bass.ds(2 * i + b + 2, 1)].rearrange("a p c -> p (a c)"), ov_w[b])
                sp.wait_ge(ov_acc, 6 * NG * NE)
            with sp.Else():
                pass
            for t in range(T):
                sp.wait_ge(acc_done, 6 * (PAIRS - 1) + 2 * t + 2)
                sp.dma_start(io["y"][:, t, :], x2[:, t, :]).then_inc(s_y, 16)
            sp.wait_ge(s_y, 16 * T)

        @block.scalar
        def _(act):
            chain = Chain(act, act_step)
            for kind, *arg in steps:
                i = arg[0] if arg else 0
                if kind == "prep_mem":
                    act.wait_ge(s_memT[i // 4], 16)
                    act.wait_ge(s_gk, 16)
                    act.activation(memT_hi[:, i, :], memT[:, i, :], ACT.Copy, scale=gk[:, 8 + i:9 + i]).then_inc(act_hi, 1)
                elif kind == "prep_x":
                    act.wait_ge(s_xT, 16)
                    act.activation(hT_hi[:, i, :], xT[:, i, :], ACT.Copy, scale=gk[:, i:i + 1]).then_inc(act_hi, 1)
                elif kind == "prep_ff":
                    act.wait_ge(s_ffw, 16)
                    act.activation(ffw_hi[:, :], ffw, ACT.Copy).then_inc(act_hi, 1)
                elif kind == "norm1":
                    act.wait_ge(s_memtok, 16)
                    for t in range(2):
                        act.activation(scratch[:, t, :], memtok[:, t, :], ACT.Square, accum_out=ss[:, 3 + t:4 + t]).then_inc(ss_ready, 1)
                    act.wait_ge(s_xtok, 16)
                    for t in range(T):
                        act.wait_ge(ss_ready, 1 + t)
                        act.activation(scratch[:, t % 2, :], xtok[:, t, :], ACT.Square, accum_out=ss[:, t:t + 1]).then_inc(ss_ready, 1)
                elif kind == "split":
                    act.wait_ge(raw_in[i % RAW_SLOTS], 16 * (i // RAW_SLOTS + 1))
                    if i >= PART_SLOTS:
                        act.wait_ge(gran_used, i - PART_SLOTS + 1)
                    act.activation(w_hi[:, i % PART_SLOTS, :], raw[:, i % RAW_SLOTS, :], ACT.Copy).then_inc(hi_ready, 1)
                elif kind == "evac":
                    act.wait_ge(rstd_ready, 1)
                    act.wait_ge(gran_used, FIRST[i + 1])
                    if i < C_RQK:
                        dst = (mk, mv)[i][:, :, :]
                    elif i < C_GATE:
                        dst = z[:, Z_OF[i], :, :]
                    else:
                        dst = z[:, GATE_SLOT[i - C_GATE], :, :]
                    if i == C_RQK:
                        act.wait_ge(act_lo, 17)
                    elif i == C_GATE:
                        act.wait_ge(turn_ready, 8)
                    elif i == C_GATE + 1:
                        act.wait_ge(turn_ready, 12)
                        act.wait_ge(s_fk_out, 16)
                    elif i == C_GATE + 2:
                        act.wait_ge(turn_ready, 16)
                    elif i >= C_GATE + 3:
                        act.wait_ge(st_ready, 5)
                        act.wait_ge(kmask_ready, 1)
                        act.wait_ge(ret_rows, HR)
                    f = ACT.Silu if i == C_RG else ACT.Copy
                    for t in range(CHUNKS[i][2]):
                        sc = rstd[:, 3 + t:4 + t] if i < C_RQK else rstd[:, t:t + 1]
                        last = t == CHUNKS[i][2] - 1
                        act.activation(dst[:, t, :], ps[:, bank_of(i, t), :], f, scale=sc).then_inc(acc_evac if last else tile_evac[t], 1)
                elif kind == "forget":
                    act.wait_ge(zneg_ready, 1)
                    chain(act.activation(ze, zneg, ACT.Exp))
                    act.activation(zl, ze, ACT.Ln, bias=1.0).then_inc(ln_ready, 1)
                elif kind == "turn":
                    if i % 2 == 0:
                        turn_out(act, lambda o, a, m: act.activation(o, a, ACT.Copy, scale=m), i)
                    if i == 2:
                        act.wait_ge(even_turned, 1)
                        act.wait_ge(odd_turned, 1)
                        for hl in range(2):
                            for b2 in range(2):
                                ins = act.activation(qdup[64 * b2:64 * b2 + 64, hl::2, :], rqkT[64 * hl:64 * hl + 64, 0:2, SEQ:TOK], ACT.Copy)
                        ins.then_inc(qdup_ready, 1)
                elif kind == "decay_sums":
                    act.wait_ge(sums_ready, 1)
                    act.activation(nf_p[:, :], ps[0:8, 3, 0:256], ACT.Copy, scale=-1.0)
                    act.activation(nf_n[:, :], ps[0:8, 3, 256:384], ACT.Copy, scale=-1.0)
                    for q in range(2):
                        act.activation(nf_c[:, 4 * q:4 * q + 4, :], ps[0:8, 4 + q, :].rearrange("p (b j) -> p b j", b=4), ACT.Copy, scale=-1.0)
                    act.activation(fq_col, ps[:, 6, 0:16], ACT.Copy).then_inc(sums_evac, 1)
                elif kind == "ret_o":
                    act.wait_ge(ret_o, i + 1)
                    if i:
                        act.wait_ge(ret_rows, i)
                    act.activation(osq[:, :], ps[:, 6, 0:TOK], ACT.Square, scale=float(P) ** -0.5).then_inc(ret_sq, 1)
                elif kind == "ret_t":
                    act.wait_ge(ret_t, i + 1)
                    act.activation(oT[:, i, :], ps[:, 7, 0:TOK], ACT.Copy).then_inc(ret_te, 1)
                elif kind == "unit_s":
                    act.wait_ge(u_max, i + 1)
                    n = keys(i)
                    src = s_sb[:, i % 2, 0:n] if units[i][0][:3] == "fox" else ps[:, 3 + i % 2, 0:n]
                    if i >= 2:
                        act.wait_ge(u_T, i - 1)
                    act.activation(p_sb[:, i % 2, 0:n], src, ACT.Exp, bias=nmax[:, i % 2:i % 2 + 1],
                                   accum_out=rsum[:, i % 2:i % 2 + 1]).then_inc(u_exp, 1)
                elif kind == "unit_p":
                    n = keys(i)
                    act.wait_ge(u_T, i + 1)
                    if i >= 2:
                        act.wait_ge(u_v, i - 1)
                    act.activation(pT[:, i % 2, 0:n], ps[:, 5, 0:n], ACT.Copy).then_inc(u_Te, 1)
                elif kind == "unit_v" and last_of(i):
                    act.wait_ge(u_v, i + 1)
                    o = ps[:, 6 + group_of(i) % 2, 0:P]
                    what, a, t = units[i]
                    if what == "foxp":
                        ins = act.activation(oT[:, 4 + a // 2, t * P:(t + 1) * P], o, ACT.Copy)
                    elif what == "memp":
                        ins = act.activation(oT[:, 8 + a, t * P:(t + 1) * P], o, ACT.Copy)
                    elif what == "foxs":
                        cols = slice(SEQ + a * NI, SEQ + (a + 1) * NI)
                        for hl in range(2):
                            half = slice(64 * hl, 64 * hl + 64)
                            ins = act.activation(oT[half, 4:8, cols],
                                                 o[half, :].rearrange("p (g i) -> p g i", i=2 * NI)[:, :, hl * NI:(hl + 1) * NI], ACT.Copy)
                    else:
                        for b2 in range(2):
                            b = 2 * a + b2
                            ins = act.activation(oT[:, 8:12, SEQ + b * NI:SEQ + (b + 1) * NI],
                                                 o[:, 64 * b2:64 * b2 + 64].rearrange("p (h i) -> p h i", h=HM), ACT.Copy)
                    ins.then_inc(u_oe, 1)
                elif kind == "parts":
                    if i == 0:
                        act.wait_ge(ret_te, HR)
                    elif i == 1:
                        act.wait_ge(u_oe, NGROUP - NB // 2)
                        act.wait_ge(qb_ready, NB)
                    else:
                        act.wait_ge(u_oe, NGROUP)
                    for j in range(4 * i, 4 * i + 4):
                        act.activation(oT_hi[:, j, :], oT[:, j, :], ACT.Copy).then_inc(ot_hi, 1)
                elif kind == "gates":
                    act.wait_ge(acc_evac, C_BR)
                    for c in range(6):
                        act.activation(z[:, GATE_SLOT[c], :, :], z[:, GATE_SLOT[c], :, :], ACT.Sigmoid).then_inc(gate_ready, 1)
                elif kind == "turn_merged":
                    for j in range(4 * i, 4 * i + 4):
                        act.wait_ge(mt_ready, j + 1)
                        act.activation(mT_hi[:, j, :], ps[:, 6 + j % 2, 0:TOK], ACT.Copy).then_inc(mt_hi, 1)
                elif kind == "squares2":
                    act.wait_ge(x2_ready, i + 1)
                    act.wait_ge(u_oe, NGROUP)
                    for t in range(T):
                        if 3 * i + t:
                            act.wait_ge(ss2_ready, 3 * i + t)
                        act.activation(sq_scratch[:, :], x2[:, t, 512 * i:512 * i + 512], ACT.Square, accum_out=ss2[:, 3 * i + t:3 * i + t + 1]).then_inc(ss2_ready, 1)
                elif kind == "turn_x2":
                    for j in range(4 * i + 1, 4 * i + 4, 2):
                        act.wait_ge(x2t_ready, j + 1)
                        act.activation(h2T[:, j, :], ps[:, 7, 0:TOK], ACT.Copy, scale=gk[:, 16 + j:17 + j]).then_inc(x2t_odd, 1)
                elif kind == "x_parts":
                    act.wait_ge(rstd2_ready, 1)
                    for t in range(T):
                        act.activation(x_hi[:, t, :], x2[:, t, :], ACT.Copy, scale=rstd2[:, t:t + 1]).then_inc(xhi_ready, 1)
                elif kind == "route":
                    act.wait_ge(route_in, 1)
                    act.activation(r_e4, r_d4, ACT.Exp)
                    act.activation(r_e2, r_d2, ACT.Exp).then_inc(route_exp, 1)
            for what, a, *m in moe:
                if what == "rows_out":
                    act.wait_ge(rows_ready, 1)
                    for j in range(4):
                        act.activation(slotrow[:, j, :], ps[:, j, 0:TOK], ACT.Copy).then_inc(rows_out, 1)
                elif what == "gather":
                    act.wait_ge(xg_ready, 8 * a + m[0] + 1)
                    act.activation(xs[:, a % 2, m[0], :], ps[:, MISC[m[1] % 3], 0:256], ACT.Copy, scale=gk[:, 16 + m[0]:17 + m[0]]).then_inc(xs_ready, 1)
                elif what == "silu":
                    act.wait_ge(gu_ready, a + 1)
                    if a >= 2:
                        act.wait_ge(h_ready, a - 1)
                    act.activation(act_g[:, a % 2, :], ps[:, 2 + a % 2, 0:DE], ACT.Silu).then_inc(silu_ready, 1)
                elif what == "y_out":
                    act.wait_ge(dn_ready, a + 1)
                    if a >= 2:
                        act.wait_ge(acc_done, 6 * (a - 1))
                    for n in range(2):
                        act.activation(y_hi[:, a % 2, 512 * n:512 * n + 512], ps[:, 5 + n, :], ACT.Copy).then_inc(yhi_ready, 1)
            with if_overflow(act):
                for k in range(KT):
                    act.wait_ge(ov_x, k + 1)
                    act.activation(ov_h2T[:, k, :], ps[:, k, 0:TOK], ACT.Copy, scale=gk[:, 16 + k:17 + k]).then_inc(ov_xT, 1)
                with act.Fori(0, NG * NE) as e:
                    for t in range(T):
                        act.wait_ge(ov_gu, 3 * e + t + 1)
                        act.activation(ov_g[:, t, :], ps[:, t, 0:DE], ACT.Silu).then_inc(ov_silu, 1)
                    for t in range(T):
                        act.wait_ge(ov_tr, 3 * e + t + 1)
                        act.activation(ov_hT[:, t, :], ps[:, 3 + t, 0:DE], ACT.Copy).then_inc(ov_hTe, 1)
            with act.Else():
                pass

        @block.vector
        def _(dve):
            chain = Chain(dve, dve_step)
            for kind, *arg in steps:
                i = arg[0] if arg else 0
                if kind == "prep_mem":
                    dve.wait_ge(act_hi, i + 1)
                    dve.scalar_tensor_tensor(memT_lo[:, i, :], memT[:, i, :], gk[:, 8 + i:9 + i], memT_hi[:, i, :].bitcast(F32),
                                             ALU.mult, ALU.subtract).then_inc(act_lo, 1)
                elif kind == "prep_x":
                    dve.wait_ge(act_hi, KT + i + 1)
                    dve.scalar_tensor_tensor(hT_lo[:, i, :], xT[:, i, :], gk[:, i:i + 1], hT_hi[:, i, :].bitcast(F32),
                                             ALU.mult, ALU.subtract).then_inc(act_lo, 1)
                elif kind == "prep_ff":
                    dve.wait_ge(act_hi, 2 * KT + 1)
                    dve.tensor_tensor(ffw_lo[:, :], ffw, ffw_hi[:, :].bitcast(F32), ALU.subtract).then_inc(act_lo, 1)
                elif kind == "norm1":
                    dve.wait_ge(ss_ready, 5)
                    chain(dve.tensor_scalar(ss, ss, 1.0 / D, EPS, ALU.mult, ALU.add))
                    rsqrt(dve, chain, rstd, ss, 5).then_inc(rstd_ready, 1)
                elif kind == "split":
                    dve.wait_ge(hi_ready, i + 1)
                    if i >= PART_SLOTS:
                        dve.wait_ge(gran_used, i - PART_SLOTS + 1)
                    dve.tensor_tensor(w_lo[:, i % PART_SLOTS, :], raw[:, i % RAW_SLOTS, :], w_hi[:, i % PART_SLOTS, :].bitcast(F32),
                                      ALU.subtract).then_inc(lo_ready, 1)
                elif kind == "post" and i in NORMS:
                    _, rows, n, g, order = NORMS[i]
                    dve.wait_ge(sq_ready, order + 1)
                    chain(dve.tensor_reduce(hs[:, 0:rows], zq[:, 0:rows * n].rearrange("p (r n) -> p r n", n=n), AX, ALU.add))
                    chain(dve.tensor_scalar(hs[:, 0:rows], hs[:, 0:rows], 1.0 / n, EPS, ALU.mult, ALU.add))
                    if order:
                        dve.wait_ge(post_done, POSTED[last_norm[order - 1]])
                    rsqrt(dve, chain, hr[:, 0:rows], hs[:, 0:rows], rows).then_inc(hr_ready, 1)
                elif kind == "forget":
                    dve.wait_ge(ff_ready, 1)
                    dve.wait_ge(s_gain, 16)
                    for t in range(T):
                        ins = dve.scalar_tensor_tensor(zf[:, 8 * t:8 * t + 8], ps[:, 6, 8 * t:8 * t + 8], rstd[:, t:t + 1], gn("forget"), ALU.mult, ALU.add)
                    chain(ins)
                    dve.scalar_tensor_tensor(zneg, zf, -1.0, zf, ALU.mult, ALU.min).then_inc(zneg_ready, 1)
                    dve.wait_ge(ln_ready, 1)
                    dve.scalar_tensor_tensor(logf, zf, 0.0, zl, ALU.min, ALU.subtract).then_inc(logf_ready, 1)
                elif kind == "turn" and i % 2 == 1:
                    turn_out(dve, lambda o, a, m: dve.tensor_scalar(o, a, m, None, ALU.mult), i)
                elif kind == "ret_s":
                    dve.wait_ge(ret_s, i + 1)
                    dve.wait_ge(post_done, 6)
                    dve.wait_ge(s_dtab, 16)
                    if i >= 2:
                        dve.wait_ge(ret_o, i - 1)
                    b = 3 + i % 2
                    dve.tensor_tensor(sT[:, i % 2, 0:256], ps[:, b, 0:256], dtab[:, i, :], ALU.mult)
                    dve.tensor_tensor(sT[:, i % 2, 256:384], ps[:, b, 256:384], dtab[:, i, 0:P], ALU.mult)
                    dve.tensor_tensor(sT[:, i % 2, 384:512], ps[:, b, 384:512], cst("decay_s")[:, i * P:(i + 1) * P], ALU.mult).then_inc(ret_m, 1)
                    dve.wait_ge(qdup_ready, 1)
                    dve.wait_ge(s_qtab, 16)
                    dve.tensor_tensor(qmask[:, i % 2, :, :], qdup[:, i, :].unsqueeze(1).to_broadcast([P, 4, P]), qtab[:, i, :, :],
                                      ALU.mult).then_inc(ret_q, 1)
                elif kind == "decay_query":
                    dve.wait_ge(fqs_psum, 1)
                    chain(dve.tensor_tensor(pick8.rearrange("p (b i) -> p b i", b=NB), ps[:, 5, 0:P].rearrange("p (b i) -> p b i", b=NB),
                                            cst("pick").unsqueeze(1).to_broadcast([P, NB, NI]), ALU.mult))
                    dve.tensor_reduce(fq_s, pick8.rearrange("p (b i) -> p b i", b=NB), AX, ALU.add, negate=True).then_inc(fqs_ready, 1)
                elif kind == "ret_o":
                    dve.wait_ge(ret_sq, i + 1)
                    chain(dve.tensor_reduce(rss, osq[:, :].rearrange("p (t v) -> p t v", t=T), AX, ALU.add))
                    chain(dve.tensor_scalar(rss, rss, EPS, None, ALU.add))
                    chain(rsqrt(dve, chain, rrs, rss, T))
                    if i:
                        dve.wait_ge(ret_t, i)
                    rows = orow[:, :].rearrange("p (t v) -> p t v", t=T)
                    chain(dve.tensor_tensor(rows, ps[:, 6, 0:TOK].rearrange("p (t v) -> p t v", t=T), rg[:, :, i * P:(i + 1) * P], ALU.mult))
                    dve.tensor_tensor(rows, rows, rrs.unsqueeze(2).to_broadcast([P, T, P]), ALU.mult).then_inc(ret_rows, 1)
                elif kind == "ret_state":
                    dve.wait_ge(s_state, 16)
                    for h in range(HR):
                        dve.wait_ge(st_ready, h + 1)
                        dve.scalar_tensor_tensor(state[:, :, h, :], state[:, :, h, :], GAMMA_N[h], ps[:, 3 + h, :].rearrange("p (b v) -> p b v", b=4),
                                                 ALU.mult, ALU.add).then_inc(st_done, 1)
                    dve.wait_ge(st_ready, 5)
                    dve.tensor_copy(stp[:, :, :], ps[:, 7, 0:256].rearrange("p (g v) -> p g v", g=2)).then_inc(st_done, 1)
                elif kind == "unit_s":
                    what, a, t = units[i]
                    n = keys(i)
                    dve.wait_ge(u_s, i + 1)
                    if i == 0:
                        dve.wait_ge(sums_evac, 1)
                    if i >= 2:
                        dve.wait_ge(u_exp, i - 1)
                    row = s_sb[:, i % 2, :]
                    psc = ps[:, 3 + i % 2, :]
                    if what == "foxp":
                        m = cst("zeros_causal")[:, 256 - n:256]
                        chain(dve.scalar_tensor_tensor(row[:, 0:n], psc[:, 0:n], fq_col[:, 8 * t + a:8 * t + a + 1], m, ALU.add, ALU.add))
                    elif what == "foxs":
                        dve.tensor_scalar(row[:, 0:P], psc[:, 0:P], fq_s[:, a:a + 1], None, ALU.add)
                        m = cst("maskwin")[:, (NB - 1 - a) * NI:(NB - 1 - a) * NI + P]
                        chain(dve.scalar_tensor_tensor(row[:, P:256], psc[:, P:256], fq_s[:, a:a + 1], m, ALU.add, ALU.add))
                    src = row if what[:3] == "fox" else psc
                    dve.tensor_reduce(nmax[:, i % 2:i % 2 + 1], src[:, 0:n], AX, ALU.max, negate=True).then_inc(u_max, 1)
                elif kind == "unit_w":
                    n = keys(i)
                    dve.wait_ge(u_exp, i + 1)
                    chain(dve.reciprocal(rinv[:, i % 2:i % 2 + 1], rsum[:, i % 2:i % 2 + 1]))
                    dve.tensor_scalar(p_sb[:, i % 2, 0:n], p_sb[:, i % 2, 0:n], rinv[:, i % 2:i % 2 + 1], None, ALU.mult).then_inc(u_p, 1)
                elif kind == "merge":
                    c = i - C_BR
                    dve.wait_ge(gran_used, FIRST[i + 1])
                    dve.wait_ge(gate_ready, c + 1)
                    for t in range(T):
                        dve.tensor_tensor(z[:, GATE_SLOT[c], t, :], ps[:, bank_of(i, t), :], z[:, GATE_SLOT[c], t, :], ALU.mult).then_inc(br_mul, 1)
                elif kind == "parts":
                    for j in range(4 * i, 4 * i + 4):
                        dve.wait_ge(ot_hi, j + 1)
                        dve.tensor_tensor(oT_lo[:, j, :], oT[:, j, :], oT_hi[:, j, :].bitcast(F32), ALU.subtract).then_inc(ot_lo, 1)
                elif kind == "turn_merged":
                    for j in range(4 * i, 4 * i + 4):
                        dve.wait_ge(mt_hi, j + 1)
                        dve.tensor_tensor(mT_lo[:, j, :], ps[:, 6 + j % 2, 0:TOK], mT_hi[:, j, :].bitcast(F32), ALU.subtract).then_inc(mt_evac, 1)
                elif kind == "residual":
                    dve.wait_ge(gran_used, FIRST[C_OUT + i + 1])
                    dve.wait_ge(s_x2, 16)
                    for t in range(T):
                        ins = dve.tensor_tensor(x2[:, t, 512 * i:512 * i + 512], ps[:, bank_of(C_OUT + i, t), :], x2[:, t, 512 * i:512 * i + 512], ALU.add)
                    ins.then_inc(x2_ready, 1)
                elif kind == "turn_x2":
                    for j in range(4 * i, 4 * i + 4, 2):
                        dve.wait_ge(x2t_ready, j + 1)
                        dve.tensor_scalar(h2T[:, j, :], ps[:, 6, 0:TOK], gk[:, 16 + j:17 + j], None, ALU.mult).then_inc(x2t_even, 1)
                elif kind == "norm2":
                    dve.wait_ge(ss2_ready, 2 * T)
                    chain(dve.tensor_tensor(ss2[:, 0:T], ss2[:, 0:T], ss2[:, T:2 * T], ALU.add))
                    chain(dve.tensor_scalar(ss2[:, 0:T], ss2[:, 0:T], 1.0 / D, EPS, ALU.mult, ALU.add))
                    rsqrt(dve, chain, rstd2, ss2[:, 0:T], T).then_inc(rstd2_ready, 1)
                    dve.wait_ge(rstd2_ready, 1)
                elif kind == "route":
                    route(dve, chain)
            for what, a, *m in moe:
                if what == "pick":
                    if a >= 2:
                        dve.wait_ge(xs_ready, 8 * (a - 1))
                    for t in range(T):
                        col = 3 * a + t
                        chain(dve.tensor_scalar(pick[:, a % 2, t, :], cst2("iota"), r_q1[:, col:col + 1], None, ALU.is_equal))
                        dve.scalar_tensor_tensor(pick[:, a % 2, t, :], cst2("iota"), r_q2[:, col:col + 1], pick[:, a % 2, t, :].bitcast(F32),
                                                 ALU.is_equal, ALU.add).then_inc(pick_ready, 1)
                elif what == "gu" and a == 0:
                    overflow_weights(dve, chain)
                elif what == "slot_weight":
                    if a == 0:
                        dve.wait_ge(rows_out, 4)
                    sid = cst2("slot")[:, a:a + 1]
                    chain(dve.scalar_tensor_tensor(back_a[:, :], slotrow[:, 0, :], sid, slotrow[:, 2, :], ALU.is_equal, ALU.mult, accum_out=r_wa[:, a:a + 1]))
                    chain(dve.scalar_tensor_tensor(back_a[:, :], slotrow[:, 1, :], sid, slotrow[:, 3, :], ALU.is_equal, ALU.mult, accum_out=r_wb[:, a:a + 1]))
                    chain(dve.tensor_tensor(r_wa[:, a:a + 1], r_wa[:, a:a + 1], r_wb[:, a:a + 1], ALU.add))
                elif what == "y_out":
                    for n in range(2):
                        dve.wait_ge(yhi_ready, 2 * a + n + 1)
                        if a >= 2:
                            dve.wait_ge(acc_done, 6 * (a - 1))
                        cols = slice(512 * n, 512 * n + 512)
                        dve.tensor_tensor(y_lo[:, a % 2, cols], ps[:, 5 + n, :], y_hi[:, a % 2, cols].bitcast(F32), ALU.subtract).then_inc(ylo_ready, 1)
                elif what == "hT_out":
                    dve.wait_ge(hT_ready, a + 1)
                    if a >= 2:
                        dve.wait_ge(dn_ready, a - 1)
                    dve.tensor_copy(act_T[:, a % 2, :], ps[:, 4, 0:256]).then_inc(hT_evac, 1)
                elif what == "h":
                    dve.wait_ge(silu_ready, a + 1)
                    if a >= 2:
                        dve.wait_ge(hT_ready, a - 1)
                    dve.scalar_tensor_tensor(act_h[:, a % 2, :], ps[:, 2 + a % 2, DE:2 * DE], r_wa[:, a:a + 1], act_g[:, a % 2, :],
                                             ALU.mult, ALU.mult).then_inc(h_ready, 1)
                elif what == "scatter":
                    j = m[0]
                    t, n = divmod(j, 2)
                    dve.wait_ge(sc_ready, 6 * a + j + 1)
                    cols = slice(512 * n, 512 * n + 512)
                    if a:
                        dve.wait_ge(acc_done, 6 * (a - 1) + j + 1)
                    dve.tensor_tensor(x2[:, t, cols], ps[:, MISC[m[1] % 3], :], x2[:, t, cols], ALU.add).then_inc(acc_done, 1)
            with if_overflow(dve):
                dve.wait_ge(acc_done, 6 * PAIRS)
                with dve.Fori(0, NG * NE) as e:
                    for t in range(T):
                        dve.wait_ge(ov_silu, 3 * e + t + 1)
                        dve.scalar_tensor_tensor(ov_h[:, t, :], ps[:, t, DE:2 * DE], r_over[:, bass.ds(e + 32 * t, 1)], ov_g[:, t, :],
                                                 ALU.mult, ALU.mult).then_inc(ov_hd, 1)
                    dve.wait_ge(ov_acc, 6 * e)
                    for j in range(6):
                        t, n = divmod(j, 2)
                        cols = slice(512 * n, 512 * n + 512)
                        dve.wait_ge(ov_down, 6 * e + j + 1)
                        dve.tensor_tensor(x2[:, t, cols], ps[:, j, :], x2[:, t, cols], ALU.add).then_inc(ov_acc, 1)
            with dve.Else():
                pass

        @block.gpsimd
        def _(pool):
            chain = Chain(pool, pool_step)

            def store(dst, src, s):
                pool.dma_start(dst, src).then_inc(s, 16)

            for kind, *arg in steps:
                i = arg[0] if arg else 0
                if kind == "post":
                    pool.wait_ge(acc_evac, i + 1)
                    if POSTED.get(i, 1) > 1:
                        pool.wait_ge(post_done, POSTED[i] - 1)
                    if i in NORMS:
                        rows_ap, rows, n, g, order = NORMS[i]
                        x = rows_ap.rearrange("p t (h n) -> p (t h) n", n=n)
                        sq = zq[:, 0:rows * n].rearrange("p (r n) -> p r n", n=n)
                        if order:
                            pool.wait_ge(hr_ready, order)
                        pool.tensor_tensor(sq, x, x, ALU.mult).then_inc(sq_ready, 1)
                        pool.wait_ge(hr_ready, order + 1)
                        pool.wait_ge(s_gain, 16)
                        chain(pool.tensor_tensor(x, x, hr[:, 0:rows].unsqueeze(2).to_broadcast([P, rows, n]), ALU.mult))
                        pool.tensor_tensor(x, x, gn(g).unsqueeze(1).to_broadcast([P, rows, n]), ALU.mult).then_inc(post_done, 1)
                        if i == C_MK:
                            pool.wait_ge(post_done, POSTED[i])
                            store(io["mem_k"], mk[:, :, :], s_out)
                        if i == C_FK:
                            pool.wait_ge(post_done, POSTED[i])
                            store(io["fox_k"], fk, s_fk_out)
                    elif i == C_RQK:
                        pool.wait_ge(s_const, 16)
                        rows = rqk.rearrange("p t (h f) -> p t h f", f=64)
                        a, b = rows[:, :, :, 0:32], rows[:, :, :, 32:64]
                        cos = cst("cos").rearrange("p (t f) -> p t f", t=T).unsqueeze(2).to_broadcast([P, T, 8, 32])
                        sin = cst("sin").rearrange("p (t f) -> p t f", t=T).unsqueeze(2).to_broadcast([P, T, 8, 32])
                        ra = zq[:, 0:768].rearrange("p (t h f) -> p t h f", t=T, f=32)
                        rb = zq[:, 768:1536].rearrange("p (t h f) -> p t h f", t=T, f=32)
                        chain(pool.tensor_tensor(ra, a, cos, ALU.mult))
                        chain(pool.tensor_tensor(rb, b, sin, ALU.mult))
                        chain(pool.tensor_tensor(ra, ra, rb, ALU.subtract))
                        chain(pool.tensor_tensor(rb, a, sin, ALU.mult))
                        chain(pool.tensor_tensor(b, b, cos, ALU.mult))
                        chain(pool.tensor_tensor(b, b, rb, ALU.add))
                        pool.tensor_copy(a, ra).then_inc(post_done, 1)
                    elif i == C_RG:
                        rows = rg.rearrange("p t (h v) -> p (t h) v", v=P)
                        pool.tensor_tensor(rows, rows, gn("ret").unsqueeze(1).to_broadcast([P, T * HR, P]), ALU.mult).then_inc(post_done, 1)
                    else:
                        if i == C_MV:
                            store(io["mem_v"], mv[:, :, :], s_out)
                        if i == C_FV:
                            store(io["fox_v"], fv, s_out)
                elif kind == "forget":
                    pool.wait_ge(logf_ready, 1)
                    store(io["logf"], logf, s_out)
                elif kind == "turn" and i == 8:
                    pool.wait_ge(turn_ready, 4)
                    k4 = rqk[:, :, 256:512].rearrange("p t (h f) -> p t h f", f=64)
                    kd = cst("kdec").rearrange("p (t h) -> p t h", t=T).unsqueeze(3).to_broadcast([P, T, HR, 64])
                    chain(pool.tensor_tensor(k4, k4, kd, ALU.mult))
                    for b in range(NB):
                        ins = pool.tensor_tensor(kmask[:, b // 2, :, b % 2, :], rqk[:, 2, 256:512].rearrange("p (h f) -> p h f", f=64),
                                                 cst("inbatch")[:, b:b + 1].unsqueeze(2).to_broadcast([P, HR, 64]), ALU.mult)
                    ins.then_inc(kmask_ready, 1)
                elif kind == "ret_state":
                    pool.wait_ge(st_done, 5)
                    store(io["state_s"], state[:, :, :, :], s_state_out)
                    store(io["state_p"], stp[:, :, :], s_stp_out)
                    pool.wait_ge(s_state_out, 16)
                    pool.wait_ge(s_stp_out, 16)
                    pool.wait_ge(s_out, 16 * 4)
                    pool.wait_ge(even_turned, 10)
                    pool.wait_ge(odd_turned, 10)
                    for b in range(4):
                        store(foxc[b][:, :], io["foxc"][b], foxc_in[b])
                    pool.memset(qb_f[:, :, :], 0.0)
                    pool.memset(qb_m[:, :, :], 0.0).then_inc(work_zero, 1)
                    pool.wait_ge(work_zero, 1)
                elif kind == "unit_s" and i + 1 < NU:
                    what, a, t = units[i + 1]
                    if what == "foxs":
                        if a >= 2:
                            pool.wait_ge(u_s, i)
                        cols = slice(SEQ + a * NI, SEQ + (a + 1) * NI)
                        pool.wait_ge(even_turned, 4)
                        pool.wait_ge(odd_turned, 4)
                        if a:
                            pool.wait_ge(qb_ready, a)
                        for hl in range(2):
                            half = slice(64 * hl, 64 * hl + 64)
                            if hl:
                                chain(ins)
                            ins = pool.tensor_copy(qb_f[half, a % 2, :].rearrange("p (g c) -> p g c", c=160)[:, :, hl * NI:(hl + 1) * NI],
                                                   fqT[half, :, cols])
                        ins.then_inc(qb_ready, 1)
                    elif what == "mems":
                        if a >= 2:
                            pool.wait_ge(u_s, i)
                        pool.wait_ge(qb_ready, NB + a)
                        for b2 in range(2):
                            b = 2 * a + b2
                            if b2:
                                chain(ins)
                            ins = pool.tensor_copy(qb_m[:, b % 4, :].rearrange("p (h c) -> p h c", c=80)[:, :, 0:NI],
                                                   mqT[:, :, SEQ + b * NI:SEQ + (b + 1) * NI])
                        ins.then_inc(qb_ready, 1)
                elif kind == "unit_v" and units[i][0] == "foxs" and units[i][1] + 4 < NB:
                    b = units[i][1] + 4
                    pool.wait_ge(u_v, i + 1)
                    store(foxc[b % 4][:, :], io["foxc"][b], foxc_in[b % 4])
                elif kind == "merge" and i >= C_BR + 2:
                    c = i - C_BR
                    pool.wait_ge(br_mul, 3 * c + 3)
                    if c >= 4:
                        pool.wait_ge(br_add, c - 3)
                    pool.tensor_tensor(z[:, GATE_SLOT[c % 2], :, :], z[:, GATE_SLOT[c % 2], :, :], z[:, GATE_SLOT[c], :, :], ALU.add).then_inc(br_add, 1)
                elif kind == "x_parts":
                    pool.wait_ge(rstd2_ready, 1)
                    for t in range(T):
                        chain(pool.tensor_scalar(x_scaled[:, t, :], x2[:, t, :], rstd2[:, t:t + 1], None, ALU.mult))
                        pool.wait_ge(xhi_ready, t + 1)
                        pool.tensor_tensor(x_lo[:, t, :], x_scaled[:, t, :], x_hi[:, t, :].bitcast(F32), ALU.subtract).then_inc(xparts_ready, 1)
                        pool.wait_ge(xparts_ready, t + 1)
            for what, a, *m in moe:
                if what == "back":
                    if a == 0:
                        pool.wait_ge(rows_out, 4)
                        pool.wait_ge(s_const2, 16)
                    else:
                        pool.wait_ge(back_ready, a)
                    if a >= 2:
                        pool.wait_ge(acc_done, 6 * (a - 1))
                    sid = cst2("slot")[:, a:a + 1]
                    chain(pool.tensor_scalar(back[:, a % 2, :], slotrow[:, 0, :], sid, None, ALU.is_equal))
                    chain(pool.tensor_scalar(back_b[:, :], slotrow[:, 1, :], sid, None, ALU.is_equal))
                    pool.tensor_tensor(back[:, a % 2, :], back[:, a % 2, :].bitcast(F32), back_b[:, :], ALU.add).then_inc(back_ready, 1)
            pool.wait_ge(s_out, 16 * 4)
            pool.wait_ge(s_fk_out, 16)

        @block.tensor
        def _(pe):
            mm = nc.tensor.matmul

            def parts(out, xh, xl, wh, wl, start, stop):
                mm(out, xh, wh, start=start, stop=False, skip_group_check=True)
                mm(out, xh, wl, start=False, stop=False, skip_group_check=True)
                return mm(out, xl, wh, start=False, stop=stop, skip_group_check=True)

            for kind, *arg in steps:
                i = arg[0] if arg else 0
                if kind == "k":
                    c = chunk_of[i]
                    what, kt, nt = CHUNKS[c]
                    if i == FIRST[c]:
                        if c == C_BR + 4:
                            pe.wait_ge(u_exp, NU)
                            pe.wait_ge(u_Te, NU)
                    if c in (0, C_RQK):
                        pe.wait_ge(act_lo, (KT if c else 0) + 2 * (i - FIRST[c]) + 2)
                    if what == "br":
                        pe.wait_ge(ot_lo, 4 * ((c - C_BR) // 2) + 2 * (i - FIRST[c]) + 2)
                    if what == "out":
                        pe.wait_ge(mt_evac, 2 * (i - FIRST[c]) + 2)
                    pe.wait_ge(lo_ready, i + 1)
                    for kk in range(2):
                        k = 2 * (i - FIRST[c]) + kk
                        first, last = k == 0, k == kt - 1
                        cols = slice(512 * kk, 512 * kk + 512)
                        for t in range(nt):
                            tok = slice(t * P, t * P + P)
                            acc = ps[:, bank_of(c, t), :]
                            if first:
                                wait_bank(pe, c, t)
                            xh, xl = {"mem": (memT_hi, memT_lo), "br": (oT_hi, oT_lo), "out": (mT_hi, mT_lo)}.get(what, (hT_hi, hT_lo))
                            j = 4 * ((c - C_BR) // 2) + k if what == "br" else k
                            w = i % PART_SLOTS
                            ins = parts(acc, xh[:, j, tok], xl[:, j, tok], w_hi[:, w, cols], w_lo[:, w, cols], first, last)
                    ins.then_inc(gran_used, 1)
                elif kind == "forget":
                    pe.wait_ge(act_lo, 2 * KT + 1)
                    for t in range(T):
                        for k in range(KT):
                            tok = slice(t * P, t * P + P)
                            ins = parts(ps[:, 6, 8 * t:8 * t + 8], hT_hi[:, k, tok], hT_lo[:, k, tok], ffw_hi[:, 8 * k:8 * k + 8], ffw_lo[:, 8 * k:8 * k + 8],
                                        k == 0, k == KT - 1)
                    ins.then_inc(ff_ready, 1)
                elif kind == "turn":
                    name, j = turns[i]
                    if i == 0:
                        pe.wait_ge(s_const, 16)
                        pe.wait_ge(acc_evac, C_GATE - 1)
                        pe.wait_ge(zneg_ready, 1)
                    pe.wait_ge(post_done, POSTED[{"rqk": C_RQK, "fq": C_FQ, "fk": C_FK, "mq": C_MQ, "mk": C_MK}[name]])
                    if i >= 5:
                        turn_wait(pe, i - 5)
                    rows = {"rqk": rqk, "fq": fq, "fk": fk, "mq": mq, "mk": mk[:, :, :]}[name]
                    for t in range(2 if name == "mk" else T):
                        ins = nc.tensor.transpose(ps[:, 3 + i % 5, t * P:(t + 1) * P], rows[:, t, j * P:(j + 1) * P], ident)
                    ins.then_inc(turn_ready, 1)
                elif kind == "decay_sums":
                    for j in range(15, 20):
                        turn_wait(pe, j)
                    pe.wait_ge(logf_ready, 1)
                    pe.wait_ge(s_logc, 16)
                    up1 = const[:, CONST["upper"][0]:CONST["upper"][0] + 256]
                    lf = [logf[:, 8 * t:8 * t + 8] for t in range(T)]
                    kw = dict(skip_group_check=True)
                    mm(ps[0:8, 3, 0:256], lf[0], up1, start=True, stop=False, **kw)
                    mm(ps[0:8, 3, 128:256], lf[1], cst("upper"), start=False, stop=True, **kw)
                    for b in range(NB):
                        win = cst("batchwin")[:, (NB - 1 - b) * NI:(NB - 1 - b) * NI + P]
                        mm(ps[0:8, 3, 256:384], logc[:, 8 * b:8 * b + 8], win, start=b == 0, stop=False, **kw)
                    mm(ps[0:8, 3, 256:384], lf[2], cst("upper_in_batch"), start=False, stop=True, **kw)
                    for b in range(NB):
                        mm(ps[0:8, 4 + b // 4, (b % 4) * P:(b % 4) * P + P], logc[:, 8 * b:8 * b + 8], cst("upper"), start=True, stop=True, **kw)
                    mm(ps[:, 6, 0:8], cst("upper"), lf[0], start=True, stop=True, **kw)
                    mm(ps[:, 6, 8:16], cst("ones"), lf[0], start=True, stop=False, **kw)
                    mm(ps[:, 6, 8:16], cst("upper"), lf[1], start=False, stop=True, **kw).then_inc(sums_ready, 1)
                elif kind == "decay_query":
                    pe.wait_ge(sums_evac, 1)
                    sel = cst("headsel")[0:8, :]
                    mm(ps[:, 5, 0:P], sel, nf_n[:, :], start=True, stop=True).then_inc(fqs_psum, 1)
                elif kind == "ret_s":
                    h, b = i, 3 + i % 2
                    pe.wait_ge(sums_evac, 1)
                    if h >= 2:
                        pe.wait_ge(ret_m, h - 1)
                    half = slice(64 * (h % 2), 64 * (h % 2) + 64)
                    q, k = rqkT[half, h // 2, :], rqkT[half, 2 + h // 2, :]
                    mm(ps[:, b, 0:256], k[:, 0:P], q[:, 0:256], start=True, stop=True, skip_group_check=True)
                    mm(ps[:, b, 256:384], k[:, P:256], q[:, P:256], start=True, stop=True, skip_group_check=True)
                    mm(ps[:, b, 384:512], k[:, SEQ:TOK], q[:, SEQ:TOK], start=True, stop=True, skip_group_check=True).then_inc(ret_s, 1)
                elif kind == "ret_o":
                    h = i
                    pe.wait_ge(ret_m, h + 1)
                    pe.wait_ge(ret_q, h + 1)
                    pe.wait_ge(s_state, 16)
                    if h:
                        pe.wait_ge(ret_rows, h)
                    s, v = sT[:, h % 2, :], rv[:, :, h * P:(h + 1) * P]
                    kw = dict(skip_group_check=True)
                    mm(ps[:, 6, 0:P], s[:, 0:P], v[:, 0, :], start=True, stop=True, **kw)
                    mm(ps[:, 6, P:2 * P], s[:, P:2 * P], v[:, 0, :], start=True, stop=False, **kw)
                    mm(ps[:, 6, P:2 * P], s[:, 2 * P:3 * P], v[:, 1, :], start=False, stop=True, **kw)
                    mm(ps[:, 6, 2 * P:3 * P], s[:, 3 * P:4 * P], v[:, 2, :], start=True, stop=False, **kw)
                    for bp in range(4):
                        ins = mm(ps[:, 6, 2 * P:3 * P], qmask[:, h % 2, bp, :], state[:, bp, h, :], start=False, stop=bp == 3, **kw)
                    ins.then_inc(ret_o, 1)
                elif kind == "ret_t":
                    pe.wait_ge(ret_rows, i + 1)
                    if i:
                        pe.wait_ge(ret_te, i)
                    for t in range(T):
                        ins = nc.tensor.transpose(ps[:, 7, t * P:(t + 1) * P], orow[:, t * P:(t + 1) * P], ident)
                    ins.then_inc(ret_t, 1)
                elif kind == "ret_state":
                    pe.wait_ge(kmask_ready, 1)
                    pe.wait_ge(fqs_ready, 1)
                    pe.wait_ge(ret_te, HR)
                    pe.wait_ge(ret_m, HR)
                    for h in range(HR):
                        for bp in range(4):
                            ins = mm(ps[:, 3 + h, bp * P:(bp + 1) * P], kmask[:, bp, h, :, :].rearrange("p a f -> p (a f)"), rv[:, 2, h * P:(h + 1) * P],
                                     start=True, stop=True, skip_group_check=True)
                        ins.then_inc(st_ready, 1)
                    for h in range(HR):
                        half = slice(64 * (h % 2), 64 * (h % 2) + 64)
                        for t in range(2):
                            ins = mm(ps[half, 7, (h // 2) * P:(h // 2) * P + P], rqk[:, t, 256 + h * 64:256 + h * 64 + 64], rv[:, t, h * P:(h + 1) * P],
                                     start=t == 0, stop=t == 1, skip_group_check=True)
                    ins.then_inc(st_ready, 1)
                elif kind == "unit_s":
                    what, a, t = units[i]
                    bank = ps[:, 3 + i % 2, :]
                    kw = dict(skip_group_check=True)
                    if i == 0:
                        pe.wait_ge(st_done, 5)
                    if i >= 2:
                        pe.wait_ge(u_exp, i - 1)
                    if what == "foxp":
                        n, half = keys(i), slice(64 * (a % 2), 64 * (a % 2) + 64)
                        mm(bank[:, 0:n], fqT[half, a // 2, t * P:(t + 1) * P], fkT[half, a // 2, 0:n], start=True, stop=False, **kw)
                        ins = mm(bank[:, 0:n], ident[0:8, a:a + 1].to_broadcast([8, P]), nf_p[:, 0:n], start=False, stop=True, **kw)
                    elif what == "memp":
                        ins = mm(bank[:, 0:256], mqT[:, a, t * P:(t + 1) * P], mkT[:, a, :], start=True, stop=True, **kw)
                    elif what == "foxs":
                        pe.wait_ge(qb_ready, a + 1)
                        pe.wait_ge(foxc_in[a % 4], 16 * (a // 4 + 1))
                        sel = cst("headsel")[0:8, :]
                        for hp in range(4):
                            mm(bank[:, 0:P], qb_f[:, a % 2, hp * P:(hp + 1) * P], foxc[a % 4][:, hp * P:(hp + 1) * P], start=hp == 0, stop=False, **kw)
                        mm(bank[:, 0:P], sel, nf_c[:, a, :], start=False, stop=True, **kw)
                        for hp in range(4):
                            mm(bank[:, P:256], qb_f[:, a % 2, hp * P:(hp + 1) * P], fkT[:, hp, SEQ:TOK], start=hp == 0, stop=False, **kw)
                        ins = mm(bank[:, P:256], sel, nf_n[:, :], start=False, stop=True, **kw)
                    else:
                        pe.wait_ge(qb_ready, NB + a + 1)
                        for b2 in range(2):
                            b = 2 * a + b2
                            pe.wait_ge(memk_in[b % 4], 16 * (b // 4 + 1))
                            for h in range(HM):
                                ins = mm(ps[64 * b2:64 * b2 + 64, 3 + i % 2, 0:256], qb_m[:, b % 4, 64 * h:64 * h + 64], memk[b % 4][:, 256 * h:256 * h + 256],
                                         start=h == 0, stop=h == 3, **kw)
                    ins.then_inc(u_s, 1)
                elif kind == "unit_p":
                    pe.wait_ge(u_p, i + 1)
                    if i:
                        pe.wait_ge(u_Te, i)
                    for k in range(keys(i) // P):
                        ins = nc.tensor.transpose(ps[:, 5, k * P:(k + 1) * P], p_sb[:, i % 2, k * P:(k + 1) * P], ident)
                    ins.then_inc(u_T, 1)
                elif kind == "unit_v":
                    what, a, t = units[i]
                    nk = keys(i) // P
                    g = group_of(i)
                    bank = ps[:, 6 + g % 2, :]
                    pr = pT[:, i % 2, :]
                    kw = dict(skip_group_check=True)
                    pe.wait_ge(u_Te, i + 1)
                    if g >= 2:
                        pe.wait_ge(u_oe, g - 1)
                    if what == "foxp":
                        for k in range(nk):
                            ins = mm(ps[64 * (a % 2):64 * (a % 2) + 64, 6 + g % 2, 0:P], fv[:, k, 64 * a:64 * a + 64], pr[:, k * P:(k + 1) * P],
                                     start=k == 0, stop=k == nk - 1, **kw)
                    elif what == "memp":
                        for k in range(nk):
                            ins = mm(bank[:, 0:P], mv[:, k, a * P:(a + 1) * P], pr[:, k * P:(k + 1) * P], start=k == 0, stop=k == 1, **kw)
                    elif what == "foxs":
                        for hp in range(4):
                            cols = slice(32 * hp, 32 * hp + 32)
                            mm(bank[:, cols], foxc[a % 4][:, 512 + hp * P:512 + (hp + 1) * P], pr[:, cols], start=True, stop=False, **kw)
                            ins = mm(bank[:, cols], fv[:, 2, hp * P:(hp + 1) * P], pr[:, P + 32 * hp:P + 32 * hp + 32], start=False, stop=True, **kw)
                    else:
                        for b2 in range(2):
                            b = 2 * a + b2
                            pe.wait_ge(memv_in[b % 4], 16 * (b // 4 + 1))
                            for h in range(HM):
                                c0 = 64 * b2 + NI * h
                                for k in range(2):
                                    v0 = 512 * k + P * h
                                    ins = mm(bank[:, c0:c0 + NI], memv[b % 4][:, v0:v0 + P], pr[:, k * P + c0:k * P + c0 + NI],
                                             start=k == 0, stop=k == 1, **kw)
                    ins.then_inc(u_v, 1)
                elif kind == "turn_merged":
                    for j in range(4 * i, 4 * i + 4):
                        pe.wait_ge(br_add, 3 + i)
                        if j == 0:
                            pe.wait_ge(u_oe, NGROUP)
                        if j >= 2:
                            pe.wait_ge(mt_evac, j - 1)
                        for t in range(T):
                            ins = nc.tensor.transpose(ps[:, 6 + j % 2, t * P:(t + 1) * P], z[:, GATE_SLOT[j // 4], t, (j % 4) * P:(j % 4 + 1) * P], ident)
                        ins.then_inc(mt_ready, 1)
                elif kind == "turn_x2":
                    pe.wait_ge(x2_ready, i + 1)
                    pe.wait_ge(mt_evac, 8)
                    for j in range(4 * i, 4 * i + 4):
                        if j >= 2:
                            pe.wait_ge(x2t_odd if j % 2 else x2t_even, j // 2)
                        for t in range(T):
                            ins = nc.tensor.transpose(ps[:, 6 + j % 2, t * P:(t + 1) * P], x2[:, t, j * P:(j + 1) * P], ident)
                        ins.then_inc(x2t_ready, 1)
                elif kind == "logits":
                    pe.wait_ge(x2t_even, 2 * i + 2)
                    pe.wait_ge(x2t_odd, 2 * i + 2)
                    pe.wait_ge(s_wr, 16)
                    for t in range(T):
                        for k in range(4 * i, 4 * i + 4):
                            ins = mm(ps[:, bank_of(C_OUT, t), 0:36], h2T[:, k, t * P:(t + 1) * P], wr[:, k, :], start=k == 0, stop=k == KT - 1, skip_group_check=True)
                    if i:
                        ins.then_inc(lg_ready, 1)
            kw = dict(skip_group_check=True)

            def misc_free(m):
                if m >= 3:
                    old, q, j = misc_steps[m - 3]
                    if old == "gather":
                        pe.wait_ge(xs_ready, 8 * q + j + 1)
                    else:
                        pe.wait_ge(acc_done, 6 * q + j + 1)

            for what, a, *m in moe:
                if what == "rank":
                    pe.wait_ge(taken_ready, 1)
                    pe.wait_ge(s_const2, 16)
                    for t in range(T):
                        for u in range(t + 1):
                            mm(ps[:, 6, 32 * t:32 * t + 32], cst2("before") if u == t else cst("ones"), r_m[:, 32 * u:32 * u + 32], start=u == 0, stop=u == t, **kw)
                    for u in range(T):
                        ins = mm(ps[0:1, 6, 96:128], cst("ones")[:, 0:1], r_m[:, 32 * u:32 * u + 32], start=u == 0, stop=u == 2, **kw)
                    ins.then_inc(rank_ready, 1)
                elif what == "rows_out":
                    pe.wait_ge(slots_ready, 1)
                    for j, col in enumerate((r_s1, r_s2, r_w1, r_w2)):
                        for t in range(T):
                            ins = nc.tensor.transpose(ps[:, j, t * P:(t + 1) * P], col[:, t:t + 1].to_broadcast([P, P]), ident)
                    ins.then_inc(rows_ready, 1)
                elif what == "gather":
                    k, mi = m
                    if k == 0:
                        pe.wait_ge(pick_ready, 3 * (a + 1))
                    if a == 0 and k == 0:
                        pe.wait_ge(rows_out, 4)
                        pe.wait_ge(xparts_ready, T)
                    misc_free(mi)
                    bank = ps[:, MISC[mi % 3], 0:256]
                    for t in range(T):
                        for x in (x_hi, x_lo):
                            ins = mm(bank, x[:, t, k * P:(k + 1) * P], pick[:, a % 2, t, :], start=t == 0 and x is x_hi, stop=t == 2 and x is x_lo, **kw)
                    ins.then_inc(xg_ready, 1)
                elif what == "gu":
                    pe.wait_ge(xs_ready, 8 * (a // 2 + 1))
                    if a >= 2:
                        pe.wait_ge(h_ready, a - 1)
                    for k in range(KT):
                        for e2 in range(2):
                            e = 2 * a + e2
                            if k % 4 == 0:
                                pe.wait_ge(wgu_in[k // 4][e % 4], 16 * (e // 4 + 1))
                            c0 = CAP * (e % 4)
                            ins = mm(ps[64 * e2:64 * e2 + 64, 2 + a % 2, :], xs[:, (a // 2) % 2, k, c0:c0 + CAP], wgu[e % 4][:, 512 * k:512 * k + 512],
                                     start=k == 0, stop=k == KT - 1, **kw)
                        if k == 3:
                            ins.then_inc(gu_half, 1)
                    ins.then_inc(gu_ready, 1)
                elif what == "hT_out":
                    pe.wait_ge(h_ready, a + 1)
                    if a:
                        pe.wait_ge(hT_evac, a)
                    for f in range(2):
                        ins = nc.tensor.transpose(ps[:, 4, f * P:(f + 1) * P], act_h[:, a % 2, f * P:(f + 1) * P], ident)
                    ins.then_inc(hT_ready, 1)
                elif what == "down":
                    pe.wait_ge(hT_evac, a + 1)
                    if a:
                        pe.wait_ge(ylo_ready, 2 * a)
                    for n in range(2):
                        for f in range(2):
                            for e2 in range(2):
                                e = 2 * a + e2
                                if n == 0 and f == 0:
                                    pe.wait_ge(wdn_in[e % 4], 16 * (e // 4 + 1))
                                o = D * f + 512 * n
                                ins = mm(ps[64 * e2:64 * e2 + 64, 5 + n, :], act_T[:, a % 2, f * P + 64 * e2:f * P + 64 * e2 + 64], wdn[e % 4][:, o:o + 512],
                                         start=f == 0, stop=f == 1, **kw)
                    ins.then_inc(dn_ready, 1)
                elif what == "scatter":
                    j, mi = m
                    t, n = divmod(j, 2)
                    if j == 0:
                        pe.wait_ge(ylo_ready, 2 * a + 2)
                        pe.wait_ge(back_ready, a + 1)
                    misc_free(mi)
                    for y in (y_hi, y_lo):
                        ins = mm(ps[:, MISC[mi % 3], :], back[:, a % 2, t * P:(t + 1) * P], y[:, a % 2, 512 * n:512 * n + 512], start=y is y_hi, stop=y is y_lo, **kw)
                    ins.then_inc(sc_ready, 1)
            with if_overflow(pe):
                pe.wait_ge(acc_done, 6 * PAIRS)
                for k in range(KT):
                    for t in range(T):
                        for x in (x_hi, x_lo):
                            ins = mm(ps[:, k, t * P:(t + 1) * P], x[:, t, k * P:(k + 1) * P].bitcast(F32), ident, start=x is x_hi, stop=x is x_lo, **kw)
                    ins.then_inc(ov_x, 1)
                pe.wait_ge(ov_xT, KT)
                with pe.Fori(0, NG * NE // 2) as i:
                    for b in range(2):
                        pe.wait_ge(ov_w[b], 16 * i + 16)
                        pe.wait_ge(ov_acc, 12 * i + 6 * b)
                        for t in range(T):
                            for k in range(KT):
                                ins = mm(ps[:, t, :], ov_h2T[:, k, t * P:(t + 1) * P], wgu_o[b][:, 512 * k:512 * k + 512], start=k == 0, stop=k == KT - 1, **kw)
                            ins.then_inc(ov_gu, 1)
                        for t in range(T):
                            pe.wait_ge(ov_hd, 6 * i + 3 * b + t + 1)
                            for f in range(2):
                                ins = nc.tensor.transpose(ps[:, 3 + t, f * P:(f + 1) * P], ov_h[:, t, f * P:(f + 1) * P], ident)
                            ins.then_inc(ov_tr, 1)
                        pe.wait_ge(ov_hTe, 6 * i + 3 * b + 3)
                        for j in range(6):
                            t, n = divmod(j, 2)
                            for f in range(2):
                                o = 4096 + D * f + 512 * n
                                ins = mm(ps[:, j, :], ov_hT[:, t, f * P:(f + 1) * P], wgu_o[b][:, o:o + 512], start=f == 0, stop=f == 1, **kw)
                            ins.then_inc(ov_down, 1)
            with pe.Else():
                pass


def constants():
    a = np.zeros((P, N_CONST), np.float64)
    p = np.arange(P)

    def put(name, x):
        o, n = CONST[name]
        a[:, o:o + n] = x.reshape(P, n)

    i16, b16 = p % NI, p // NI
    put("ident", np.eye(P))
    put("upper", (p[None, :] >= p[:, None]).astype(float))
    put("ones", np.ones((P, P)))
    win = np.zeros((P, 240))
    win[:, 112:128] = 1.0
    put("batchwin", win)
    win = np.full((P, 240), -BIG)
    win[:, 112:128] = np.where(np.arange(NI)[None, :] <= i16[:, None], 0.0, -BIG)
    put("maskwin", win)
    put("upper_in_batch", ((p[None, :] >= p[:, None]) & (b16[None, :] == b16[:, None])).astype(float))
    zc = np.zeros((P, 256))
    zc[:, 128:] = np.where(p[None, :] <= p[:, None], 0.0, -BIG)
    put("zeros_causal", zc)
    pos = np.concatenate([np.arange(SEQ), PAST + i16]).astype(np.float32)
    inv = (np.float32(10000.0) ** (-np.arange(32, dtype=np.float32) / np.float32(32))).astype(np.float32)
    ang = (pos[:, None] * inv[None, :]).astype(np.float32).astype(np.float64).reshape(T, P, 32).transpose(1, 0, 2)
    put("cos", np.cos(ang))
    put("sin", np.sin(ang))
    lg = np.log1p(-2.0 ** (-5.0 - np.arange(HR)))
    scale = 64 ** -0.5
    diff = p[None, :] - p[:, None]
    dec = np.where((diff >= 0)[:, None, :] & (b16[:, None] == b16[None, :])[:, None, :], np.exp(diff[:, None, :] * lg[None, :, None]), 0.0) * scale
    put("decay_s", dec)
    kd = np.concatenate([SEQ - 1 - np.arange(SEQ), NI - 1 - i16]).reshape(T, P).T
    put("kdec", np.exp(kd[:, :, None] * lg[None, None, :]) * scale)
    put("inbatch", (b16[:, None] == np.arange(NB)[None, :]).astype(float))
    put("headsel", (b16[None, :] == p[:, None]).astype(float))
    put("pick", (i16[:, None] == np.arange(NI)[None, :]).astype(float))
    put("rev4", np.tile(4.0 - np.arange(4), (P, T)))
    put("rev8", np.tile(8.0 - np.arange(8), (P, T)))
    i = np.arange(256)
    d2 = i[None, :] - p[:, None]
    dtab = np.where((d2 >= 0)[:, None, :], np.exp(np.maximum(d2, 0)[:, None, :] * lg[None, :, None]), 0.0) * scale
    qt = np.exp((i16[None, :] + 1.0) * lg[:, None])
    own = (2 * np.arange(4)[None, :, None] + (p // 64)[:, None, None]) == b16[None, None, :]
    qtab = qt[None, :, None, :] * own[:, None, :, :]
    c2 = np.zeros((P, N_CONST2))
    e = np.arange(32)
    for name, x in (("before", (p[None, :] > p[:, None]).astype(float)), ("iota", np.tile(np.arange(256), (P, 1))),
                    ("slot", P * np.arange(PAIRS)[None, :] + p[:, None]), ("first_slot", np.tile(CAP * e, (P, T))),
                    ("quad_slot", np.tile(np.repeat(4 * CAP * np.arange(QUADS), T), (P, 1)))):
        o, n = CONST2[name]
        c2[:, o:o + n] = x
    f = np.float32
    return c2.astype(f), a.astype(f), dtab.astype(f), qtab.astype(f)


OUTS = [("y", (P, T, D)), ("fox_k", (P, T, 512)), ("fox_v", (P, T, 512)), ("logf", (P, T * 8)), ("mem_k", (P, 2, 512)), ("mem_v", (P, 2, 512)),
        ("state_s", (P, 4, HR, P)), ("state_p", (P, 2, P))]


def kernel(**inputs):
    from concourse import bacc
    from concourse.bass_utils import run_bass_kernel_spmd

    g = {k: np.ascontiguousarray(v) for k, v in inputs.items()}
    c = np.ascontiguousarray
    x = np.concatenate([g["x_prompt"].reshape(SEQ, D), g["x_sample"].reshape(P, D)])
    mem = g["mem_prompt"].reshape(NMEM, D)

    def by_token(a, t):
        return c(a.reshape(t, P, -1).transpose(1, 0, 2))

    def turned(a):
        return c(a.reshape(-1, KT, P).transpose(2, 1, 0))

    def granules(w):
        k, n = w.shape
        return w.reshape(k // 256, 2, P, n // 512, 512).transpose(3, 0, 2, 1, 4).reshape(-1, P, GRAN)

    w = g["w_in"][0]
    sizes = [256, 256, 512, 512, 512, 512, 512, 8, 512, 3072]
    cut = np.cumsum([0] + sizes)
    parts = [w[:, cut[i]:cut[i + 1]] for i in range(10)]
    wff = parts[7]
    win = np.concatenate(parts[:6] + [parts[8], parts[6], parts[9]], axis=1)
    stream = [granules(g["w_mem_kv"][0]), granules(win), granules(g["w_br_ret"][0]), granules(g["w_br_fox"][0]), granules(g["w_br_mem"][0]),
              granules(g["w_out"][0])]
    const2, const, dtab, qtab = constants()
    gk = np.concatenate([g[n].reshape(KT, P).T for n in ("g_norm1", "g_mem_in", "g_norm2")], axis=1)
    gain = np.concatenate([g["g_fox_q"][0], g["g_fox_k"][0], g["g_mem_q"][0], g["g_mem_k"][0], g["g_ret_out"][0], g["b_forget"][0],
                           g["b_route_group"][0], g["b_route_expert"][0]])
    fk = g["cache_fox_k"][0].transpose(0, 2, 3, 1).reshape(NB, 4, P, P).transpose(0, 2, 1, 3).reshape(NB, P, 512)
    foxc = np.concatenate([fk, g["cache_fox_v"][0].reshape(NB, P, 512)], axis=2)
    mkc = g["cache_mem_k"][0].transpose(0, 3, 2, 1).reshape(NB, P, 1024)
    mvc = g["cache_mem_v"][0].reshape(NB, 2, P, 512).transpose(0, 2, 1, 3).reshape(NB, P, 1024)
    gu = np.concatenate([g["w_exp_gate"].reshape(32, KT, P, DE), g["w_exp_up"].reshape(32, KT, P, DE)], axis=3).transpose(0, 2, 1, 3).reshape(32, P, 4096)
    dn = g["w_exp_down"].reshape(32, 2, P, D).transpose(0, 2, 1, 3).reshape(32, P, 2048)
    arrays = {
        "xT": turned(x), "xtok": by_token(x, T), "memT": turned(mem), "memtok": by_token(mem, 2), "gk": c(gk), "gain": c(np.tile(gain, (P, 1))),
        "const": const, "const2": const2, "dtab": dtab, "qtab": qtab, "ffw": c(wff.reshape(KT, P, 8).transpose(1, 0, 2).reshape(P, 64)),
        "logc": c(g["cache_fox_logf"][0].transpose(1, 0, 2).reshape(P, 64)), "wstream": c(np.concatenate(stream)),
        "state": c(g["state_ret"][0].reshape(4, 2, HR, 64, P).transpose(1, 3, 0, 2, 4).reshape(P, 4, HR, P)),
        "foxc": c(foxc), "memc": c(np.concatenate([mkc, mvc], axis=2)),
        "wr": c(np.concatenate([g["w_route_group"][0], g["w_route_expert"][0]], axis=1).reshape(KT, P, 36).transpose(1, 0, 2)),
        "wexp": c(np.concatenate([gu, dn], axis=2)),
    }
    nc = bacc.Bacc("TRN2", target_bir_lowering=False, num_devices=1)
    io = {k: nc.dram_tensor(f"in_{k}", v.shape, mybir.dt.from_np(v.dtype), kind="ExternalInput").ap() for k, v in arrays.items()}
    io.update({k: nc.dram_tensor(f"out_{k}", s, F32, kind="ExternalOutput").ap() for k, s in OUTS})
    program(nc, io)
    r = run_bass_kernel_spmd(nc, [{f"in_{k}": v for k, v in arrays.items()}], core_ids=[0]).results[0]
    o = {k: np.asarray(r[f"out_{k}"]).reshape(s) for k, s in OUTS}

    def rows(a):
        return a.transpose(1, 0, 2).reshape(a.shape[0] * a.shape[1], -1)

    y, fk, fv = rows(o["y"]), rows(o["fox_k"]), rows(o["fox_v"])
    lf = rows(o["logf"].reshape(P, T, 8))
    mk, mv = rows(o["mem_k"]), rows(o["mem_v"])
    st_s = o["state_s"].reshape(2, 64, 4, HR, P).transpose(2, 0, 3, 1, 4).reshape(1, NB, HR, 64, P)
    st_p = o["state_p"].reshape(2, 64, 2, P).transpose(2, 0, 1, 3).reshape(1, 1, HR, 64, P)
    return (y[:SEQ].reshape(1, SEQ, D), y[SEQ:].reshape(NB, NI, D), st_p, fk[:SEQ].reshape(1, 1, SEQ, HF, 64), fv[:SEQ].reshape(1, 1, SEQ, HF, 64),
            lf[:SEQ].reshape(1, 1, SEQ, HF), mk.reshape(1, 1, NMEM, HM, P), mv.reshape(1, 1, NMEM, HM, P), st_s,
            fk[SEQ:].reshape(1, NB, NI, HF, 64), fv[SEQ:].reshape(1, NB, NI, HF, 64), lf[SEQ:].reshape(1, NB, NI, HF))
```
